# Optimizing a Trainium2 kernel written in Bass

```python
import math
import jax, jax.numpy as jnp
from jax import lax
import numpy as np

D_MODEL = 1024
BATCH = 1
SEQ = 512
DEPTH = 2

N_MIXERS = 2
N_A = (DEPTH + 1) // 2
N_B = DEPTH // 2
HG_HEAD_DIM = 128
HG_HEADS = D_MODEL // HG_HEAD_DIM
HG_DIM = HG_HEADS * HG_HEAD_DIM
HG_CHUNK = 64
D_INNER = 2 * D_MODEL
SSM_HEAD_DIM = 64
SSM_HEADS = D_INNER // SSM_HEAD_DIM
SSM_GROUPS = 8
SSM_HPG = SSM_HEADS // SSM_GROUPS
SSM_STATE = 128
SSM_CONV = 5
SSD_CHUNK = 128
GN = SSM_GROUPS * SSM_STATE
CONV_DIM = D_INNER + 2 * GN
B_PROJ = 2 * D_INNER + 2 * GN + 2 * SSM_HEADS
D_FF = ((8 * D_MODEL // 3 + 255) // 256) * 256
FFN_CONV = 3
EPS = 1e-6


def rmsnorm(x, w):
    xf = x.astype(jnp.float32)
    y = xf * lax.rsqrt(jnp.mean(xf * xf, axis=-1, keepdims=True) + EPS)
    return (y * w.astype(jnp.float32)).astype(x.dtype)

def group_rmsnorm(x, w, groups):
    shp = x.shape
    xf = x.astype(jnp.float32).reshape(*shp[:-1], groups, shp[-1] // groups)
    y = xf * lax.rsqrt(jnp.mean(xf * xf, axis=-1, keepdims=True) + EPS)
    y = y.reshape(shp) * w.astype(jnp.float32)
    return y.astype(x.dtype)

def dwconv_centred(x, w, b):
    ch = x.shape[-1]
    y = lax.conv_general_dilated(x, w[:, None, :].astype(x.dtype), window_strides=(1,), padding='SAME',
                                 dimension_numbers=('NWC', 'WIO', 'NWC'), feature_group_count=ch)
    return y + b.astype(x.dtype)

def flip(t):
    return jnp.flip(t, axis=1)

def gla_chunked(q, k, v, logf):
    bsz, seq, h, dk = q.shape
    dv = v.shape[-1]
    nc = seq // HG_CHUNK

    def chunks(t):
        return t.reshape(bsz, nc, HG_CHUNK, h, t.shape[-1]).transpose(1, 0, 3, 2, 4)

    lower = jnp.tril(jnp.ones((HG_CHUNK, HG_CHUNK), dtype=bool))

    def step(state, inp):
        qc, kc, vc, gc = inp
        b = jnp.cumsum(gc, axis=2)
        o_inter = jnp.einsum('bhtk,bhkv->bhtv', qc * jnp.exp(b), state)
        rel = jnp.where(lower[:, :, None], b[:, :, :, None, :] - b[:, :, None, :, :], -jnp.inf)
        att = jnp.einsum('bhtsk,bhsk->bhts', qc[:, :, :, None, :] * jnp.exp(rel), kc)
        o = o_inter + jnp.einsum('bhts,bhsv->bhtv', att, vc)
        b_last = b[:, :, -1:, :]
        state = (jnp.exp(b_last)[:, :, 0, :, None] * state
                 + jnp.einsum('bhsk,bhsv->bhkv', kc * jnp.exp(b_last - b), vc))
        return state, o

    state0 = jnp.zeros((bsz, h, dk, dv), q.dtype)
    _, o = lax.scan(step, state0, (chunks(q), chunks(k), chunks(v), chunks(logf)))
    return o.transpose(1, 0, 3, 2, 4).reshape(bsz, seq, h, dv)

def hgrn2_mixer(u, w_in, lb, norm_w, w_out):
    bsz, seq, _ = u.shape
    q, f_fw, f_bw, iv, g = jnp.split(u @ w_in, 5, axis=-1)

    def heads(t):
        return t.reshape(bsz, seq, HG_HEADS, HG_HEAD_DIM)

    def gate(fr):
        f = lb + (1.0 - lb) * jax.nn.sigmoid(fr.astype(jnp.float32))
        return heads(jnp.log(f)).astype(u.dtype), heads(1.0 - f).astype(u.dtype)

    q = heads(jax.nn.silu(q))
    iv = heads(iv)
    logf_fw, k_fw = gate(f_fw)
    logf_bw, k_bw = gate(f_bw)
    o = gla_chunked(q, k_fw, iv, logf_fw) + flip(gla_chunked(flip(q), flip(k_bw), flip(iv), flip(logf_bw)))
    o = rmsnorm(o, norm_w) * jax.nn.silu(heads(g))
    return o.reshape(bsz, seq, HG_DIM) @ w_out

def ssd_chunked(x, dt, a, bm, cm):
    bsz, seq = x.shape[:2]
    nc = seq // SSD_CHUNK
    c = SSD_CHUNK
    xd = (x * dt[..., None]).reshape(bsz, nc, c, SSM_GROUPS, SSM_HPG, SSM_HEAD_DIM)
    la = (dt * a).reshape(bsz, nc, c, SSM_GROUPS, SSM_HPG).transpose(0, 3, 4, 1, 2)
    a_cum = jnp.cumsum(la, axis=-1)
    bc = bm.reshape(bsz, nc, c, SSM_GROUPS, SSM_STATE)
    cc = cm.reshape(bsz, nc, c, SSM_GROUPS, SSM_STATE)
    lower = jnp.tril(jnp.ones((c, c), dtype=bool))
    lmat = jnp.exp(jnp.where(lower, a_cum[..., :, None] - a_cum[..., None, :], -jnp.inf))
    cb = jnp.einsum('bclgn,bcsgn->bgcls', cc, bc)
    y_diag = jnp.einsum('bgjcls,bcsgjp->bclgjp', cb[:, :, None] * lmat, xd)
    decay_s = jnp.exp(a_cum[..., -1:] - a_cum).transpose(0, 3, 4, 1, 2)[..., None]
    states = jnp.einsum('bcsgn,bcsgjp->bcgjpn', bc, xd * decay_s)
    a_last = a_cum[..., -1]
    a_cs = jnp.cumsum(a_last, axis=-1)
    a_excl = a_cs - a_last
    before = jnp.tril(jnp.ones((nc, nc), dtype=bool), k=-1)
    w = jnp.exp(jnp.where(before, a_excl[..., :, None] - a_cs[..., None, :], -jnp.inf))
    h_in = jnp.einsum('bgjzc,bcgjpn->bzgjpn', w, states)
    y_off = (jnp.einsum('bzlgn,bzgjpn->bzlgjp', cc, h_in)
             * jnp.exp(a_cum).transpose(0, 3, 4, 1, 2)[..., None])
    return (y_diag + y_off).reshape(bsz, seq, SSM_GROUPS, SSM_HPG, SSM_HEAD_DIM)

def mamba2_mixer(u, w_in, conv_w, conv_b, dt_bias, a_log, d_skip, norm_w, w_out):
    bsz, seq, _ = u.shape
    z, xbc, dt_raw = jnp.split(u @ w_in, [D_INNER, D_INNER + CONV_DIM], axis=-1)
    xbc = jax.nn.silu(dwconv_centred(xbc, conv_w, conv_b))
    xs, bm, cm = jnp.split(xbc, [D_INNER, D_INNER + GN], axis=-1)
    xs = xs.reshape(bsz, seq, SSM_GROUPS, SSM_HPG, SSM_HEAD_DIM)
    bm = bm.reshape(bsz, seq, SSM_GROUPS, SSM_STATE)
    cm = cm.reshape(bsz, seq, SSM_GROUPS, SSM_STATE)
    dt = jax.nn.softplus(dt_raw.reshape(bsz, seq, 2, SSM_HEADS) + dt_bias)
    a = -jnp.exp(a_log).reshape(2, SSM_GROUPS, SSM_HPG)
    dt_fw = dt[:, :, 0].reshape(bsz, seq, SSM_GROUPS, SSM_HPG)
    dt_bw = dt[:, :, 1].reshape(bsz, seq, SSM_GROUPS, SSM_HPG)
    y = (ssd_chunked(xs, dt_fw, a[0], bm, cm)
         + flip(ssd_chunked(flip(xs), flip(dt_bw), a[1], flip(bm), flip(cm)))
         + xs * d_skip.reshape(SSM_GROUPS, SSM_HPG, 1))
    y = y.reshape(bsz, seq, D_INNER) * jax.nn.silu(z)
    y = group_rmsnorm(y, norm_w, SSM_GROUPS)
    return y @ w_out

def conv_glu(u, w_in, conv_w, conv_b, w_out):
    gate, val = jnp.split(u @ w_in, 2, axis=-1)
    return (jax.nn.silu(dwconv_centred(gate, conv_w, conv_b)) * val) @ w_out

def first_inputs(seed: int = 0) -> dict:
    key = jax.random.key(seed)
    ks = jax.random.split(key, 20)

    def nrm(k, shape, scale):
        return scale * jax.random.normal(k, shape, jnp.float32)

    dt = jnp.exp(jax.random.uniform(ks[10], (N_B, 2, SSM_HEADS), jnp.float32)
                 * (math.log(0.1) - math.log(1e-3)) + math.log(1e-3))
    return {
        "x": nrm(ks[0], (BATCH, SEQ, D_MODEL), 1.0),
        "norm1_w": 1.0 + nrm(ks[1], (DEPTH, D_MODEL), 0.02),
        "norm2_w": 1.0 + nrm(ks[2], (DEPTH, D_MODEL), 0.02),
        "a_w_in": nrm(ks[3], (N_A, D_MODEL, 5 * HG_DIM), D_MODEL ** -0.5),
        "a_lb_logits": nrm(ks[4], (DEPTH + 1, HG_DIM), 0.1),
        "a_norm_w": 1.0 + nrm(ks[5], (N_A, HG_HEAD_DIM), 0.02),
        "a_w_out": nrm(ks[6], (N_A, HG_DIM, D_MODEL), HG_DIM ** -0.5),
        "b_w_in": nrm(ks[7], (N_B, D_MODEL, B_PROJ), D_MODEL ** -0.5),
        "b_conv_w": nrm(ks[8], (N_B, SSM_CONV, CONV_DIM), SSM_CONV ** -0.5),
        "b_conv_b": nrm(ks[9], (N_B, CONV_DIM), 0.02),
        "b_dt_bias": dt + jnp.log(-jnp.expm1(-dt)),
        "b_a_log": jnp.log(jax.random.uniform(ks[11], (N_B, 2, SSM_HEADS), jnp.float32, 1.0, 16.0)),
        "b_d_skip": 1.0 + nrm(ks[12], (N_B, SSM_HEADS), 0.02),
        "b_norm_w": 1.0 + nrm(ks[13], (N_B, D_INNER), 0.02),
        "b_w_out": nrm(ks[14], (N_B, D_INNER, D_MODEL), D_INNER ** -0.5),
        "ffn_w_in": nrm(ks[15], (DEPTH, D_MODEL, 2 * D_FF), D_MODEL ** -0.5),
        "ffn_conv_w": nrm(ks[16], (DEPTH, FFN_CONV, D_FF), FFN_CONV ** -0.5),
        "ffn_conv_b": nrm(ks[17], (DEPTH, D_FF), 0.02),
        "ffn_w_out": nrm(ks[18], (DEPTH, D_FF, D_MODEL), D_FF ** -0.5),
        "final_norm_w": 1.0 + nrm(ks[19], (D_MODEL,), 0.02),
    }

def first_block(x, norm1_w, norm2_w, a_w_in, a_lb_logits, a_norm_w, a_w_out, b_w_in, b_conv_w, b_conv_b,
              b_dt_bias, b_a_log, b_d_skip, b_norm_w, b_w_out, ffn_w_in, ffn_conv_w, ffn_conv_b, ffn_w_out,
              final_norm_w):
    lower_bounds = jnp.cumsum(jax.nn.softmax(a_lb_logits.astype(jnp.float32), axis=0), axis=0)
    h = x
    for i in range(DEPTH):
        u = rmsnorm(h, norm1_w[i])
        j = i // N_MIXERS
        if i % N_MIXERS == 0:
            h = h + hgrn2_mixer(u, a_w_in[j], lower_bounds[i], a_norm_w[j], a_w_out[j])
        else:
            h = h + mamba2_mixer(u, b_w_in[j], b_conv_w[j], b_conv_b[j], b_dt_bias[j], b_a_log[j],
                                 b_d_skip[j], b_norm_w[j], b_w_out[j])
        h = h + conv_glu(rmsnorm(h, norm2_w[i]), ffn_w_in[i], ffn_conv_w[i], ffn_conv_b[i], ffn_w_out[i])
    return rmsnorm(h, final_norm_w)


_first_inputs = first_inputs


def first_inputs(seed=0):
    import zlib

    import numpy as np

    out = dict(_first_inputs(seed))
    spreads = {}
    factors = {'norm2_w': 2.799,
     'a_lb_logits': 8.0,
     'a_norm_w': 3.362,
     'b_d_skip': 8.0,
     'b_norm_w': 4.371,
     'ffn_conv_b': 4.259,
     'final_norm_w': 2.838}
    for name, (base, spread) in spreads.items():
        noise = np.random.default_rng([zlib.crc32(name.encode()), seed]).standard_normal(out[name].shape)
        drawn = base * np.exp(spread * noise) if base else spread * noise
        out[name] = __import__('jax').numpy.asarray(drawn.astype(out[name].dtype))
    for name, factor in factors.items():
        out[name] = (out[name] * factor).astype(out[name].dtype)
    return out


_narrow_inputs = first_inputs


def first_inputs(seed=0):

    out = dict(_narrow_inputs(seed))
    wider = {'b_conv_b': 3.74, 'b_d_skip': 7.13, 'b_norm_w': 4.48, 'final_norm_w': 3.19}
    for name, times in wider.items():
        mean = out[name].mean()
        out[name] = (mean + times * (out[name] - mean)).astype(out[name].dtype)
    return out


DEPTH_2 = 1

HEAD_DIM = 64
SB_HEADS = 8
SW_HEADS = 8
SW_KV_HEADS = 2
SW_GROUP = SW_HEADS // SW_KV_HEADS
WINDOW = 128
BLOCK = 128
D_FF_2 = 4 * D_MODEL
PLE_DIM = 256
N_BUCKETS = 32
MAX_DISTANCE = 128

SB_W = SB_HEADS * HEAD_DIM
SW_QW = SW_HEADS * HEAD_DIM
SW_KVW = SW_KV_HEADS * HEAD_DIM
IN_COLS = 3 * SB_W + SW_QW + 2 * SW_KVW + 2 * D_MODEL


def rmsnorm_2(x, g):
    xf = x.astype(jnp.float32)
    r = lax.rsqrt(jnp.mean(xf * xf, axis=-1, keepdims=True) + EPS)
    return (xf * r).astype(x.dtype) * g

def t5_causal_bucket(dist):
    max_exact = N_BUCKETS // 2
    d = jnp.maximum(dist, 0)
    df = jnp.maximum(d, 1).astype(jnp.float32)
    large = max_exact + (jnp.log(df / max_exact) / math.log(MAX_DISTANCE / max_exact)
                         * (N_BUCKETS - max_exact)).astype(jnp.int32)
    large = jnp.minimum(large, N_BUCKETS - 1)
    return jnp.where(d < max_exact, d, large)

def stick_breaking_attention(q, k, v):
    b_, s_, h_, dh = q.shape
    nb = s_ // BLOCK
    scale = dh ** -0.5
    qb = q.reshape(b_, nb, BLOCK, h_, dh).transpose(1, 0, 3, 2, 4)
    kpos = jnp.arange(s_)

    def one_block(args):
        qblk, n = args
        z = jnp.einsum('bhqd,bshd->bhqs', qblk, k).astype(jnp.float32) * scale
        qpos = n * BLOCK + jnp.arange(BLOCK)
        causal = kpos[None, :] < qpos[:, None]
        log_beta = jax.nn.log_sigmoid(z)
        log_1mb = jnp.where(causal, jax.nn.log_sigmoid(-z), 0.0)
        suffix = lax.cumsum(log_1mb, axis=3, reverse=True) - log_1mb
        a = jnp.where(causal, jnp.exp(log_beta + suffix), 0.0)
        return jnp.einsum('bhqs,bshd->bqhd', a.astype(v.dtype), v)

    o = lax.map(one_block, (qb, jnp.arange(nb)))
    return o.transpose(1, 0, 2, 3, 4).reshape(b_, s_, h_ * dh)

def sliding_window_sink_attention(q, k, v, sinks, bias):
    b_, s_ = q.shape[:2]
    nb = s_ // BLOCK
    scale = HEAD_DIM ** -0.5
    qb = q.reshape(b_, nb, BLOCK, SW_KV_HEADS, SW_GROUP, HEAD_DIM)
    pad = jnp.zeros((b_, BLOCK, SW_KV_HEADS, HEAD_DIM), k.dtype)
    kp = jnp.concatenate([pad, k], axis=1).reshape(b_, nb + 1, BLOCK, SW_KV_HEADS, HEAD_DIM)
    vp = jnp.concatenate([pad, v], axis=1).reshape(b_, nb + 1, BLOCK, SW_KV_HEADS, HEAD_DIM)
    kb = jnp.concatenate([kp[:, :-1], kp[:, 1:]], axis=2)
    vb = jnp.concatenate([vp[:, :-1], vp[:, 1:]], axis=2)
    s = jnp.einsum('bnqkgd,bnskd->bnkgqs', qb, kb).astype(jnp.float32) * scale + bias
    i = jnp.arange(BLOCK)[:, None]
    j = jnp.arange(2 * BLOCK)[None, :]
    dist = BLOCK + i - j
    band = (dist >= 0) & (dist < WINDOW)
    key_abs = (jnp.arange(nb)[:, None, None] - 1) * BLOCK + j[None]
    valid = band[None] & (key_abs >= 0)
    s = jnp.where(valid[None, :, None, None], s, -jnp.inf)
    sink = sinks.astype(jnp.float32).reshape(SW_KV_HEADS, SW_GROUP)[None, None, :, :, None, None]
    m = jnp.maximum(jnp.max(s, axis=-1, keepdims=True), sink)
    e = jnp.exp(s - m)
    denom = jnp.sum(e, axis=-1, keepdims=True) + jnp.exp(sink - m)
    pr = (e / denom).astype(v.dtype)
    o = jnp.einsum('bnkgqs,bnskd->bnqkgd', pr, vb)
    return o.reshape(b_, s_, SW_HEADS * HEAD_DIM)

def window_bias(rel_bias):
    i = jnp.arange(BLOCK)[:, None]
    j = jnp.arange(2 * BLOCK)[None, :]
    dist = BLOCK + i - j
    bias = rel_bias[t5_causal_bucket(dist)]
    return bias.transpose(2, 0, 1).reshape(SW_KV_HEADS, SW_GROUP, BLOCK, 2 * BLOCK)

def second_inputs(seed: int = 0) -> dict:
    key = jax.random.key(seed)
    ks = jax.random.split(key, 20)
    f32 = jnp.float32

    def nrm(k, shape, fan_in):
        return jax.random.normal(k, shape, f32) * (fan_in ** -0.5)

    return {
        "x": jax.random.normal(ks[0], (BATCH, SEQ, D_MODEL), f32),
        "p": jax.random.normal(ks[1], (DEPTH_2, BATCH, SEQ, PLE_DIM), f32),
        "w_in": nrm(ks[2], (DEPTH_2, D_MODEL, IN_COLS), D_MODEL),
        "w_up_a": nrm(ks[3], (DEPTH_2, SB_W, D_MODEL), SB_W),
        "w_up_b": nrm(ks[4], (DEPTH_2, SW_QW, D_MODEL), SW_QW),
        "w_o": nrm(ks[5], (DEPTH_2, D_MODEL, D_MODEL), D_MODEL),
        "w_ff1": nrm(ks[6], (DEPTH_2, D_MODEL, D_FF_2), D_MODEL),
        "w_ff2": nrm(ks[7], (DEPTH_2, D_FF_2, D_MODEL), D_FF_2),
        "w_pe": nrm(ks[8], (DEPTH_2, PLE_DIM, D_MODEL), PLE_DIM),
        "w_pg": nrm(ks[9], (DEPTH_2, D_MODEL, D_MODEL), D_MODEL),
        "g_mix": 1.0 + 0.01 * jax.random.normal(ks[10], (DEPTH_2, D_MODEL), f32),
        "g_mlp": 1.0 + 0.01 * jax.random.normal(ks[11], (DEPTH_2, D_MODEL), f32),
        "g_pe": 1.0 + 0.01 * jax.random.normal(ks[12], (DEPTH_2, D_MODEL), f32),
        "g_final": 1.0 + 0.01 * jax.random.normal(ks[13], (D_MODEL,), f32),
        "sinks": 0.5 * jax.random.normal(ks[14], (DEPTH_2, SW_HEADS), f32),
        "rel_bias": 0.5 * jax.random.normal(ks[15], (N_BUCKETS, SW_HEADS), f32),
    }

def second_block(x, p, w_in, w_up_a, w_up_b, w_o, w_ff1, w_ff2, w_pe, w_pg,
              g_mix, g_mlp, g_pe, g_final, sinks, rel_bias):
    b_, s_, _ = x.shape
    bias = window_bias(rel_bias)
    o1 = SB_W
    o2 = o1 + SB_W
    o3 = o2 + SB_W
    o4 = o3 + SW_QW
    o5 = o4 + SW_KVW
    o6 = o5 + SW_KVW
    o7 = o6 + D_MODEL
    for i in range(DEPTH_2):
        h = rmsnorm_2(x, g_mix[i])
        proj = h @ w_in[i]
        q_a = proj[..., :o1].reshape(b_, s_, SB_HEADS, HEAD_DIM)
        k_a = proj[..., o1:o2].reshape(b_, s_, SB_HEADS, HEAD_DIM)
        v_a = proj[..., o2:o3].reshape(b_, s_, SB_HEADS, HEAD_DIM)
        q_b = proj[..., o3:o4].reshape(b_, s_, SW_HEADS, HEAD_DIM)
        k_b = proj[..., o4:o5].reshape(b_, s_, SW_KV_HEADS, HEAD_DIM)
        v_b = proj[..., o5:o6].reshape(b_, s_, SW_KV_HEADS, HEAD_DIM)
        gate_a = proj[..., o6:o7]
        gate_b = proj[..., o7:]
        y_a = stick_breaking_attention(q_a, k_a, v_a) @ w_up_a[i]
        y_b = sliding_window_sink_attention(q_b, k_b, v_b, sinks[i], bias) @ w_up_b[i]
        merged = jax.nn.sigmoid(gate_a) * y_a + jax.nn.sigmoid(gate_b) * y_b
        x = x + merged @ w_o[i]
        h = rmsnorm_2(x, g_mlp[i])
        x = x + jnp.square(jax.nn.relu(h @ w_ff1[i])) @ w_ff2[i]
        pe = p[i] @ w_pe[i]
        x = x + pe * jax.nn.sigmoid(rmsnorm_2(x, g_pe[i]) @ w_pg[i])
    return rmsnorm_2(x, g_final)


_first_inputs_2 = second_inputs


def second_inputs(seed=0):
    import zlib

    import numpy as np

    out = dict(_first_inputs_2(seed))
    spreads = {}
    factors = {}
    for name, (base, spread) in spreads.items():
        noise = np.random.default_rng([zlib.crc32(name.encode()), seed]).standard_normal(out[name].shape)
        drawn = base * np.exp(spread * noise) if base else spread * noise
        out[name] = __import__('jax').numpy.asarray(drawn.astype(out[name].dtype))
    for name, factor in factors.items():
        out[name] = (out[name] * factor).astype(out[name].dtype)
    return out


_narrow_inputs_2 = second_inputs


def second_inputs(seed=0):

    out = dict(_narrow_inputs_2(seed))
    wider = {'g_mix': 12.0, 'g_mlp': 7.61, 'g_pe': 12.0, 'g_final': 6.2, 'sinks': 12.0}
    for name, times in wider.items():
        mean = out[name].mean()
        out[name] = (mean + times * (out[name] - mean)).astype(out[name].dtype)
    return out


DEPTH_3 = 1

GRID_W = 64
CTX_LEN = 256
D_CONV = 1024
CONV_WIDTH = 31
N_HEADS = 8
QK_NOPE = 128
QK_ROPE = 64
V_DIM = 128
Q_LORA = 384
KV_LORA = 256
ROPE_THETA = 10000.0
Q_BLOCK = 128
ATTN_SCALE = (QK_NOPE + QK_ROPE) ** -0.5
D_FF_3 = ((8 * D_MODEL // 3 + 255) // 256) * 256

_OFF_Q = 2 * D_CONV
_OFF_KV = _OFF_Q + Q_LORA
_OFF_KR = _OFF_KV + KV_LORA
_OFF_GATE = _OFF_KR + QK_ROPE
D_IN = _OFF_GATE + 2 * D_MODEL


def rms_norm(x, g):
    xf = x.astype(jnp.float32)
    y = xf * lax.rsqrt(jnp.mean(jnp.square(xf), axis=-1, keepdims=True) + EPS)
    return (y * g.astype(jnp.float32)).astype(x.dtype)

def layer_norm(x, g, b):
    xf = x.astype(jnp.float32)
    mu = jnp.mean(xf, axis=-1, keepdims=True)
    var = jnp.mean(jnp.square(xf - mu), axis=-1, keepdims=True)
    y = (xf - mu) * lax.rsqrt(var + EPS)
    return (y * g.astype(jnp.float32) + b.astype(jnp.float32)).astype(x.dtype)

def modulate(h, shift, scale):
    return h * (1 + scale) + shift

def axial_angles(rows):
    row = jnp.repeat(jnp.arange(rows, dtype=jnp.float32), GRID_W)
    col = jnp.tile(jnp.arange(GRID_W, dtype=jnp.float32), rows)
    axis_dim = QK_ROPE // 2
    inv_freq = ROPE_THETA ** (-jnp.arange(0, axis_dim, 2, dtype=jnp.float32) / axis_dim)
    return row[:, None] * inv_freq, col[:, None] * inv_freq

def rotate_segment(x, ang):
    x1, x2 = jnp.split(x, 2, axis=-1)
    cos = jnp.cos(ang).astype(x.dtype)
    sin = jnp.sin(ang).astype(x.dtype)
    return jnp.concatenate([x1 * cos - x2 * sin, x2 * cos + x1 * sin], axis=-1)

def axial_rope(x, ang_row, ang_col):
    xr, xc = jnp.split(x, 2, axis=-1)
    return jnp.concatenate([rotate_segment(xr, ang_row), rotate_segment(xc, ang_col)], axis=-1)

def mla_query(q_a, g_q, w_uq):
    bsz, n, _ = q_a.shape
    q = (rms_norm(q_a, g_q) @ w_uq).reshape(bsz, n, N_HEADS, QK_NOPE + QK_ROPE)
    return q[..., :QK_NOPE], q[..., QK_NOPE:]

def mla_kv(kv_a, g_kv, w_ukv):
    bsz, n, _ = kv_a.shape
    kv = (rms_norm(kv_a, g_kv) @ w_ukv).reshape(bsz, n, N_HEADS, QK_NOPE + V_DIM)
    return kv[..., :QK_NOPE], kv[..., QK_NOPE:]

def mla_attend(q_nope, q_rope, k_nope, k_rope, v):
    s = (jnp.einsum('bqhd,bkhd->bhqk', q_nope, k_nope)
         + jnp.einsum('bqhr,bkr->bhqk', q_rope, k_rope))
    p = jax.nn.softmax(s.astype(jnp.float32) * ATTN_SCALE, axis=-1).astype(v.dtype)
    return jnp.einsum('bhqk,bkhd->bqhd', p, v)

def blocked_mla(q_nope, q_rope, k_nope, k_rope, v):
    bsz, n = q_nope.shape[:2]
    nb = n // Q_BLOCK

    def to_blocks(t):
        return jnp.moveaxis(t.reshape(bsz, nb, Q_BLOCK, *t.shape[2:]), 1, 0)

    out = lax.map(lambda qs: mla_attend(qs[0], qs[1], k_nope, k_rope, v),
                  (to_blocks(q_nope), to_blocks(q_rope)))
    return jnp.moveaxis(out, 0, 1).reshape(bsz, n, N_HEADS * V_DIM)

def conformer_conv(conv_in, w_dw, b_dw, ln_g, ln_b, w_pw):
    a, g = jnp.split(conv_in, 2, axis=-1)
    u = a * jax.nn.sigmoid(g)
    u = lax.conv_general_dilated(
        u, w_dw[:, None, :], window_strides=(1,),
        padding=((CONV_WIDTH // 2, CONV_WIDTH // 2),),
        dimension_numbers=('NWC', 'WIO', 'NWC'),
        feature_group_count=D_CONV) + b_dw
    u = jax.nn.silu(layer_norm(u, ln_g, ln_b))
    return u @ w_pw

def merge_branches(y_conv, y_mla, gates, w_out):
    g_conv, g_mla = jnp.split(gates, 2, axis=-1)
    return (jax.nn.sigmoid(g_conv) * y_conv + jax.nn.sigmoid(g_mla) * y_mla) @ w_out

def swiglu(h, w_13, w_2):
    a, b = jnp.split(h @ w_13, 2, axis=-1)
    return (jax.nn.silu(a) * b) @ w_2

def third_inputs(seed: int = 0) -> dict:
    key = jax.random.key(seed)
    ks = jax.random.split(key, 24)
    f32 = jnp.float32

    def nrm(k, shape, scale=1.0):
        return scale * jax.random.normal(k, shape, f32)

    def gain(k, n):
        return 1.0 + 0.01 * jax.random.normal(k, (DEPTH_3, n), f32)

    return {
        "x": nrm(ks[0], (BATCH, SEQ, D_MODEL)),
        "c": nrm(ks[1], (BATCH, D_MODEL)),
        "ctx": nrm(ks[2], (BATCH, CTX_LEN, D_MODEL)),
        "c_ctx": nrm(ks[3], (D_MODEL,)),
        "w_mod": nrm(ks[4], (DEPTH_3, D_MODEL, 6 * D_MODEL), 0.5 * D_MODEL ** -0.5),
        "b_mod": nrm(ks[5], (DEPTH_3, 6 * D_MODEL), 0.01),
        "g_mix": gain(ks[6], D_MODEL),
        "g_ffn": gain(ks[7], D_MODEL),
        "w_in": nrm(ks[8], (DEPTH_3, D_MODEL, D_IN), D_MODEL ** -0.5),
        "g_q": gain(ks[9], Q_LORA),
        "g_kv": gain(ks[10], KV_LORA),
        "w_uq": nrm(ks[11], (DEPTH_3, Q_LORA, N_HEADS * (QK_NOPE + QK_ROPE)), Q_LORA ** -0.5),
        "w_ukv": nrm(ks[12], (DEPTH_3, KV_LORA, N_HEADS * (QK_NOPE + V_DIM)), KV_LORA ** -0.5),
        "w_o_mla": nrm(ks[13], (DEPTH_3, N_HEADS * V_DIM, D_MODEL), (N_HEADS * V_DIM) ** -0.5),
        "w_dw": nrm(ks[14], (DEPTH_3, CONV_WIDTH, D_CONV), CONV_WIDTH ** -0.5),
        "b_dw": nrm(ks[15], (DEPTH_3, D_CONV), 0.01),
        "ln_g": gain(ks[16], D_CONV),
        "ln_b": nrm(ks[17], (DEPTH_3, D_CONV), 0.01),
        "w_pw": nrm(ks[18], (DEPTH_3, D_CONV, D_MODEL), D_CONV ** -0.5),
        "w_out": nrm(ks[19], (DEPTH_3, D_MODEL, D_MODEL), D_MODEL ** -0.5),
        "w_13": nrm(ks[20], (DEPTH_3, D_MODEL, 2 * D_FF_3), D_MODEL ** -0.5),
        "w_2": nrm(ks[21], (DEPTH_3, D_FF_3, D_MODEL), D_FF_3 ** -0.5),
        "g_final": 1.0 + 0.01 * jax.random.normal(ks[22], (D_MODEL,), f32),
    }

def third_block(x, c, ctx, c_ctx, w_mod, b_mod, g_mix, g_ffn, w_in, g_q, g_kv, w_uq, w_ukv,
              w_o_mla, w_dw, b_dw, ln_g, ln_b, w_pw, w_out, w_13, w_2, g_final):
    bsz, n, _ = x.shape
    ROWS = n // GRID_W
    ang_r, ang_c = axial_angles(ROWS)
    silu_c = jax.nn.silu(c)
    silu_cc = jax.nn.silu(c_ctx)

    for l in range(DEPTH_3):
        last = l == DEPTH_3 - 1
        mx = jnp.split((silu_c @ w_mod[l] + b_mod[l])[:, None, :], 6, axis=-1)
        mc = jnp.split(silu_cc @ w_mod[l] + b_mod[l], 6, axis=-1)

        hx = modulate(rms_norm(x, g_mix[l]), mx[0], mx[1])
        hc = modulate(rms_norm(ctx, g_mix[l]), mc[0], mc[1])

        zx = hx @ w_in[l]
        conv_x, qa_x, kva_x, kr_x, gt_x = jnp.split(
            zx, [_OFF_Q, _OFF_KV, _OFF_KR, _OFF_GATE], axis=-1)
        qn_x, qr_x = mla_query(qa_x, g_q[l], w_uq[l])
        kn_x, v_x = mla_kv(kva_x, g_kv[l], w_ukv[l])
        qr_x = axial_rope(qr_x, ang_r[:, None], ang_c[:, None])
        kr_x = axial_rope(kr_x, ang_r, ang_c)

        if last:
            zc = hc @ w_in[l][:, _OFF_KV:_OFF_GATE]
            kva_c, kr_c = jnp.split(zc, [KV_LORA], axis=-1)
        else:
            zc = hc @ w_in[l]
            conv_c, qa_c, kva_c, kr_c, gt_c = jnp.split(
                zc, [_OFF_Q, _OFF_KV, _OFF_KR, _OFF_GATE], axis=-1)
        kn_c, v_c = mla_kv(kva_c, g_kv[l], w_ukv[l])

        k_nope = jnp.concatenate([kn_c, kn_x], axis=1)
        k_rope = jnp.concatenate([kr_c, kr_x], axis=1)
        v_all = jnp.concatenate([v_c, v_x], axis=1)
        att_x = blocked_mla(qn_x, qr_x, k_nope, k_rope, v_all) @ w_o_mla[l]
        y_conv_x = conformer_conv(conv_x, w_dw[l], b_dw[l], ln_g[l], ln_b[l], w_pw[l])
        x = x + mx[2] * merge_branches(y_conv_x, att_x, gt_x, w_out[l])

        hx2 = modulate(rms_norm(x, g_ffn[l]), mx[3], mx[4])
        x = x + mx[5] * swiglu(hx2, w_13[l], w_2[l])

        if not last:
            qn_c, qr_c = mla_query(qa_c, g_q[l], w_uq[l])
            att_c = mla_attend(qn_c, qr_c, kn_c, kr_c, v_c).reshape(
                bsz, ctx.shape[1], N_HEADS * V_DIM) @ w_o_mla[l]
            y_conv_c = conformer_conv(conv_c, w_dw[l], b_dw[l], ln_g[l], ln_b[l], w_pw[l])
            ctx = ctx + mc[2] * merge_branches(y_conv_c, att_c, gt_c, w_out[l])
            hc2 = modulate(rms_norm(ctx, g_ffn[l]), mc[3], mc[4])
            ctx = ctx + mc[5] * swiglu(hc2, w_13[l], w_2[l])

    return rms_norm(x, g_final)


_first_inputs_3 = third_inputs


def third_inputs(seed=0):
    import zlib

    import numpy as np

    out = dict(_first_inputs_3(seed))
    spreads = {}
    factors = {'ctx': 8.0,
     'c_ctx': 3.62,
     'b_mod': 6.151,
     'g_mix': 8.0,
     'g_ffn': 31.908,
     'g_q': 8.0,
     'g_kv': 8.0,
     'w_uq': 4.091,
     'b_dw': 42.24,
     'ln_g': 61.532,
     'ln_b': 60.071,
     'g_final': 32.671}
    for name, (base, spread) in spreads.items():
        noise = np.random.default_rng([zlib.crc32(name.encode()), seed]).standard_normal(out[name].shape)
        drawn = base * np.exp(spread * noise) if base else spread * noise
        out[name] = __import__('jax').numpy.asarray(drawn.astype(out[name].dtype))
    for name, factor in factors.items():
        out[name] = (out[name] * factor).astype(out[name].dtype)
    return out


_narrow_inputs_3 = third_inputs


def third_inputs(seed=0):

    out = dict(_narrow_inputs_3(seed))
    wider = {'g_ffn': 4.43, 'ln_g': 4.66, 'ln_b': 4.63, 'g_final': 6.49}
    for name, times in wider.items():
        mean = out[name].mean()
        out[name] = (mean + times * (out[name] - mean)).astype(out[name].dtype)
    return out


def setup_inputs(seed=0):
    out = dict(first_inputs(seed))
    for name, value in second_inputs(seed + 1).items():
        if name != "x":
            out[name + "_2"] = value
    for name, value in third_inputs(seed + 2).items():
        if name != "x":
            out[name + "_3"] = value
    return out


def reference(
    x, norm1_w, norm2_w, a_w_in, a_lb_logits, a_norm_w, a_w_out, b_w_in, b_conv_w, b_conv_b,
    b_dt_bias, b_a_log, b_d_skip, b_norm_w, b_w_out, ffn_w_in, ffn_conv_w, ffn_conv_b,
    ffn_w_out, final_norm_w, p_2, w_in_2, w_up_a_2, w_up_b_2, w_o_2, w_ff1_2, w_ff2_2, w_pe_2,
    w_pg_2, g_mix_2, g_mlp_2, g_pe_2, g_final_2, sinks_2, rel_bias_2, c_3, ctx_3, c_ctx_3,
    w_mod_3, b_mod_3, g_mix_3, g_ffn_3, w_in_3, g_q_3, g_kv_3, w_uq_3, w_ukv_3, w_o_mla_3,
    w_dw_3, b_dw_3, ln_g_3, ln_b_3, w_pw_3, w_out_3, w_13_3, w_2_3, g_final_3,
):
    x = first_block(
        x, norm1_w, norm2_w, a_w_in, a_lb_logits, a_norm_w, a_w_out, b_w_in, b_conv_w, b_conv_b,
        b_dt_bias, b_a_log, b_d_skip, b_norm_w, b_w_out, ffn_w_in, ffn_conv_w, ffn_conv_b,
        ffn_w_out, final_norm_w,
    )
    x = second_block(
        x, p_2, w_in_2, w_up_a_2, w_up_b_2, w_o_2, w_ff1_2, w_ff2_2, w_pe_2, w_pg_2, g_mix_2,
        g_mlp_2, g_pe_2, g_final_2, sinks_2, rel_bias_2,
    )
    return third_block(
        x, c_3, ctx_3, c_ctx_3, w_mod_3, b_mod_3, g_mix_3, g_ffn_3, w_in_3, g_q_3, g_kv_3,
        w_uq_3, w_ukv_3, w_o_mla_3, w_dw_3, b_dw_3, ln_g_3, ln_b_3, w_pw_3, w_out_3, w_13_3,
        w_2_3, g_final_3,
    )


_drawn_inputs = setup_inputs


def setup_inputs(seed=0):
    import zlib

    import numpy as np

    out = dict(_drawn_inputs(seed))
    spreads = {}
    factors = {}
    for name, (base, spread) in spreads.items():
        noise = np.random.default_rng([zlib.crc32(name.encode()), seed]).standard_normal(out[name].shape)
        drawn = base * np.exp(spread * noise) if base else spread * noise
        out[name] = __import__('jax').numpy.asarray(drawn.astype(out[name].dtype))
    for name, factor in factors.items():
        out[name] = (out[name] * factor).astype(out[name].dtype)
    return out
```

```python
from collections import deque
from contextlib import ExitStack

import numpy as np
import concourse.bass as bass
from concourse import mybir

F32 = mybir.dt.float32
F32R = mybir.dt.float32r
U8 = mybir.dt.uint8
ALU = mybir.AluOpType
ACT = mybir.ActivationFunctionType
AX_X = mybir.AxisListType.X
ADD, SUB, MUL, MAX, MIN = ALU.add, ALU.subtract, ALU.mult, ALU.max, ALU.min

P = 128
T = 512
NT = T // P
D = 1024
DT = D // P
SLOT = 2048
N_STAGE = 2
N_SPLIT = 3
LEAD = 2
EPS = 1e-6
NEG = -1e30

HG_HEADS = 8
GROUPS = 8
HEADS_PER_GROUP = 4
HEAD_P = 64
D_INNER = 2048
GN = 1024
N_DT = 64
FF = 2816
FF_TILES = FF // P
FF2_TILES = 4096 // P
N_BUCKETS = 32
WINDOW = 128
CTX = 256
KEYS = CTX + T
KT3 = KEYS // P
QK_NOPE = 128
QK_ROPE = 64
ATTN_SCALE = float((QK_NOPE + QK_ROPE) ** -0.5)
CONV_W = 31
HALO = CONV_W // 2
SUB_LEVELS = [1, 2, 4, 8, 16, 32, 64]



def chunks_of(n, size):
    return [(a, min(size, n - a)) for a in range(0, n, size)]


def ffn_plan(tag, n_tiles, hidden_slots, out_name, out_index, extra=()):
    extra = list(extra)
    plan = []
    parts = chunks_of(n_tiles, 4)
    for i in range(len(parts) + 1):
        if i < len(parts):
            for slot in hidden_slots(*parts[i]):
                plan.append(slot)
                if extra:
                    plan.append(extra.pop(0))
        if i > 0:
            t0, n = parts[i - 1]
            width = SLOT // n
            for c in range(0, D, width):
                plan.append(((tag + "_out", t0, c), n, [(out_name, out_index, t0 * P, c, width)]))
    return plan + extra


def weight_plan():
    plan = []
    for h in range(HG_HEADS):
        a = ("a_w_in", 0, 0)
        if h % 2 == 0:
            plan.append((("gla_v", h), DT, [(*a, 3 * D + h * P, 2 * P)]))
        plan.append((("gla_qf", h), DT, [(*a, h * P, P), (*a, D + h * P, P)]))
        plan.append((("gla_bg", h), DT, [(*a, 2 * D + h * P, P), (*a, 4 * D + h * P, P)]))
    for c in range(0, D, 256):
        plan.append((("gla_out", c), DT, [("a_w_out", 0, 0, c, 256)]))

    def glu(tag, name, index):
        def slots(t0, n):
            return [((tag, t), DT, [(name, index, 0, t * P, P), (name, index, 0, FF + t * P, P)])
                    for t in range(t0, t0 + n)]
        return slots

    mod = [(("mod", c), DT, [("w_mod_3", 0, 0, c, 256)]) for c in range(0, 6 * D, 256)]
    plan += ffn_plan("ffn0", FF_TILES, glu("ffn0", "ffn_w_in", 0), "ffn_w_out", 0, mod)
    b = ("b_w_in", 0, 0)
    plan.append((("m_dt",), DT, [(*b, 2 * D_INNER + 2 * GN, N_DT)]))

    def m_proj(g):
        return [(("m_x", g), DT, [(*b, D_INNER + g * 256, 256)]),
                (("m_bc", g), DT, [(*b, 2 * D_INNER + g * P, P), (*b, 2 * D_INNER + GN + g * P, P)])]
    plan += m_proj(0)
    for g in range(GROUPS):
        plan.append((("m_z", g), DT, [(*b, g * 256, 256)]))
        if g + 1 < GROUPS:
            plan += m_proj(g + 1)
        plan.append((("m_out", g), 2, [("b_w_out", 0, g * 256, 0, D)]))
    plan += ffn_plan("ffn1", FF_TILES, glu("ffn1", "ffn_w_in", 1), "ffn_w_out", 1)

    w = ("w_in_2", 0, 0)
    plan.append((("b2_w_k",), DT, [(*w, 2048 + 64 * (i // 2), 64) for i in range(4)]))
    plan.append((("b2_w_v",), DT, [(*w, 2176, 128)]))
    for c in (0, 256):
        plan.append((("b2_w_q", c), DT, [(*w, 1536 + c, 256)]))
    for p in range(4):
        if p % 2 == 0:
            plan.append((("b2_s_v", p), DT, [(*w, 1024 + p * P, 256)]))
        plan.append((("b2_s_qk", p), DT, [(*w, p * P, P), (*w, 512 + p * P, P)]))
    for c in (0, 512):
        plan.append((("b2_up_a", c), 4, [("w_up_a_2", 0, 0, c, 512)]))
    for c in range(0, D, 256):
        plan.append((("b2_gate_a", c), DT, [(*w, 2304 + c, 256)]))
    for c in (0, 512):
        plan.append((("b2_up_b", c), 4, [("w_up_b_2", 0, 0, c, 512)]))
    for c in range(0, D, 256):
        plan.append((("b2_gate_b", c), DT, [(*w, 3328 + c, 256)]))
    for c in range(0, D, 256):
        plan.append((("b2_o", c), DT, [("w_o_2", 0, 0, c, 256)]))

    def ff1(t0, n):
        return [(("ff2", t), DT, [("w_ff1_2", 0, 0, t * P, 256)]) for t in range(t0, t0 + n, 2)]
    plan += ffn_plan("ff2", FF2_TILES, ff1, "w_ff2_2", 0)
    plan.append((("b2_pe",), 2, [("w_pe_2", 0, 0, 0, D)]))
    for c in range(0, D, 256):
        plan.append((("b2_pg", c), DT, [("w_pg_2", 0, 0, c, 256)]))

    w = ("w_in_3", 0, 0)
    plan.append((("c_kv",), DT, [(*w, 2432, 256)]))
    plan.append((("c_kr",), DT, [(*w, 2688, QK_ROPE)]))
    plan.append((("c_q",), DT, [(*w, 2048, 256)]))
    plan.append((("c_q2",), DT, [(*w, 2304, 128)]))
    for t in range(DT):
        plan.append((("c_conv", t), DT, [(*w, t * P, P), (*w, D + t * P, P)]))
    for h in range(8):
        plan.append((("c_ukv", h), 2, [("w_ukv_3", 0, 0, h * 256, 256)]))
        plan.append((("c_uq", h), 3, [("w_uq_3", 0, 0, h * 192, 192)]))
    for c in range(0, 2 * D, 256):
        plan.append((("c_gate", c), DT, [(*w, 2752 + c, 256)]))
    for c in range(0, D, 256):
        plan.append((("c_omla", c), DT, [("w_o_mla_3", 0, 0, c, 256)]))
    for c in range(0, D, 256):
        plan.append((("c_pw", c), DT, [("w_pw_3", 0, 0, c, 256)]))
    for c in range(0, D, 256):
        plan.append((("c_out", c), DT, [("w_out_3", 0, 0, c, 256)]))
    plan += ffn_plan("ffn3", FF_TILES, glu("ffn3", "w_13_3", 0), "w_2_3", 0)
    return plan


def column_plan():
    n = [("norm1", 16), ("norm2", 16), ("lb", 24), ("a_norm", 1), ("conv_w", 5 * 32), ("conv_b", 32),
         ("d_skip", 16), ("b_norm", 16), ("dt_bias", 1), ("a_log", 1), ("ffn_cw", 2 * 3 * FF_TILES),
         ("ffn_cb", 2 * FF_TILES), ("final", 8), ("g_mix_2", 8), ("g_mlp_2", 8), ("g_pe_2", 8),
         ("g_final_2", 8), ("c_c", 16), ("b_mod", 48), ("g_mix_3", 8), ("g_ffn_3", 8), ("g_q", 3),
         ("g_kv", 2), ("w_dw", 31 * 8), ("b_dw", 8), ("ln_g", 8), ("ln_b", 8), ("g_final_3", 8)]
    at, out = 0, {}
    for name, count in n:
        out[name] = (at, count)
        at += count
    return out, at


def bucket_of(dist):
    d = np.maximum(dist, 0)
    df = np.maximum(d, 1).astype(np.float32)
    large = 16 + (np.log(df / np.float32(16)) / np.float32(np.log(8.0)) * np.float32(16)).astype(np.int32)
    return np.where(d < 16, d, np.minimum(large, N_BUCKETS - 1))


def shape_constants():
    s, t = np.arange(P)[:, None], np.arange(P)[None, :]
    levels = np.zeros((P, len(SUB_LEVELS) + 1, P), np.float32)
    for i, half in enumerate(SUB_LEVELS):
        levels[:, i, :] = (s // (2 * half) == t // (2 * half)) & (s // half != t // half)
    levels[:, len(SUB_LEVELS), :] = s > t
    f = np.zeros((P, 8, P), np.float32)
    f[:, 0, :] = s == t
    f[:, 1, :] = 1.0
    f[:, 2, :] = s <= t
    f[:, 3, :] = s >= t
    f[:, 4, :] = s < t
    f[:, 5, :] = s > t
    for base in range(0, P, 32):
        for i in range(16):
            f[base + 16 + i, 6, base + i] = -1.0
            f[base + i, 6, base + 16 + i] = 1.0
    f[:, 7, :] = s + t == P - 1
    dist = 255 - np.arange(384)
    onehot = np.zeros((N_BUCKETS, 384), np.float32)
    inside = (dist >= 0) & (dist < WINDOW)
    onehot[bucket_of(dist)[inside], np.nonzero(inside)[0]] = 1.0
    outside = np.zeros((8, 384), np.float32)
    outside[:, ~inside] = NEG
    pos = np.arange(T)
    inv = (np.float32(10000.0) ** (-np.arange(0, 32, 2, dtype=np.float32) / np.float32(32))).astype(np.float32)
    row = (pos // 64).astype(np.float32)[None, :] * inv[:, None]
    col = (pos % 64).astype(np.float32)[None, :] * inv[:, None]
    ang = np.concatenate([row, row, col, col] * 2, 0)
    rope = np.stack([np.cos(ang), np.sin(ang)], 1).astype(np.float32)
    return {"const_levels": levels, "const_f": f, "const_onehot": onehot, "const_outside": outside,
            "const_rope": rope}



class Engine:

    def __init__(self, e, done):
        self.e, self.done, self.count, self.passed = e, done, 0, {}

    def wait(self, *marks):
        for sem, value in marks:
            if value > self.passed.get(sem.name, 0):
                self.passed[sem.name] = value
                self.e.wait_ge(sem, value)

    def __call__(self, instruction, *marks):
        self.wait(*marks)
        instruction(self.e).then_inc(self.done, 1)
        self.count += 1
        return (self.done, self.count)

    def quiet(self, instruction, *marks):
        self.wait(*marks)
        instruction(self.e)

    def last(self):
        return (self.done, self.count)


class Buf:

    def __init__(self, ap):
        self.ap, self.busy = ap, ()


class Pool_of:

    def __init__(self, bufs):
        self.idle = deque(bufs)

    def take(self):
        return self.idle.popleft()

    def give(self, buf, *marks):
        buf.busy = marks
        self.idle.append(buf)


def together(*gens):
    gens = [(list(g) if isinstance(g, (list, tuple)) else g) for g in gens]
    live = [g for g in gens if g is not None]
    while live:
        for g in list(live):
            try:
                next(g)
            except StopIteration:
                live.remove(g)


def run(g):
    for _ in g:
        pass


def build(nc, ins, out, debug=None):
    plan = weight_plan()
    cols, n_cols = column_plan()
    ctx = ExitStack()
    with ctx:
        def sb(name, shape, dt=F32, c=ctx):
            return c.enter_context(nc.sbuf_tensor(name, shape, dt))

        def sem(name):
            return ctx.enter_context(nc.semaphore(name))

        PE = Engine(nc.tensor, sem("pe_done"))
        VE = Engine(nc.vector, sem("vector_done"))
        AC = Engine(nc.scalar, sem("scalar_done"))
        PO = Engine(nc.gpsimd, sem("pool_done"))
        SP = Engine(nc.sync, sem("sync_done"))
        s_stage = [sem(f"stage{i}_filled") for i in range(N_STAGE)]
        s_load = sem("constants_loaded")
        s_io = sem("scratch_dma")

        psum = ctx.enter_context(nc.psum_tensor("banks", [P, 8, T], F32))
        banks = Pool_of([Buf(psum[:, i, :]) for i in range(8)])

        x = sb("x", [P, DT, T])
        u_hi, u_lo = sb("u_hi", [P, DT, T], F32R), sb("u_lo", [P, DT, T], F32R)
        stage = sb("stage", [P, N_STAGE, SLOT])
        w_hi, w_lo = sb("w_hi", [P, N_SPLIT, SLOT], F32R), sb("w_lo", [P, N_SPLIT, SLOT], F32R)
        vec = sb("vec", [P, n_cols])
        cf = sb("cf", [P, 8, P])
        ident, ones, m_le, m_ge, m_lt, m_gt, rotate, turn = (cf[:, i, :] for i in range(8))
        levels = sb("levels", [P, len(SUB_LEVELS) + 1, P], U8)
        modv = sb("modv", [P, 48, 2])
        work = Pool_of([Buf(sb(f"work{i}", [P, T])[:, :]) for i in range(4)])

        def column(name, i, n=1):
            return vec[:, cols[name][0] + i:cols[name][0] + i + n]

        def load(dst, src):
            nc.sync.dma_start(dst, src).then_inc(s_load, 16)
            load.count += 16
        load.count = 0
        load(x[:, :, :], ins["x_t"].rearrange("(k p) t -> p k t", p=P))
        load(vec[:, :], ins["vectors"])
        load(cf[:, :, :], ins["const_f"])
        levels_scope = ExitStack()
        levels_f = sb("levels_f", [P, len(SUB_LEVELS) + 1, P], F32, levels_scope)
        load(levels_f[:, :, :], ins["const_levels"])
        loaded = (s_load, load.count)
        VE(lambda e: e.tensor_copy(levels[:, :, :], levels_f[:, :, :]), loaded)

        stream = {"loaded": 0, "split": 0, "used": 0}
        released = {}
        split_busy = [()] * N_SPLIT
        split_at = {}
        n_split = [0]
        split_ready = {}
        limit = len(plan) if debug is None else debug.get("slots", len(plan))

        def is_raw(s):
            return plan[s][0][0] == "mod"

        def slot_size(s):
            return plan[s][1] * sum(piece[4] for piece in plan[s][2])

        def pump():
            while stream["loaded"] < limit:
                s = stream["loaded"]
                if s >= N_STAGE and s - N_STAGE not in released:
                    return
                stream["loaded"] = s + 1
                SP.wait(*released.get(s - N_STAGE, ()))
                n = slot_size(s)
                nc.sync.dma_start(stage[:, s % N_STAGE, 0:n], ins["weights"][s, :, 0:n]).then_inc(
                    s_stage[s % N_STAGE], 16)

        def filled(s):
            return (s_stage[s % N_STAGE], 16 * (s // N_STAGE + 1))

        def split(s):
            if s >= limit or s < stream["split"]:
                return
            stream["split"] = s + 1
            if is_raw(s):
                return
            b, n, st = n_split[0] % N_SPLIT, slot_size(s), s % N_STAGE
            n_split[0] += 1
            split_at[s] = b
            m_hi = AC(lambda e: e.activation(w_hi[:, b, 0:n], stage[:, st, 0:n], ACT.Copy),
                      filled(s), *split_busy[b])
            m_lo = PO(lambda e: e.tensor_tensor(w_lo[:, b, 0:n], stage[:, st, 0:n],
                                                w_hi[:, b, 0:n].bitcast(F32), SUB), filled(s), m_hi,
                      *split_busy[b])
            split_ready[s] = (m_hi, m_lo)
            released[s] = (m_hi, m_lo)
            pump()

        pump()

        class Weights:
            pass

        def use(key):
            s = stream["used"]
            assert plan[s][0] == key, (plan[s][0], key)
            stream["used"] = s + 1
            for i in range(s, s + LEAD + 1):
                split(i)
            w = Weights()
            w.s, kt = s, plan[s][1]
            n = slot_size(s)
            if is_raw(s):
                w.raw = stage[:, s % N_STAGE, 0:n].rearrange("p (k c) -> p k c", k=kt)
                w.ready = (filled(s),)
                w.b = None
            else:
                w.b = split_at[s]
                w.hi = w_hi[:, w.b, 0:n].rearrange("p (k c) -> p k c", k=kt)
                w.lo = w_lo[:, w.b, 0:n].rearrange("p (k c) -> p k c", k=kt)
                w.ready = split_ready[s]
            return w

        def used(w, mark):
            if w.b is None:
                released[w.s] = (mark,)
                pump()
            else:
                split_busy[w.b] = (mark,)

        def product(bank, dst, terms, *marks):
            PE.wait(*bank.busy, *marks)
            for i, (a_hi, a_lo, b_hi, b_lo, need) in enumerate(terms):
                PE.wait(*need)
                first, end = i == 0, i == len(terms) - 1
                nc.tensor.matmul(dst, a_hi, b_hi, start=first, stop=False)
                nc.tensor.matmul(dst, a_hi, b_lo, start=False, stop=False)
                last = nc.tensor.matmul(dst, a_lo, b_hi, start=False, stop=end)
            last.then_inc(PE.done, 1)
            PE.count += 1
            return PE.last()

        class Split:

            def __init__(self, hi, lo, n):
                self.hi, self.lo, self.n = hi, lo, n
                self.ready = [()] * n
                self.busy = ()

        U = Split(u_hi, u_lo, DT)

        def split_to(dst, k, src, m_src, n=T, c0=0, on=None):
            hi, lo = dst.hi[:, k, c0:c0 + n], dst.lo[:, k, c0:c0 + n]
            m1 = AC(lambda e: e.activation(hi, src, ACT.Copy), *m_src, *dst.busy)
            m2 = (on or VE)(lambda e: e.tensor_tensor(lo, src, hi.bitcast(F32), SUB), m1, *m_src, *dst.busy)
            dst.ready[k] = (*dst.ready[k], m1, m2)
            return (m1, m2)

        def feature_tile(w, c, X, width=P, n=T, c0=0):
            bank = banks.take()
            kt = plan[w.s][1]
            terms = [(w.hi[:, k, c:c + width], w.lo[:, k, c:c + width], X.hi[:, k, c0:c0 + n],
                      X.lo[:, k, c0:c0 + n], X.ready[k]) for k in range(kt)]
            return bank, product(bank, bank.ap[0:width, 0:n], terms, *w.ready)

        def token_tile(w, c, width, X, t0):
            bank = banks.take()
            kt = plan[w.s][1]
            terms = [(X.hi[:, k, t0:t0 + P], X.lo[:, k, t0:t0 + P], w.hi[:, k, c:c + width],
                      w.lo[:, k, c:c + width], X.ready[k]) for k in range(kt)]
            return bank, product(bank, bank.ap[:, 0:width], terms, *w.ready)

        def fmm(bank_ap, pairs, *marks):
            PE.wait(*marks)
            for i, (a, b) in enumerate(pairs):
                last = nc.tensor.matmul(bank_ap, a, b, start=i == 0, stop=i == len(pairs) - 1)
            last.then_inc(PE.done, 1)
            PE.count += 1
            return PE.last()

        def inverse_rms(tiles, width, n=T, rows=P):
            bank = banks.take()
            PE.wait(*bank.busy)
            for i, (ap, marks) in enumerate(tiles):
                sq = work.take()
                m = AC(lambda e: e.activation(sq.ap[:, 0:n], ap, ACT.Square), *marks, *sq.busy)
                last = PE(lambda e: e.matmul(bank.ap[:, 0:n], ones, sq.ap[:, 0:n], start=i == 0,
                                             stop=i == len(tiles) - 1), m, loaded)
                work.give(sq, last)
            r = work.take()
            m = VE(lambda e: e.tensor_scalar(r.ap[:, 0:n], bank.ap[:, 0:n], 1.0 / width, EPS, MUL, ADD),
                   last, *r.busy)
            banks.give(bank, m)
            m = AC(lambda e: e.activation(r.ap[:, 0:n], r.ap[:, 0:n], ACT.Sqrt), m)
            m = VE(lambda e: e.reciprocal(r.ap[:, 0:n], r.ap[:, 0:n]), m)
            return r, m

        x_ready = [(loaded,) for _ in range(DT)]

        def norm_to(dst, tiles, gains, width, n=T, c0=0, shifts=None, need=()):
            r, m_r = inverse_rms(tiles, width, n)
            readers = []
            for k, (ap, marks) in enumerate(tiles):
                t = work.take()
                m = VE(lambda e: e.scalar_tensor_tensor(out=t.ap[:, 0:n], in0=ap, scalar=gains(k),
                                                        in1=r.ap[:, 0:n], op0=MUL, op1=MUL),
                       m_r, loaded, *need, *marks, *t.busy)
                readers.append(m)
                if shifts is not None:
                    m = VE(lambda e: e.tensor_scalar(t.ap[:, 0:n], t.ap[:, 0:n], shifts(k), None, ADD), m)
                dst.ready[k] = () if c0 == 0 else dst.ready[k]
                work.give(t, *split_to(dst, k, t.ap[:, 0:n], (m,), n, c0))
            work.give(r, readers[-1])
            return readers

        def x_tiles():
            return [(x[:, k, :], x_ready[k]) for k in range(DT)]

        def add_to_x(k, bank, mark, scale=None):
            if scale is None:
                m = VE(lambda e: e.tensor_tensor(x[:, k, :], x[:, k, :], bank.ap, ADD), mark, *x_ready[k])
            else:
                m = VE(lambda e: e.scalar_tensor_tensor(out=x[:, k, :], in0=bank.ap, scalar=scale(k), in1=x[:, k, :],
                                                        op0=MUL, op1=ADD), mark, *x_ready[k])
            x_ready[k] = (m,)
            banks.give(bank, m)

        def barrier():
            marks = [e.last() for e in (PE, VE, AC, PO) if e.count]
            for e in (PE, VE, AC, PO, SP):
                e.wait(*[m for m in marks if m[0] is not e.done])
            for e in (PE, VE, AC, PO):
                e.wait(e.last()) if e.count else None

        def begin_u():
            U.busy = (PE.last(),) if PE.count else ()
            U.ready = [()] * DT

        for e in (PE, VE, AC, PO):
            e.wait(loaded)
        levels_scope.close()
        barrier()

        def hgrn2():
            with ExitStack() as c:
                def s(name, shape, dt=F32):
                    return sb("gla_" + name, shape, dt, c)

                o = s("o", [P, DT, T])
                o_ready = [None] * DT
                lbe = s("lbe", [P, 3, DT])
                lbs = s("lbs", [P, 4, DT])
                reset = s("reset", [P, T])
                v = [Buf(s(f"v{i}", [P, NT, 256])) for i in range(2)]
                names = ("q", "kf", "kb", "lf", "lb", "gs")
                per_head = [{n: s(f"{n}{i}", [P, T]) for n in names} for i in range(2)]
                head_busy = [(), ()]
                cf_, cb_ = s("cum_f", [P, T]), s("cum_b", [P, T])
                ex = [Buf(s(f"ex{i}", [P, 2, T])) for i in range(2)]
                A = s("att", [P, T])
                k1t = s("k1t", [P, T])
                states = s("states", [P, 2, 3, P])
                e_tot = s("e_tot", [P, 2, NT])
                a_busy = [()]
                k1t_busy = [()]
                states_busy = [()]
                cum_busy = [()]

                lg = column("lb", 0, 24).rearrange("p (r k) -> p r k", r=3)
                m = VE(lambda e: e.tensor_tensor(lbs[:, 0, :], lg[:, 0, :], lg[:, 1, :], MAX), loaded)
                m = VE(lambda e: e.tensor_tensor(lbs[:, 0, :], lbs[:, 0, :], lg[:, 2, :], MAX), m)
                for i in range(3):
                    last = VE(lambda e: e.tensor_tensor(lbe[:, i, :], lg[:, i, :], lbs[:, 0, :], SUB), m)
                m = AC(lambda e: e.activation(lbe[:, :, :], lbe[:, :, :], ACT.Exp), last)
                m = VE(lambda e: e.tensor_tensor(lbs[:, 1, :], lbe[:, 0, :], lbe[:, 1, :], ADD), m)
                m = VE(lambda e: e.tensor_tensor(lbs[:, 1, :], lbs[:, 1, :], lbe[:, 2, :], ADD), m)
                m = VE(lambda e: e.reciprocal(lbs[:, 1, :], lbs[:, 1, :]), m)
                m = VE(lambda e: e.tensor_tensor(lbs[:, 2, :], lbe[:, 0, :], lbs[:, 1, :], MUL), m)
                m_lb = VE(lambda e: e.tensor_scalar(lbs[:, 3, :], lbs[:, 2, :], -1.0, 1.0, MUL, ADD), m)
                m = VE(lambda e: e.memset(reset[:, :], 1.0))
                for i in range(NT):
                    m_reset = VE(lambda e: e.memset(reset[:, i * P:i * P + 1], 0.0), m)

                begin_u()
                norm_to(U, x_tiles(), lambda k: column("norm1", k), D)
                kept = {}

                def project(h):
                    b = per_head[h % 2]
                    vb = v[h // 2 % 2]
                    if h % 2 == 0:
                        w = use(("gla_v", h))
                        marks = []
                        for t in range(NT):
                            bank, m = token_tile(w, 0, 256, U, t * P)
                            marks.append(AC(lambda e: e.activation(vb.ap[:, t, :], bank.ap[:, 0:256], ACT.Copy),
                                            m, *vb.busy))
                            banks.give(bank, marks[-1])
                        used(w, m)
                        kept["v", h // 2] = marks
                        yield
                    w = use(("gla_qf", h))
                    busy = head_busy[h % 2]

                    def swish(c, dst):
                        bank, m = feature_tile(w, c, U)
                        m1 = AC(lambda e: e.activation(dst, bank.ap, ACT.Sigmoid), m, *busy)
                        m2 = VE(lambda e: e.tensor_tensor(dst, bank.ap, dst, MUL), m1)
                        banks.give(bank, m2)
                        return m, m2

                    def gate(c, k_dst, l_dst):
                        bank, m = feature_tile(w, c, U)
                        m1 = AC(lambda e: e.activation(l_dst, bank.ap, ACT.Sigmoid), m, *busy)
                        banks.give(bank, m1)
                        m2 = VE(lambda e: e.tensor_scalar(l_dst, l_dst, lbs[:, 3, h:h + 1], lbs[:, 2, h:h + 1],
                                                          MUL, ADD), m1, m_lb)
                        m3 = VE(lambda e: e.tensor_scalar(k_dst, l_dst, -1.0, 1.0, MUL, ADD), m2)
                        return m, (l_dst, m3)

                    _, kept["q", h] = swish(0, b["q"][:, :])
                    m, g1 = gate(P, b["kf"][:, :], b["lf"][:, :])
                    used(w, m)
                    yield
                    w = use(("gla_bg", h))
                    _, g2 = gate(0, b["kb"][:, :], b["lb"][:, :])
                    m, kept["gs", h] = swish(P, b["gs"][:, :])
                    used(w, m)
                    for name, (ap, m3) in (("lf", g1), ("lb", g2)):
                        kept[name, h] = AC(lambda e: e.activation(ap, ap, ACT.Ln), m3)
                    kept["k", h] = g2[1]
                    yield

                def attend(h):
                    b = per_head[h % 2]
                    q, kf, kb, lf, lbw, gs = (b[n][:, :] for n in names)
                    vv = v[h // 2 % 2].ap[:, :, (h % 2) * P:(h % 2) * P + P]
                    mf = VE(lambda e: e.tensor_tensor_scan(cf_[:, :], reset[:, :], lf, 0.0, MUL, ADD),
                            kept["lf", h], m_reset, *cum_busy[0])
                    mb = VE(lambda e: e.tensor_tensor_scan(cb_[:, ::-1], reset[:, :], lbw[:, ::-1], 0.0, MUL, ADD),
                            kept["lb", h], *cum_busy[0])
                    f4 = cf_[:, :].rearrange("p (c t) -> p c t", c=NT)
                    b4 = cb_[:, :].rearrange("p (c t) -> p c t", c=NT)
                    f_end, b_end = f4[:, :, P - 1:P], b4[:, :, 0:1]
                    m_et = AC(lambda e: e.activation(e_tot[:, 0, :], f_end.rearrange("p c t -> p (c t)"), ACT.Exp),
                              mf, *states_busy[0])
                    m_et = AC(lambda e: e.activation(e_tot[:, 1, :], b_end.rearrange("p c t -> p (c t)"), ACT.Exp), mb)
                    q_ready, k_ready = kept["q", h], kept["k", h]

                    e0 = ex[0]
                    m = VE(lambda e: e.tensor_tensor(e0.ap[:, 0, :], kf, kb, ADD), k_ready, *e0.busy)
                    bank = banks.take()
                    PE.wait(*bank.busy, q_ready)
                    for c_ in range(NT):
                        sl = slice(c_ * P, c_ * P + P)
                        m_pe = PE(lambda e: e.matmul(bank.ap[:, sl], e0.ap[:, 0, sl], q[:, sl], start=True,
                                                     stop=True), m)
                    e0.busy = (m_pe,)
                    m_a = VE(lambda e: e.tensor_copy(A[:, :], bank.ap), m_pe, *a_busy[0])
                    banks.give(bank, m_a)
                    yield

                    for lv, half in enumerate(SUB_LEVELS):
                        eb = ex[(lv + 1) % 2]
                        E = eb.ap[:, :, :].rearrange("p a (n s h) -> p a n s h", s=2, h=half)
                        fv = cf_[:, :].rearrange("p (n s h) -> p n s h", s=2, h=half)
                        bv = cb_[:, :].rearrange("p (n s h) -> p n s h", s=2, h=half)
                        shape = [P, T // (2 * half), half]
                        fr = fv[:, :, 0, half - 1:half].to_broadcast(shape)
                        br = bv[:, :, 1, 0:1].to_broadcast(shape)
                        VE(lambda e: e.tensor_tensor(E[:, 0, :, 0, :], fr, fv[:, :, 0, :], SUB), mf, mb, *eb.busy)
                        VE(lambda e: e.tensor_tensor(E[:, 0, :, 1, :], br, bv[:, :, 1, :], SUB))
                        VE(lambda e: e.tensor_tensor(E[:, 1, :, 0, :], bv[:, :, 0, :], br, SUB))
                        m = VE(lambda e: e.tensor_tensor(E[:, 1, :, 1, :], fv[:, :, 1, :], fr, SUB))
                        m = AC(lambda e: e.activation(eb.ap[:, :, :], eb.ap[:, :, :], ACT.Exp), m)
                        kfv = kf.rearrange("p (n s h) -> p n s h", s=2, h=half)
                        kbv = kb.rearrange("p (n s h) -> p n s h", s=2, h=half)
                        VE(lambda e: e.tensor_tensor(E[:, 0, :, 0, :], E[:, 0, :, 0, :], kfv[:, :, 0, :], MUL), m)
                        m1 = VE(lambda e: e.tensor_tensor(E[:, 0, :, 1, :], E[:, 0, :, 1, :], kbv[:, :, 1, :], MUL))
                        m2 = PO(lambda e: e.tensor_tensor(eb.ap[:, 1, :], eb.ap[:, 1, :], q, MUL), m, q_ready)
                        bank = banks.take()
                        PE.wait(*bank.busy, m1, m2)
                        for c_ in range(NT):
                            sl = slice(c_ * P, c_ * P + P)
                            m_pe = PE(lambda e: e.matmul(bank.ap[:, sl], eb.ap[:, 0, sl], eb.ap[:, 1, sl],
                                                         start=True, stop=True))
                        eb.busy = (m_pe,)
                        m_a = VE(lambda e: e.copy_predicated(
                            A[:, :].rearrange("p (c t) -> p c t", c=NT),
                            levels[:, lv:lv + 1, :].to_broadcast([P, NT, P]),
                            bank.ap.rearrange("p (c t) -> p c t", c=NT)), m_pe, m_a)
                        banks.give(bank, m_a)
                        yield

                    parts = []
                    for d, (k_, cum, end, tot) in enumerate(((kf, f4, f_end, 0), (kb, b4, b_end, 1))):
                        eb = ex[d]
                        e4 = eb.ap[:, 0, :].rearrange("p (c t) -> p c t", c=NT)
                        m = VE(lambda e: e.tensor_tensor(e4, end.to_broadcast([P, NT, P]), cum, SUB), *eb.busy)
                        m = AC(lambda e: e.activation(eb.ap[:, 0, :], eb.ap[:, 0, :], ACT.Exp), m)
                        m = PO(lambda e: e.tensor_tensor(eb.ap[:, 0, :], eb.ap[:, 0, :], k_, MUL), m)
                        mq = AC(lambda e: e.activation(eb.ap[:, 1, :], (cf_ if d == 0 else cb_)[:, :], ACT.Exp),
                                mf, mb, *eb.busy)
                        mq = PO(lambda e: e.tensor_tensor(eb.ap[:, 1, :], eb.ap[:, 1, :], q, MUL), mq)
                        which = (0, 1, 2) if d == 0 else (3, 2, 1)
                        bank = banks.take()
                        PE.wait(*bank.busy, m)
                        for i, c_ in enumerate(which):
                            m_pe = PE(lambda e: e.transpose(bank.ap[:, i * P:i * P + P],
                                                            eb.ap[:, 0, c_ * P:c_ * P + P], ident))
                        m_t = AC(lambda e: e.activation(k1t[:, 0:3 * P], bank.ap[:, 0:3 * P], ACT.Copy), m_pe,
                                 *k1t_busy[0])
                        banks.give(bank, m_t)
                        bank = banks.take()
                        PE.wait(*bank.busy, m_t, *kept["v", h // 2])
                        for i, c_ in enumerate(which):
                            m_pe = PE(lambda e: e.matmul(bank.ap[:, i * P:i * P + P], k1t[:, i * P:i * P + P],
                                                         vv[:, c_, :], start=True, stop=True))
                        k1t_busy[0] = (m_pe,)
                        m_s = VE(lambda e: e.tensor_copy(states[:, d, 0, :], bank.ap[:, 0:P]), m_pe, *states_busy[0])
                        for i in (1, 2):
                            m_s = VE(lambda e: e.scalar_tensor_tensor(
                                out=states[:, d, i, :], in0=states[:, d, i - 1, :],
                                scalar=e_tot[:, tot, which[i]:which[i] + 1], in1=bank.ap[:, i * P:i * P + P],
                                op0=MUL, op1=ADD), m_s, m_et)
                        banks.give(bank, m_s)
                        parts.append((mq, m_s))
                        yield
                    o_bank = banks.take()
                    PE.wait(*o_bank.busy, m_a, *parts[0], *parts[1])
                    for c_ in range(NT):
                        sl = slice(c_ * P, c_ * P + P)
                        pairs = [(vv[:, c_, :], A[:, sl])]
                        if c_ > 0:
                            pairs.append((states[:, 0, c_ - 1, :], ex[0].ap[:, 1, sl]))
                        if c_ < NT - 1:
                            pairs.append((states[:, 1, NT - 2 - c_, :], ex[1].ap[:, 1, sl]))
                        m_o = fmm(o_bank.ap[:, sl], pairs)
                    a_busy[0] = states_busy[0] = (m_o,)
                    ex[0].busy = ex[1].busy = (m_o,)
                    if h % 2 == 1:
                        v[h // 2 % 2].busy = (m_o,)
                    cum_busy[0] = (VE.last(), AC.last(), PO.last())
                    yield
                    r, m_r = inverse_rms([(o_bank.ap, (m_o,))], P)
                    t = work.take()
                    m = VE(lambda e: e.scalar_tensor_tensor(out=t.ap, in0=o_bank.ap, scalar=column("a_norm", 0),
                                                            in1=r.ap, op0=MUL, op1=MUL), m_r, m_o, *t.busy)
                    banks.give(o_bank, m)
                    work.give(r, m)
                    m = VE(lambda e: e.tensor_tensor(o[:, h, :], t.ap, gs, MUL), m, kept["gs", h])
                    work.give(t, m)
                    o_ready[h] = m
                    head_busy[h % 2] = (VE.last(), AC.last(), PO.last(), m_o)
                    yield

                run(project(0))
                for h in range(1, HG_HEADS):
                    together(project(h), attend(h - 1))
                run(attend(HG_HEADS - 1))
                begin_u()
                for h in range(HG_HEADS):
                    split_to(U, h, o[:, h, :], (o_ready[h],))
                for c0 in range(0, D, 256):
                    w = use(("gla_out", c0))
                    for j in range(2):
                        bank, m = feature_tile(w, j * P, U)
                        add_to_x(c0 // P + j, bank, m)
                    used(w, m)
                barrier()

        def mod_slot():
            c0 = mod_slot.next
            mod_slot.next += 256
            w = use(("mod", c0))
            bank = banks.take()
            PE.wait(*bank.busy, *w.ready, mod_slot.ready)
            for j in range(2):
                for k in range(DT):
                    last = nc.tensor.matmul(bank.ap[:, 2 * j:2 * j + 2], w.raw[:, k, j * P:(j + 1) * P],
                                            mod_slot.c[:, k, :], start=k == 0, stop=k == DT - 1)
            last.then_inc(PE.done, 1)
            PE.count += 1
            m = PE.last()
            used(w, m)
            i = c0 // P
            bias = column("b_mod", i, 2).rearrange("p (j o) -> p j o", o=1).to_broadcast([P, 2, 2])
            m = VE(lambda e: e.tensor_tensor(modv[:, i:i + 2, :], bank.ap[:, 0:4].rearrange(
                "p (j o) -> p j o", j=2), bias, ADD), m, loaded)
            banks.give(bank, m)
            mod_slot.done = m
        mod_slot.next = 0

        silu_c = sb("silu_c", [P, DT, 2])
        m = AC(lambda e: e.activation(silu_c[:, :, :], column("c_c", 0, 16).rearrange(
            "p (k o) -> p k o", k=DT), ACT.Silu), loaded)
        mod_slot.ready, mod_slot.c = m, silu_c

        def mlp(tag, n_tiles, per_slot, hidden, extra=0, scale=None):
            with ExitStack() as c:
                bufs = [Split(sb(f"{tag}_h_hi{i}", [P, 4, T], F32R, c), sb(f"{tag}_h_lo{i}", [P, 4, T], F32R, c), 4)
                        for i in range(2)]
                parts = chunks_of(n_tiles, 4)
                for i in range(len(parts) + 1):
                    if i < len(parts):
                        H = bufs[i % 2]
                        H.ready = [()] * 4
                        t0, n = parts[i]
                        for t in range(t0, t0 + n, per_slot):
                            w = use((tag, t))
                            for j in range(per_slot):
                                m = hidden(w, j, t + j, H, t + j - t0)
                            used(w, m)
                            if extra:
                                extra -= 1
                                mod_slot()
                    if i > 0:
                        H = bufs[(i - 1) % 2]
                        t0, n = parts[i - 1]
                        width = SLOT // n
                        for c0 in range(0, D, width):
                            w = use((tag + "_out", t0, c0))
                            for j in range(width // P):
                                bank, m = feature_tile(w, j * P, H)
                                add_to_x(c0 // P + j, bank, m, scale)
                            used(w, m)
                        H.busy = (m,)
                while extra:
                    extra -= 1
                    mod_slot()
                barrier()

        def conv_glu(layer):
            tag = f"ffn{layer}"

            def hidden(w, j, t, H, slot):
                gate, mg = feature_tile(w, 0, U)
                val, mv = feature_tile(w, P, U)
                tap = [column("ffn_cw", (layer * 3 + i) * FF_TILES + t) for i in range(3)]
                a = work.take()
                m = VE(lambda e: e.tensor_scalar(a.ap, gate.ap, tap[1], column("ffn_cb", layer * FF_TILES + t),
                                                 MUL, ADD), mg, *a.busy)
                m = VE(lambda e: e.scalar_tensor_tensor(out=a.ap[:, 1:T], in0=gate.ap[:, 0:T - 1], scalar=tap[0],
                                                        in1=a.ap[:, 1:T], op0=MUL, op1=ADD), m)
                m = VE(lambda e: e.scalar_tensor_tensor(out=a.ap[:, 0:T - 1], in0=gate.ap[:, 1:T], scalar=tap[2],
                                                        in1=a.ap[:, 0:T - 1], op0=MUL, op1=ADD), m)
                banks.give(gate, m)
                m = AC(lambda e: e.activation(a.ap, a.ap, ACT.Silu), m)
                m = VE(lambda e: e.tensor_tensor(a.ap, a.ap, val.ap, MUL), m, mv)
                banks.give(val, m)
                work.give(a, *split_to(H, slot, a.ap, (m,), on=VE))
                return mv

            begin_u()
            norm_to(U, x_tiles(), lambda k: column("norm2", layer * DT + k), D)
            mlp(tag, FF_TILES, 1, hidden, extra=24 if layer == 0 else 0)

        def scope(**k):
            return k

        shared = scope(nc=nc, sb=sb, PE=PE, VE=VE, AC=AC, PO=PO, SP=SP, banks=banks, work=work, x=x, U=U,
                       column=column, use=use, used=used, feature_tile=feature_tile, token_tile=token_tile,
                       fmm=fmm, inverse_rms=inverse_rms, norm_to=norm_to, x_tiles=x_tiles, add_to_x=add_to_x,
                       barrier=barrier, begin_u=begin_u, Split=Split, split_to=split_to, ident=ident, ones=ones,
                       m_le=m_le, m_ge=m_ge, m_lt=m_lt, m_gt=m_gt, rotate=rotate, turn=turn, levels=levels, modv=modv,
                       mod_slot=mod_slot, mlp=mlp, ins=ins, s_io=s_io, loaded=loaded, x_ready=x_ready, sem=sem,
                       product=product)
        stop = "all" if debug is None else debug.get("stop", "all")
        def phases():
            hgrn2()
            yield "gla"
            conv_glu(0)
            yield "ffn0"
            mamba2(shared)
            yield "mamba"
            conv_glu(1)
            final_to_x(shared, "final")
            yield "b1"
            block2(shared)
            yield "b2"
            block3(shared)
            yield "all"
        if debug is not None and debug.get("mods"):
            for _ in range(24):
                mod_slot()
        if debug is not None and "only" in debug:
            {"b2": lambda: block2(shared), "b3": lambda: block3(shared), "mamba": lambda: mamba2(shared)}[debug["only"]]()
        else:
            for name in phases():
                if name == stop:
                    break
        SP.wait(*[m for k in range(DT) for m in x_ready[k]])
        s_out = sem("result_stored")
        nc.sync.dma_start(out.rearrange("(k p) t -> p k t", p=P), x[:, :, :]).then_inc(s_out, 16)
        nc.sync.wait_ge(s_out, 16)


def final_to_x(sh, gain):
    VE, work, x, x_ready = sh["VE"], sh["work"], sh["x"], sh["x_ready"]
    r, m_r = sh["inverse_rms"](sh["x_tiles"](), D)
    for k in range(DT):
        m = VE(lambda e: e.scalar_tensor_tensor(out=x[:, k, :], in0=x[:, k, :], scalar=sh["column"](gain, k),
                                                in1=r.ap, op0=MUL, op1=MUL), m_r, *x_ready[k])
        x_ready[k] = (m,)
    work.give(r, m)



ATANH = [1.0 / (2 * k + 1) for k in range(9)]


def mamba2(sh):
    nc, PE, VE, AC, PO = sh["nc"], sh["PE"], sh["VE"], sh["AC"], sh["PO"]
    banks, work, column, use, used = sh["banks"], sh["work"], sh["column"], sh["use"], sh["used"]
    feature_tile, fmm, ident, levels, U = sh["feature_tile"], sh["fmm"], sh["ident"], sh["levels"], sh["U"]
    with ExitStack() as c:
        def s(name, shape, dt=F32):
            return sh["sb"]("m_" + name, shape, dt, c)

        acum = s("acum", [N_DT, T])
        neg_a = s("neg_a", [N_DT, 1])
        tok = s("tok", [P, 3, NT, N_DT])
        dt_tok, ac_tok, dec_tok = (tok[:, i, :, :] for i in range(3))
        e_last = s("e_last", [P, NT, N_DT])
        side = [{"x": s(f"xs{i}", [P, 2, T]), "B": s(f"B{i}", [P, T]), "C": s(f"C{i}", [P, T])} for i in range(2)]
        side_busy = [(), ()]
        z = s("z", [P, 2, T])
        z_busy = [()]
        x_tok, b_tok = s("x_tok", [P, NT, 256]), s("b_tok", [P, NT, P])
        xd = [s("xd_f", [P, NT, 256]), s("xd_b", [P, NT, 256])]
        xe = s("xe", [P, NT, 256])
        cbs = [s("cb_f", [P, T]), s("cb_b", [P, T])]
        H = s("H", [P, 2, 3, 256])
        pair = [(Buf(s(f"E{i}", [P, T])[:, :]), Buf(s(f"W{i}", [P, T])[:, :])) for i in range(2)]
        ce = [Buf(s("C_f", [P, T])[:, :]), Buf(s("C_b", [P, T])[:, :])]
        Y = sh["Split"](s("y_hi", [P, 2, T], F32R), s("y_lo", [P, 2, T], F32R), 2)
        group_busy = [()]

        sh["begin_u"]()
        sh["norm_to"](U, sh["x_tiles"](), lambda k: column("norm1", DT + k), D)

        w = use(("m_dt",))
        bank, m = feature_tile(w, 0, U, width=N_DT)
        used(w, m)
        zb, nb, rb = work.take(), work.take(), work.take()
        zz, e, r = zb.ap[0:N_DT, :], nb.ap[0:N_DT, :], rb.ap[0:N_DT, :]
        m = VE(lambda v: v.tensor_scalar(zz, bank.ap[0:N_DT, :], column("dt_bias", 0)[0:N_DT, :], None, ADD), m,
               *zb.busy)
        banks.give(bank, m)
        m = VE(lambda v: v.tensor_scalar(e, zz, -1.0, None, MUL), m, *nb.busy)
        m = VE(lambda v: v.tensor_tensor(e, e, zz, MIN), m)
        m = AC(lambda v: v.activation(e, e, ACT.Exp), m)
        m = VE(lambda v: v.tensor_scalar(r, e, 2.0, None, ADD), m, *rb.busy)
        m = VE(lambda v: v.reciprocal(r, r), m)
        m = VE(lambda v: v.tensor_tensor(r, r, e, MUL), m)
        m = VE(lambda v: v.tensor_tensor(e, r, r, MUL), m)
        qb = work.take()
        q = qb.ap[0:N_DT, :]
        m = VE(lambda v: v.tensor_scalar(q, e, ATANH[-1], None, MUL), m, *qb.busy)
        for coef in ATANH[-2:0:-1]:
            m = VE(lambda v: v.scalar_tensor_tensor(out=q, in0=q, scalar=coef, in1=e, op0=ADD, op1=MUL), m)
        m = VE(lambda v: v.scalar_tensor_tensor(out=q, in0=q, scalar=1.0, in1=r, op0=ADD, op1=MUL), m)
        m = VE(lambda v: v.tensor_scalar(q, q, 2.0, None, MUL), m)
        m_dt = VE(lambda v: v.scalar_tensor_tensor(out=zz, in0=zz, scalar=0.0, in1=q, op0=MAX, op1=ADD), m)
        m = AC(lambda v: v.activation(neg_a[:, :], column("a_log", 0)[0:N_DT, :], ACT.Exp))
        m = VE(lambda v: v.tensor_scalar(neg_a[:, :], neg_a[:, :], -1.0, None, MUL), m)
        m_la = VE(lambda v: v.tensor_scalar(e, zz, neg_a[:, 0:1], None, MUL), m, m_dt)
        m = VE(lambda v: v.memset(r, 1.0), m_dt)
        for i in range(NT):
            m = VE(lambda v: v.memset(r[:, i * P:i * P + 1], 0.0), m)
        VE(lambda v: v.tensor_tensor_scan(acum[0:32, :], r[0:32, :], e[0:32, :], 0.0, MUL, ADD), m, m_la)
        m_ac = VE(lambda v: v.tensor_tensor_scan(acum[32:64, ::-1], r[32:64, :], e[32:64, ::-1], 0.0, MUL, ADD), m)
        a4 = acum[:, :].rearrange("p (c t) -> p c t", c=NT)
        d4 = q.rearrange("p (c t) -> p c t", c=NT)
        ends = ((slice(0, 32), a4[0:32, :, P - 1:P]), (slice(32, 64), a4[32:64, :, 0:1]))
        for rows, end in ends:
            m = VE(lambda v: v.tensor_tensor(d4[rows], end.to_broadcast([32, NT, P]), a4[rows], SUB), m_ac)
        m = AC(lambda v: v.activation(q, q, ACT.Exp), m)
        m = VE(lambda v: v.tensor_tensor(q, q, zz, MUL), m)
        bank, bank2 = banks.take(), banks.take()
        PE.wait(*bank.busy, *bank2.busy, m, m_dt, m_ac)
        for i, (src, to) in enumerate(((zz, bank.ap[:, 0:256]), (acum[:, :], bank.ap[:, 256:512]), (q, bank2.ap))):
            for k in range(NT):
                m = PE(lambda v: v.transpose(to[:, k * N_DT:(k + 1) * N_DT], src[:, k * P:(k + 1) * P],
                                             ident[0:N_DT, 0:N_DT]))
        last = s("last", [N_DT, NT])
        for rows, end in ends:
            m_l = VE(lambda v: v.tensor_copy(last[rows, :], end.rearrange("p c t -> p (c t)")), m_ac)
        PE.wait(m_l)
        for k in range(NT):
            m = PE(lambda v: v.matmul(bank2.ap[:, 256 + k * N_DT:256 + (k + 1) * N_DT],
                                      last[:, k:k + 1].to_broadcast([N_DT, P]), ident[0:N_DT, 0:N_DT],
                                      start=True, stop=True))
        m1 = VE(lambda v: v.tensor_copy(tok[:, 0:2, :, :].rearrange("p a c j -> p (a c j)"), bank.ap), m)
        banks.give(bank, m1)
        m2 = VE(lambda v: v.tensor_copy(tok[:, 2, :, :].rearrange("p c j -> p (c j)"), bank2.ap[:, 0:256]), m)
        m3 = AC(lambda v: v.activation(e_last[:, :, :].rearrange("p c j -> p (c j)"), bank2.ap[:, 256:512], ACT.Exp), m2)
        banks.give(bank2, m2, m3)
        for b in (zb, nb, rb, qb):
            work.give(b, m, m2, m3)
        setup = (m1, m2, m3)
        kept = {}

        def conv(bank, m, tile, dst, busy):
            tap = [column("conv_w", i * 32 + tile) for i in range(5)]
            m = VE(lambda v: v.tensor_scalar(dst, bank.ap, tap[2], column("conv_b", tile), MUL, ADD), m, *busy)
            for i in (0, 1, 3, 4):
                o = i - 2
                a, b = max(0, -o), T - max(0, o)
                m = VE(lambda v: v.scalar_tensor_tensor(out=dst[:, a:b], in0=bank.ap[:, a + o:b + o], scalar=tap[i],
                                                        in1=dst[:, a:b], op0=MUL, op1=ADD), m)
            banks.give(bank, m)
            return AC(lambda v: v.activation(dst, dst, ACT.Silu), m)

        def project(g):
            sd, busy = side[g % 2], side_busy[g % 2]
            w = use(("m_x", g))
            marks = []
            for j in range(2):
                bank, m = feature_tile(w, j * P, U)
                marks.append(conv(bank, m, 2 * g + j, sd["x"][:, j, :], busy))
            used(w, m)
            yield
            w = use(("m_bc", g))
            for j, name in enumerate("BC"):
                bank, m = feature_tile(w, j * P, U)
                marks.append(conv(bank, m, 16 + 8 * j + g, sd[name][:, :], busy))
            used(w, m)
            kept["x", g], kept["B", g], kept["C", g] = tuple(marks[0:2]), marks[2], marks[3]
            yield

        def project_z(g):
            w = use(("m_z", g))
            marks = []
            for j in range(2):
                bank, m = feature_tile(w, j * P, U)
                marks.append(AC(lambda v: v.activation(z[:, j, :], bank.ap, ACT.Silu), m, *z_busy[0]))
                banks.give(bank, marks[-1])
            used(w, m)
            kept["z", g] = marks
            yield

        def ssd(g):
            sd = side[g % 2]
            xs, B, C = sd["x"], sd["B"], sd["C"]
            row = (4 * g, 32 + 4 * g)
            for j in range(3):
                bank = banks.take()
                src = xs[:, j, :] if j < 2 else B[:, :]
                PE.wait(*bank.busy, kept["x", g][j] if j < 2 else kept["B", g])
                for k in range(NT):
                    m = PE(lambda v: v.transpose(bank.ap[:, k * P:(k + 1) * P], src[:, k * P:(k + 1) * P], ident))
                dst = x_tok[:, :, j * P:(j + 1) * P] if j < 2 else b_tok[:, :, :]
                m = (AC if j else VE)(lambda v: (v.activation(dst, bank.ap.rearrange("p (c t) -> p c t", c=NT), ACT.Copy)
                                                 if j else
                                                 v.tensor_copy(dst, bank.ap.rearrange("p (c t) -> p c t", c=NT))),
                                      m, *group_busy[0])
                banks.give(bank, m)
                if j == 0:
                    m_x0 = m
                elif j == 1:
                    m_x1 = m
                else:
                    m_bt = m
            bank = banks.take()
            PE.wait(*bank.busy, kept["B", g], kept["C", g])
            for k in range(NT):
                sl = slice(k * P, (k + 1) * P)
                m = PE(lambda v: v.matmul(bank.ap[:, sl], B[:, sl], C[:, sl], start=True, stop=True))
            m_cb = []
            for d, mask in enumerate((sh["m_le"], sh["m_ge"])):
                m_cb.append(VE(lambda v: v.tensor_tensor(
                    cbs[d][:, :].rearrange("p (c t) -> p c t", c=NT), bank.ap.rearrange("p (c t) -> p c t", c=NT),
                    mask.rearrange("p (o t) -> p o t", o=1).to_broadcast([P, NT, P]), MUL), m, *group_busy[0]))
            banks.give(bank, m_cb[1])
            yield

            def by_head(t, d):
                return t[:, :, row[d]:row[d] + 4].rearrange("p c (h o) -> p c h o", o=1).to_broadcast(
                    [P, NT, 4, HEAD_P])

            def heads(t):
                return t.rearrange("p c (h q) -> p c h q", h=4)

            m_xd = [(VE, PO)[d](lambda v: v.tensor_tensor(heads(xd[d][:, :, :]), heads(x_tok[:, :, :]),
                                                          by_head(dt_tok, d), MUL), m_x0, m_x1, *setup,
                                *group_busy[0]) for d in range(2)]
            m_xe, m_H = (m_x0, *group_busy[0]), []
            for d in range(2):
                which = (0, 1, 2) if d == 0 else (3, 2, 1)
                m = PO(lambda v: v.tensor_tensor(heads(xe[:, :, :]), heads(x_tok[:, :, :]), by_head(dec_tok, d),
                                                 MUL), m_x1, *m_xe, *setup)
                b1, b2 = banks.take(), banks.take()
                PE.wait(*b1.busy, *b2.busy, m, m_bt)
                places = [b1.ap[:, 0:256], b1.ap[:, 256:512], b2.ap[:, 0:256]]
                for i, k in enumerate(which):
                    m = PE(lambda v: v.matmul(places[i], b_tok[:, k, :], xe[:, k, :], start=True, stop=True))
                m_xe = (m,)
                m = VE(lambda v: v.tensor_copy(H[:, d, 0, :], places[0]), m, *group_busy[0])
                for i in (1, 2):
                    k = which[i]
                    factor = e_last[:, k, row[d]:row[d] + 4].rearrange("p (h o) -> p h o", o=1).to_broadcast(
                        [P, 4, HEAD_P])
                    m = VE(lambda v: v.tensor_tensor(H[:, d, i, :].rearrange("p (h q) -> p h q", h=4),
                                                     H[:, d, i - 1, :].rearrange("p (h q) -> p h q", h=4), factor,
                                                     MUL), m)
                    m = VE(lambda v: v.tensor_tensor(H[:, d, i, :], H[:, d, i, :], places[i], ADD), m)
                banks.give(b1, m)
                banks.give(b2, m)
                m_H.append(m)
            yield

            y_banks = []
            for j in range(HEADS_PER_GROUP):
                E, W = pair[j % 2]
                if j % 2 == 0:
                    y_banks.append(banks.take())
                    PE.wait(*y_banks[-1].busy)
                bc = [banks.take(), banks.take()]
                for d in range(2):
                    PE.wait(*bc[d].busy)
                    r = row[d] + j
                    m_bc = PE(lambda v: v.matmul(bc[d].ap, ident[0:N_DT, r:r + 1].to_broadcast([N_DT, P]), acum[:, :],
                                                 start=True, stop=True), m_ac)
                m_ce = []
                for d in range(2):
                    m = AC(lambda v: v.activation(ce[d].ap, bc[d].ap, ACT.Exp), m_bc, *ce[d].busy)
                    m_e0 = m if d == 0 else m_e0
                    m_e = m
                    m_ce.append(PO(lambda v: v.tensor_tensor(ce[d].ap, ce[d].ap, C[:, :], MUL), m, kept["C", g]))

                def column_of(d):
                    return ac_tok[:, :, row[d] + j:row[d] + j + 1].to_broadcast([P, NT, P])

                def chunked(t):
                    return t.rearrange("p (c t) -> p c t", c=NT)

                m = VE(lambda v: v.tensor_tensor(chunked(E.ap), chunked(bc[0].ap), column_of(0), SUB), m_e0, *setup,
                       *E.busy)
                m2 = VE(lambda v: v.tensor_tensor(chunked(bc[1].ap), chunked(bc[1].ap), column_of(1), SUB), m_e)
                banks.give(bc[0], m, m_e)
                m = VE(lambda v: v.copy_predicated(chunked(E.ap), levels[:, len(SUB_LEVELS):, :].to_broadcast(
                    [P, NT, P]), chunked(bc[1].ap)), m, m2)
                banks.give(bc[1], m)
                m = AC(lambda v: v.activation(E.ap, E.ap, ACT.Exp), m)
                m_w = VE(lambda v: v.tensor_tensor(W.ap, E.ap, cbs[0][:, :], MUL), m, m_cb[0], *W.busy)
                m_w2 = VE(lambda v: v.tensor_tensor(E.ap, E.ap, cbs[1][:, :], MUL), m_w, m_cb[1])
                rows = slice((j % 2) * HEAD_P, (j % 2) * HEAD_P + HEAD_P)
                hc = slice(j * HEAD_P, (j + 1) * HEAD_P)
                PE.wait(m_w2, *m_xd, *m_ce, *m_H)
                for k in range(NT):
                    sl = slice(k * P, (k + 1) * P)
                    pairs = [(xd[0][:, k, hc], W.ap[:, sl]), (xd[1][:, k, hc], E.ap[:, sl])]
                    if k > 0:
                        pairs.append((H[:, 0, k - 1, hc], ce[0].ap[:, sl]))
                    if k < NT - 1:
                        pairs.append((H[:, 1, NT - 2 - k, hc], ce[1].ap[:, sl]))
                    m_y = fmm(y_banks[-1].ap[rows, sl], pairs)
                E.busy = W.busy = ce[0].busy = ce[1].busy = (m_y,)
                yield
            y_tiles = []
            for i in range(2):
                m = VE(lambda v: v.scalar_tensor_tensor(out=xs[:, i, :], in0=xs[:, i, :],
                                                        scalar=column("d_skip", 2 * g + i), in1=y_banks[i].ap,
                                                        op0=MUL, op1=ADD), m_y)
                banks.give(y_banks[i], m)
                m = VE(lambda v: v.tensor_tensor(xs[:, i, :], xs[:, i, :], z[:, i, :], MUL), m, kept["z", g][i])
                y_tiles.append((xs[:, i, :], (m,)))
            z_busy[0] = (m,)
            Y.ready = [(), ()]
            sh["norm_to"](Y, y_tiles, lambda k: column("b_norm", 2 * g + k), 256)
            marks = (VE.last(), AC.last(), PO.last(), PE.last())
            group_busy[0] = side_busy[g % 2] = marks
            yield

        def chain(*gens):
            for g in gens:
                yield from g

        run(project(0))
        for g in range(GROUPS):
            if g + 1 < GROUPS:
                together(chain(project_z(g), project(g + 1)), ssd(g))
            else:
                together(project_z(g), ssd(g))
            w = use(("m_out", g))
            for i in range(DT):
                bank, m = feature_tile(w, i * P, Y)
                sh["add_to_x"](i, bank, m)
            used(w, m)
            Y.busy = (m,)
        sh["barrier"]()



def block2(sh):
    nc, PE, VE, AC, PO, SP = (sh[n] for n in ("nc", "PE", "VE", "AC", "PO", "SP"))
    banks, work, column, use, used = sh["banks"], sh["work"], sh["column"], sh["use"], sh["used"]
    feature_tile, token_tile, fmm, ident, U = (sh[n] for n in ("feature_tile", "token_tile", "fmm", "ident", "U"))
    ins, x, x_ready, ones, Split, split_to = (sh[n] for n in ("ins", "x", "x_ready", "ones", "Split", "split_to"))
    SCALE = float(HEAD_P) ** -0.5
    with ExitStack() as outer:
        o = sh["sb"]("b2_o", [P, 8, T], F32, outer)
        o_ready = [None] * 8
        with ExitStack() as c:
            def s(name, shape, dt=F32):
                return sh["sb"]("b2_" + name, shape, dt, c)

            qk = [s(f"qk{i}", [P, 2, T]) for i in range(2)]
            qk_busy = [(), ()]
            v_s = [Buf(s(f"v{i}", [P, NT, 256])) for i in range(2)]
            q_w, k_w, v_w = s("q_w", [P, 4, T]), s("k_w", [P, 2, T]), s("v_w", [P, NT, P])
            bias = s("bias", [P, 8, 256])
            sink = s("sink", [P, 8])
            rel, onehot, outside = s("rel", [N_BUCKETS, 8]), s("onehot", [N_BUCKETS, 384]), s("outside", [8, 384])
            N_TRI = sum(T - P * i for i in range(NT))
            at = [sum(T - P * k for k in range(i)) for i in range(NT)]
            tri = [Buf((s(f"nl{i}", [P, N_TRI]), s(f"lb{i}", [P, N_TRI]))) for i in range(2)]

            s_in, s_w = sh["sem"]("b2_small_loaded"), sh["s_io"]
            nc.sync.dma_start(rel[:, :], ins["rel_bias"]).then_inc(s_in, 16)
            nc.sync.dma_start(onehot[:, :], ins["const_onehot"]).then_inc(s_in, 16)
            nc.sync.dma_start(outside[:, :], ins["const_outside"]).then_inc(s_in, 16)
            nc.sync.dma_start(sink[:, :], ins["sinks"].to_broadcast([P, 8])).then_inc(s_in, 16)
            small = (s_in, 64)
            bank = banks.take()
            PE.wait(*bank.busy, small)
            m = fmm(bank.ap[0:8, 0:384], [(rel[:, :], onehot[:, :])])
            m = VE(lambda v: v.tensor_tensor(outside[:, :], bank.ap[0:8, 0:384], outside[:, :], ADD), m, small)
            banks.give(bank, m)
            rows = nc.dram_tensor("bias_rows", (8, 384), F32, kind="Internal").ap()
            SP.wait(m)
            nc.sync.dma_start(rows, outside[:, :]).then_inc(s_w, 16)
            SP.wait((s_w, 16))
            shifted = bass.AP(tensor=rows.tensor, offset=0, ap=[[1, P], [384, 8], [1, 256]])
            nc.sync.dma_start(bias[:, :, :], shifted).then_inc(s_w, 16)
            for i in range(4):
                part = bias[:, 2 * i:2 * i + 2, :].rearrange("p h s -> p (h s)")
                bank = banks.take()
                m = fmm(bank.ap, [(sh["turn"], part)], (s_w, 32), *bank.busy)
                m_bias = VE(lambda v: v.tensor_copy(part, bank.ap), m)
                banks.give(bank, m_bias)

            sh["begin_u"]()
            sh["norm_to"](U, sh["x_tiles"](), lambda k: column("g_mix_2", k), D)
            kept = {}

            def to_sbuf(dst, bank, width, m, busy=(), n=T):
                mark = AC(lambda v: v.activation(dst, bank.ap[:, 0:n] if width is None else bank.ap[:, 0:width],
                                                 ACT.Copy), m, *busy)
                banks.give(bank, mark)
                return mark

            def project_window():
                w = use(("b2_w_k",))
                for j in range(2):
                    bank, m = feature_tile(w, j * P, U)
                    kept["wk"] = to_sbuf(k_w[:, j, :], bank, None, m)
                used(w, m)
                w = use(("b2_w_v",))
                for k in range(NT):
                    bank, m = token_tile(w, 0, P, U, k * P)
                    kept["wv"] = to_sbuf(v_w[:, k, :], bank, P, m)
                used(w, m)
                for c0 in (0, 256):
                    w = use(("b2_w_q", c0))
                    for j in range(2):
                        bank, m = feature_tile(w, j * P, U)
                        kept["wq", c0 // P + j] = to_sbuf(q_w[:, c0 // P + j, :], bank, None, m)
                    used(w, m)
                yield

            def project(p):
                if p % 2 == 0:
                    vb = v_s[p // 2]
                    w = use(("b2_s_v", p))
                    for k in range(NT):
                        bank, m = token_tile(w, 0, 256, U, k * P)
                        kept["v", p // 2] = to_sbuf(vb.ap[:, k, :], bank, 256, m)
                    used(w, m)
                    yield
                w = use(("b2_s_qk", p))
                for j in range(2):
                    bank, m = feature_tile(w, j * P, U)
                    kept["qk", p] = to_sbuf(qk[p % 2][:, j, :], bank, None, m, qk_busy[p % 2])
                used(w, m)
                yield

            def stick(p):
                o_bank = banks.take()
                PE.wait(*o_bank.busy)
                for hh in range(2):
                    buf = tri[hh]
                    nl, lb = buf.ap
                    r = slice(hh * HEAD_P, (hh + 1) * HEAD_P)
                    q, k = qk[p % 2][r, 0, :], qk[p % 2][r, 1, :]
                    m_nl, m_lb = [], []
                    for i in range(NT):
                        n, t0 = T - i * P, i * P
                        part = slice(at[i], at[i] + n)
                        bank = banks.take()
                        PE.wait(*bank.busy)
                        m = fmm(bank.ap[:, 0:n], [(k[:, t0:t0 + P], q[:, t0:T])], kept["qk", p])
                        m1 = AC(lambda v: v.activation(lb[:, part], bank.ap[:, 0:n], ACT.Abs, scale=SCALE), m,
                                *buf.busy)
                        m2 = AC(lambda v: v.activation(lb[:, part], lb[:, part], ACT.Exp, scale=-1.0), m1)
                        m2 = AC(lambda v: v.activation(lb[:, part], lb[:, part], ACT.Ln, bias=1.0), m2)
                        m3 = VE(lambda v: v.tensor_scalar(nl[:, part], bank.ap[:, 0:n], SCALE, 0.0, MUL, MAX), m1,
                                *buf.busy)
                        m3 = VE(lambda v: v.tensor_tensor(nl[:, part], nl[:, part], lb[:, part], ADD), m2, m3)
                        m4 = VE(lambda v: v.scalar_tensor_tensor(out=lb[:, part], in0=bank.ap[:, 0:n], scalar=SCALE,
                                                                 in1=nl[:, part], op0=MUL, op1=SUB), m3)
                        banks.give(bank, m4)
                        diag = slice(at[i], at[i] + P)
                        m_nl.append(PO(lambda v: v.tensor_tensor(nl[:, diag], nl[:, diag], sh["m_lt"], MUL), m4))
                        m_lb.append(m4)
                        if i % 2:
                            yield
                    m_a = []
                    for i in range(NT):
                        n = T - i * P
                        part = slice(at[i], at[i] + n)
                        bank = banks.take()
                        PE.wait(*bank.busy, *m_nl)
                        for j in range(i, NT):
                            m = PE(lambda v: v.matmul(bank.ap[:, (j - i) * P:n], sh["m_gt"] if j == i else ones,
                                                      nl[:, at[j]:at[j] + T - j * P], start=j == i,
                                                      stop=j == NT - 1))
                        m = VE(lambda v: v.tensor_tensor(lb[:, part], lb[:, part], bank.ap[:, 0:n], SUB), m, m_lb[i])
                        banks.give(bank, m)
                        m = AC(lambda v: v.activation(lb[:, part], lb[:, part], ACT.Exp), m)
                        diag = slice(at[i], at[i] + P)
                        m_a.append(PO(lambda v: v.tensor_tensor(lb[:, diag], lb[:, diag], sh["m_lt"], MUL), m))
                        if i == 1:
                            yield
                    c0 = (p % 2) * P + hh * HEAD_P
                    PE.wait(kept["v", p // 2])
                    for i in range(NT):
                        m_o = PE(lambda v: v.matmul(o_bank.ap[r, i * P:T], v_s[p // 2].ap[:, i, c0:c0 + HEAD_P],
                                                    lb[:, at[i]:at[i] + T - i * P], start=i == 0, stop=i == NT - 1),
                                 m_a[i])
                    buf.busy = (m_o,)
                    yield
                o_ready[p] = VE(lambda v: v.tensor_copy(o[:, p, :], o_bank.ap), m_o)
                banks.give(o_bank, o_ready[p])
                qk_busy[p % 2] = (m_o,)

            def window(h0):
                o_bank = banks.take()
                PE.wait(*o_bank.busy)
                for hh in range(2):
                    h = h0 + hh
                    buf = tri[hh]
                    S = buf.ap[0][:, 0:1024].rearrange("p (n s) -> p n s", n=NT)
                    cur, prev = buf.ap[1][:, 0:T], buf.ap[1][:, T:2 * T]
                    stats = buf.ap[0][:, 1024:1024 + 20].rearrange("p (k n) -> p k n", n=4)
                    r = slice(hh * HEAD_P, (hh + 1) * HEAD_P)
                    q, k = q_w[r, h // 2, :], k_w[r, h // 4, :]
                    kv = slice((h // 4) * HEAD_P, (h // 4 + 1) * HEAD_P)
                    b2 = [banks.take(), banks.take()]
                    PE.wait(*b2[0].busy, *b2[1].busy, kept["wk"], kept["wq", h // 2])
                    for n in range(NT):
                        lo = max(0, n - 1) * P
                        dst = b2[n // 2].ap[:, (n % 2) * 256 + (256 - ((n + 1) * P - lo)):(n % 2) * 256 + 256]
                        m = PE(lambda v: v.matmul(dst, q[:, n * P:(n + 1) * P], k[:, lo:(n + 1) * P], start=True,
                                                  stop=True))
                    m0 = VE(lambda v: v.memset(S[:, 0, 0:P], NEG), *buf.busy)
                    VE(lambda v: v.scalar_tensor_tensor(out=S[:, 0, P:256], in0=b2[0].ap[:, P:256], scalar=SCALE,
                                                        in1=bias[:, h, P:256], op0=MUL, op1=ADD), m, m_bias)
                    m1 = VE(lambda v: v.scalar_tensor_tensor(out=S[:, 1, :], in0=b2[0].ap[:, 256:512], scalar=SCALE,
                                                             in1=bias[:, h, :], op0=MUL, op1=ADD))
                    m2 = VE(lambda v: v.scalar_tensor_tensor(
                        out=S[:, 2:4, :], in0=b2[1].ap.rearrange("p (n s) -> p n s", n=2), scalar=SCALE,
                        in1=bias[:, h:h + 1, :].to_broadcast([P, 2, 256]), op0=MUL, op1=ADD))
                    banks.give(b2[0], m1)
                    banks.give(b2[1], m2)
                    m = VE(lambda v: v.tensor_reduce(stats[:, 0, :], S, AX_X, MAX), m2)
                    sk = sink[:, h:h + 1]
                    m = VE(lambda v: v.tensor_scalar(stats[:, 0, :], stats[:, 0, :], sk, None, MAX), m, small)
                    VE(lambda v: v.tensor_scalar(stats[:, 1, :], stats[:, 0, :], -1.0, sk, MUL, ADD), m)
                    m = VE(lambda v: v.tensor_tensor(S, S, stats[:, 0, :].rearrange("p (n o) -> p n o", o=1).to_broadcast(
                        [P, NT, 256]), SUB))
                    AC(lambda v: v.activation(stats[:, 1, :], stats[:, 1, :], ACT.Exp), m)
                    m = AC(lambda v: v.activation(S, S, ACT.Exp))
                    m = VE(lambda v: v.tensor_reduce(stats[:, 2, :], S, AX_X, ADD), m)
                    m = VE(lambda v: v.tensor_tensor(stats[:, 2, :], stats[:, 2, :], stats[:, 1, :], ADD), m)
                    m = VE(lambda v: v.reciprocal(stats[:, 3, :], stats[:, 2, :]), m)
                    m = VE(lambda v: v.tensor_tensor(S, S, stats[:, 3, :].rearrange("p (n o) -> p n o", o=1).to_broadcast(
                        [P, NT, 256]), MUL), m)
                    yield
                    b2 = [banks.take(), banks.take()]
                    PE.wait(*b2[0].busy, *b2[1].busy, m)
                    for n in range(NT):
                        m = PE(lambda v: v.transpose(b2[0].ap[:, n * P:(n + 1) * P], S[:, n, P:256], ident))
                        if n:
                            m = PE(lambda v: v.transpose(b2[1].ap[:, n * P:(n + 1) * P], S[:, n, 0:P], ident))
                    m1 = AC(lambda v: v.activation(cur, b2[0].ap, ACT.Copy), m)
                    m2 = AC(lambda v: v.activation(prev[:, P:T], b2[1].ap[:, P:T], ACT.Copy))
                    banks.give(b2[0], m1)
                    banks.give(b2[1], m2)
                    PE.wait(m2, kept["wv"])
                    for n in range(NT):
                        sl = slice(n * P, (n + 1) * P)
                        pairs = [(v_w[:, n, kv], cur[:, sl])]
                        if n:
                            pairs.append((v_w[:, n - 1, kv], prev[:, sl]))
                        m_o = fmm(o_bank.ap[r, sl], pairs)
                    buf.busy = (m_o,)
                    yield
                i = 4 + h0 // 2
                o_ready[i] = VE(lambda v: v.tensor_copy(o[:, i, :], o_bank.ap), m_o)
                banks.give(o_bank, o_ready[i])

            run(project_window())

            def windows():
                for h0 in range(0, 8, 2):
                    yield from window(h0)

            together(project(0), windows())
            for p in range(4):
                together(project(p + 1) if p < 3 else None, stick(p))
            sh["barrier"]()
        with ExitStack() as c:
            def s(name, shape, dt=F32):
                return sh["sb"]("b2_" + name, shape, dt, c)

            y = [s("y_a", [P, DT, T]), s("y_b", [P, DT, T])]
            V = Split(s("o_hi", [P, 4, T], F32R), s("o_lo", [P, 4, T], F32R), 4)
            merged = [None] * DT
            for b, name in enumerate("ab"):
                V.ready = [()] * 4
                for k in range(4):
                    split_to(V, k, o[:, 4 * b + k, :], (o_ready[4 * b + k],))
                up = []
                for c0 in (0, 512):
                    w = use(("b2_up_" + name, c0))
                    for j in range(4):
                        bank, m = feature_tile(w, j * P, V)
                        up.append(VE(lambda v: v.tensor_copy(y[b][:, c0 // P + j, :], bank.ap), m))
                        banks.give(bank, up[-1])
                    used(w, m)
                V.busy = (m,)
                for c0 in range(0, D, 256):
                    w = use(("b2_gate_" + name, c0))
                    for j in range(2):
                        k = c0 // P + j
                        bank, m = feature_tile(w, j * P, U)
                        t = work.take()
                        m1 = AC(lambda v: v.activation(t.ap, bank.ap, ACT.Sigmoid), m, *t.busy)
                        banks.give(bank, m1)
                        m2 = VE(lambda v: v.tensor_tensor(y[b][:, k, :], y[b][:, k, :], t.ap, MUL), m1, up[k])
                        work.give(t, m2)
                        if b:
                            m2 = VE(lambda v: v.tensor_tensor(y[1][:, k, :], y[1][:, k, :], y[0][:, k, :], ADD), m2)
                            merged[k] = m2
                    used(w, m)
            sh["begin_u"]()
            for k in range(DT):
                split_to(U, k, y[1][:, k, :], (merged[k],))
            for c0 in range(0, D, 256):
                w = use(("b2_o", c0))
                for j in range(2):
                    bank, m = feature_tile(w, j * P, U)
                    sh["add_to_x"](c0 // P + j, bank, m)
                used(w, m)
            sh["barrier"]()

    def hidden(w, j, t, H, slot):
        bank, m = feature_tile(w, j * P, U)
        a = work.take()
        m1 = AC(lambda v: v.activation(a.ap, bank.ap, ACT.Relu), m, *a.busy)
        banks.give(bank, m1)
        m1 = VE(lambda v: v.tensor_tensor(a.ap, a.ap, a.ap, MUL), m1)
        work.give(a, *split_to(H, slot, a.ap, (m1,)))
        return m

    sh["begin_u"]()
    sh["norm_to"](U, sh["x_tiles"](), lambda k: column("g_mlp_2", k), D)
    sh["mlp"]("ff2", FF2_TILES, 2, hidden)

    with ExitStack() as c:
        p_in = sh["sb"]("b2_p", [P, 2, T], F32, c)
        V = Split(sh["sb"]("b2_p_hi", [P, 2, T], F32R, c), sh["sb"]("b2_p_lo", [P, 2, T], F32R, c), 2)
        pe_out = sh["sb"]("b2_pe", [P, DT, T], F32, c)
        s_p = sh["sem"]("b2_p_loaded")
        nc.sync.dma_start(p_in[:, :, :], ins["p_t"].rearrange("(k p) t -> p k t", p=P)).then_inc(s_p, 16)
        for k in range(2):
            split_to(V, k, p_in[:, k, :], ((s_p, 16),))
        w = use(("b2_pe",))
        m_pe = []
        for k in range(DT):
            bank, m = feature_tile(w, k * P, V)
            m_pe.append(AC(lambda v: v.activation(pe_out[:, k, :], bank.ap, ACT.Copy), m))
            banks.give(bank, m_pe[-1])
        used(w, m)
        sh["begin_u"]()
        sh["norm_to"](U, sh["x_tiles"](), lambda k: column("g_pe_2", k), D)
        for c0 in range(0, D, 256):
            w = use(("b2_pg", c0))
            for j in range(2):
                k = c0 // P + j
                bank, m = feature_tile(w, j * P, U)
                t = work.take()
                m1 = AC(lambda v: v.activation(t.ap, bank.ap, ACT.Sigmoid), m, *t.busy)
                banks.give(bank, m1)
                m1 = VE(lambda v: v.tensor_tensor(t.ap, t.ap, pe_out[:, k, :], MUL), m1, m_pe[k])
                m1 = VE(lambda v: v.tensor_tensor(x[:, k, :], x[:, k, :], t.ap, ADD), m1, *x_ready[k])
                work.give(t, m1)
                x_ready[k] = (m1,)
            used(w, m)
        sh["barrier"]()
    final_to_x(sh, "g_final_2")



def block3(sh):
    nc, PE, VE, AC, PO, SP = (sh[n] for n in ("nc", "PE", "VE", "AC", "PO", "SP"))
    banks, work, column, use, used = sh["banks"], sh["work"], sh["column"], sh["use"], sh["used"]
    feature_tile, token_tile, fmm, ident, U = (sh[n] for n in ("feature_tile", "token_tile", "fmm", "ident", "U"))
    ins, x, x_ready, ones, Split, split_to = (sh[n] for n in ("ins", "x", "x_ready", "ones", "Split", "split_to"))
    modv, m_mod = sh["modv"], sh["mod_slot"].done
    SHIFT1, SCALE1, GATE1, SHIFT2, SCALE2, GATE2 = range(0, 48, DT)
    with ExitStack() as outer:
        gains = sh["sb"]("c_gains", [P, 3, DT], F32, outer)
        for i, (g, at, who) in enumerate((("g_mix_3", SCALE1, 0), ("g_mix_3", SCALE1, 1), ("g_ffn_3", SCALE2, 0))):
            m = VE(lambda v: v.tensor_scalar(gains[:, i, :], modv[:, at:at + DT, who], 1.0, None, ADD), m_mod)
            m_gain = VE(lambda v: v.tensor_tensor(gains[:, i, :], gains[:, i, :], column(g, 0, DT), MUL), m)
        saved = nc.dram_tensor("x_saved", (P, DT, T), F32, kind="Internal").ap()
        s_save = sh["sem"]("x_saved_and_back")
        conv = sh["sb"]("c_conv", [P, DT, T + 2 * HALO], F32, outer)
        m_halo = PO(lambda v: v.memset(conv[:, :, 0:HALO], 0.0))
        m_halo = PO(lambda v: v.memset(conv[:, :, HALO + T:], 0.0))
        conv_ready, conv_done = [None] * DT, [None] * DT

        sh["begin_u"]()
        readers = sh["norm_to"](U, sh["x_tiles"](), lambda k: gains[:, 0, k:k + 1], D,
                                shifts=lambda k: modv[:, SHIFT1 + k, 0:1], need=(m_gain,))
        SP.wait(*[m for k in range(DT) for m in x_ready[k]])
        nc.sync.dma_start(saved, x[:, :, :]).then_inc(s_save, 16)
        O, o_ready = x, [None] * DT
        with ExitStack() as c:
            def s(name, shape, dt=F32, c=c):
                return sh["sb"]("c_" + name, shape, dt, c)

            kv = Split(s("kv_hi", [P, 2, KEYS], F32R), s("kv_lo", [P, 2, KEYS], F32R), 2)
            qa = Split(s("qa_hi", [P, 3, T], F32R), s("qa_lo", [P, 3, T], F32R), 3)
            kr = s("kr", [QK_ROPE, KEYS])
            rope = s("rope", [QK_ROPE, 2, T])
            s_in = sh["sem"]("c_context_loaded")
            nc.sync.dma_start(rope[:, :, :], ins["const_rope"][0:QK_ROPE]).then_inc(s_in, 16)

            def rotary(buf, ap, mark):
                bank = banks.take()
                m = fmm(bank.ap[0:QK_ROPE, :], [(sh["rotate"][0:QK_ROPE, 0:QK_ROPE], ap)], mark, *bank.busy)
                t = work.take()
                m1 = VE(lambda v: v.tensor_tensor(t.ap[0:QK_ROPE, :], bank.ap[0:QK_ROPE, :], rope[:, 1, :], MUL), m,
                        (s_in, 16), *t.busy)
                banks.give(bank, m1)
                m2 = VE(lambda v: v.tensor_tensor(ap, ap, rope[:, 0, :], MUL), m1)
                m2 = VE(lambda v: v.tensor_tensor(ap, ap, t.ap[0:QK_ROPE, :], ADD), m2)
                work.give(t, m2)
                return m2

            with ExitStack() as early:
                ctx = s("ctx", [P, DT, CTX], c=early)
                nc.sync.dma_start(ctx[:, :, :], ins["ctx_t"].rearrange("(k p) t -> p k t", p=P)).then_inc(s_in, 16)
                hc = Split(s("hc_hi", [P, DT, CTX], F32R, early), s("hc_lo", [P, DT, CTX], F32R, early), DT)
                sh["norm_to"](hc, [(ctx[:, k, :], ((s_in, 32),)) for k in range(DT)],
                              lambda k: gains[:, 1, k:k + 1], D, n=CTX, shifts=lambda k: modv[:, SHIFT1 + k, 1:2])
                w = use(("c_kv",))
                held = []
                for X, n, c0 in ((hc, CTX, 0), (U, T, CTX)):
                    tiles = []
                    for j in range(2):
                        bank, m = feature_tile(w, j * P, X, n=n)
                        tiles.append((bank, m))
                    held.append((tiles, n, c0))
                used(w, m)
                for tiles, n, c0 in held:
                    marks = sh["norm_to"](kv, [(b.ap[:, 0:n], (m,)) for b, m in tiles],
                                          lambda k: column("g_kv", k), 2 * P, n=n, c0=c0)
                    for (b, _), mk in zip(tiles, marks):
                        banks.give(b, mk)
                w = use(("c_kr",))
                for X, n, c0 in ((hc, CTX, 0), (U, T, CTX)):
                    bank, m = feature_tile(w, 0, X, width=QK_ROPE, n=n)
                    m_kr = AC(lambda v: v.activation(kr[:, c0:c0 + n], bank.ap[0:QK_ROPE, 0:n], ACT.Copy), m)
                    banks.give(bank, m_kr)
                used(w, m)
                m_kr = (m_kr, rotary(None, kr[:, CTX:KEYS], m_kr))
                tiles = []
                for key, n in ((("c_q",), 2), (("c_q2",), 1)):
                    w = use(key)
                    for j in range(n):
                        tiles.append(feature_tile(w, j * P, U))
                    used(w, tiles[-1][1])
                marks = sh["norm_to"](qa, [(b.ap, (m,)) for b, m in tiles], lambda k: column("g_q", k), 3 * P)
                for (b, _), mk in zip(tiles, marks):
                    banks.give(b, mk)
                sh["barrier"]()

            def project_conv():
                for t in range(DT):
                    w = use(("c_conv", t))
                    ba, ma = feature_tile(w, 0, U)
                    bg, mg = feature_tile(w, P, U)
                    used(w, mg)
                    sg = work.take()
                    m = AC(lambda v: v.activation(sg.ap, bg.ap, ACT.Sigmoid), mg, *sg.busy)
                    banks.give(bg, m)
                    conv_ready[t] = VE(lambda v: v.tensor_tensor(conv[:, t, HALO:HALO + T], ba.ap, sg.ap, MUL), m,
                                       ma, m_halo)
                    banks.give(ba, conv_ready[t])
                    work.give(sg, conv_ready[t])
                    yield

            acc = [Buf(s(f"acc{i}", [P, T])[:, :]) for i in range(2)]

            def convolve():
                for t in range(DT):
                    a = acc[t % 2]
                    m = VE(lambda v: v.tensor_scalar(a.ap, conv[:, t, 0:T], column("w_dw", t), column("b_dw", t), MUL,
                                                     ADD), conv_ready[t], *a.busy)
                    for i in range(1, CONV_W):
                        m = VE(lambda v: v.scalar_tensor_tensor(out=a.ap, in0=conv[:, t, i:i + T],
                                                                scalar=column("w_dw", i * DT + t), in1=a.ap, op0=MUL,
                                                                op1=ADD), m)
                        if i % 5 == 0:
                            yield
                    conv_done[t] = AC(lambda v: v.activation(conv[:, t, HALO:HALO + T], a.ap, ACT.Copy), m)
                    a.busy = (conv_done[t],)
                    yield

            kn, vt = s("kn", [P, KEYS]), s("vt", [P, KT3, P])
            qn, qr = s("qn", [P, T]), s("qr", [QK_ROPE, T])
            prob = [Buf(s(f"prob{i}", [P, KEYS])[:, :]) for i in range(2)]
            prob_t = Buf(s("prob_t", [P, KT3, P]))
            st = s("stats", [P, 2, 8])
            kn_busy, q_busy = [()], [()]

            def heads():
                for h in range(8):
                    w = use(("c_ukv", h))
                    marks = []
                    for c0, n in ((0, T), (T, KEYS - T)):
                        bank, m = feature_tile(w, 0, kv, n=n, c0=c0)
                        marks.append(AC(lambda v: v.activation(kn[:, c0:c0 + n], bank.ap[:, 0:n], ACT.Copy), m,
                                        *kn_busy[0]))
                        banks.give(bank, marks[-1])
                    for k in range(KT3):
                        bank, m = token_tile(w, P, P, kv, k * P)
                        marks.append(AC(lambda v: v.activation(vt[:, k, :], bank.ap[:, 0:P], ACT.Copy), m,
                                        *kn_busy[0]))
                        banks.give(bank, marks[-1])
                    used(w, m)
                    w = use(("c_uq", h))
                    bank, m = feature_tile(w, 0, qa)
                    marks.append(AC(lambda v: v.activation(qn[:, :], bank.ap, ACT.Copy), m, *kn_busy[0]))
                    banks.give(bank, marks[-1])
                    bank, m = feature_tile(w, P, qa, width=QK_ROPE)
                    used(w, m)
                    m = AC(lambda v: v.activation(qr[:, :], bank.ap[0:QK_ROPE, :], ACT.Copy), m, *kn_busy[0])
                    banks.give(bank, m)
                    marks.append(rotary(None, qr[:, :], m))
                    yield
                    o_bank = banks.take()
                    PE.wait(*o_bank.busy)

                    def scores(n):
                        q = slice(n * P, (n + 1) * P)
                        two = [banks.take(), banks.take()]
                        PE.wait(*two[0].busy, *two[1].busy, *marks, *m_kr)
                        for b, (c0, width) in zip(two, ((0, T), (T, KEYS - T))):
                            m = fmm(b.ap[:, 0:width], [(qn[:, q], kn[:, c0:c0 + width]), (qr[:, q], kr[:, c0:c0 + width])])
                        pb, stat = prob[n % 2], st[:, n % 2, :]
                        VE(lambda v: v.tensor_reduce(stat[:, 0:1], two[0].ap, AX_X, MAX), m, *pb.busy)
                        m = VE(lambda v: v.tensor_reduce(stat[:, 1:2], two[1].ap[:, 0:KEYS - T], AX_X, MAX))
                        m = VE(lambda v: v.tensor_scalar(stat[:, 2:3], stat[:, 0:1], stat[:, 1:2], -ATTN_SCALE, MAX,
                                                         MUL), m)
                        m1 = AC(lambda v: v.activation(pb.ap[:, 0:T], two[0].ap, ACT.Exp, bias=stat[:, 2:3],
                                                       scale=ATTN_SCALE, accum_out=stat[:, 3:4]), m, *pb.busy)
                        m2 = AC(lambda v: v.activation(pb.ap[:, T:KEYS], two[1].ap[:, 0:KEYS - T], ACT.Exp,
                                                       bias=stat[:, 2:3], scale=ATTN_SCALE, accum_out=stat[:, 4:5]))
                        banks.give(two[0], m1)
                        banks.give(two[1], m2)
                        m = VE(lambda v: v.tensor_tensor(stat[:, 5:6], stat[:, 3:4], stat[:, 4:5], ADD), m1, m2)
                        m = VE(lambda v: v.reciprocal(stat[:, 6:7], stat[:, 5:6]), m)
                        return VE(lambda v: v.tensor_scalar(pb.ap, pb.ap, stat[:, 6:7], None, MUL), m)

                    def values(n, m_p):
                        pb = prob[n % 2]
                        two = [banks.take(), banks.take()]
                        PE.wait(*two[0].busy, *two[1].busy, m_p)
                        for k in range(KT3):
                            m = PE(lambda v: v.transpose(two[k // 4].ap[:, (k % 4) * P:(k % 4 + 1) * P],
                                                         pb.ap[:, k * P:(k + 1) * P], ident))
                        pb.busy = (m,)
                        flat = prob_t.ap[:, :, :].rearrange("p k t -> p (k t)")
                        m1 = AC(lambda v: v.activation(flat[:, 0:T], two[0].ap, ACT.Copy), m, *prob_t.busy)
                        m2 = AC(lambda v: v.activation(flat[:, T:KEYS], two[1].ap[:, 0:KEYS - T], ACT.Copy))
                        banks.give(two[0], m1)
                        banks.give(two[1], m2)
                        m = fmm(o_bank.ap[:, n * P:(n + 1) * P], [(vt[:, k, :], prob_t.ap[:, k, :]) for k in range(KT3)],
                                m1, m2)
                        prob_t.busy = (m,)
                        return m

                    m_p = scores(0)
                    for n in range(NT):
                        nxt = scores(n + 1) if n + 1 < NT else None
                        yield
                        m_o = values(n, m_p)
                        m_p = nxt
                    kn_busy[0] = (m_o,)
                    o_ready[h] = VE(lambda v: v.tensor_copy(O[:, h, :], o_bank.ap), m_o, (s_save, 16), *readers)
                    banks.give(o_bank, o_ready[h])
                    yield

            run(project_conv())
            together(heads(), convolve())
            sh["barrier"]()
        with ExitStack() as c:
            gate = [sh["sb"]("c_gate_conv", [P, DT, T], F32, c), sh["sb"]("c_gate_mla", [P, DT, T], F32, c)]
            g_ready = [[None] * DT, [None] * DT]
            for c0 in range(0, 2 * D, 256):
                w = use(("c_gate", c0))
                for j in range(2):
                    i, k = divmod(c0 // P + j, DT)
                    bank, m = feature_tile(w, j * P, U)
                    g_ready[i][k] = AC(lambda v: v.activation(gate[i][:, k, :], bank.ap, ACT.Sigmoid), m)
                    banks.give(bank, g_ready[i][k])
                used(w, m)
            sh["begin_u"]()
            m_o = []
            for k in range(DT):
                m_o += split_to(U, k, O[:, k, :], (o_ready[k],))
            SP.wait(*m_o)
            nc.sync.dma_start(x[:, :, :], saved).then_inc(s_save, 16)
            for k in range(DT):
                x_ready[k] = ((s_save, 32),)
            for c0 in range(0, D, 256):
                w = use(("c_omla", c0))
                for j in range(2):
                    k = c0 // P + j
                    bank, m = feature_tile(w, j * P, U)
                    g_ready[1][k] = VE(lambda v: v.tensor_tensor(gate[1][:, k, :], bank.ap, gate[1][:, k, :], MUL), m,
                                       g_ready[1][k])
                    banks.give(bank, g_ready[1][k])
                used(w, m)
            bank = banks.take()
            PE.wait(*bank.busy)
            for k in range(DT):
                m = PE(lambda v: v.matmul(bank.ap, ones, conv[:, k, HALO:HALO + T], start=k == 0, stop=k == DT - 1),
                       conv_done[k])
            mu = work.take()
            m = VE(lambda v: v.tensor_scalar(mu.ap, bank.ap, 1.0 / D, None, MUL), m, *mu.busy)
            banks.give(bank, m)
            tiles = []
            for k in range(DT):
                t = conv[:, k, HALO:HALO + T]
                m1 = VE(lambda v: v.tensor_tensor(t, t, mu.ap, SUB), m)
                tiles.append((t, (m1,)))
            work.give(mu, m1)
            r, m_r = sh["inverse_rms"](tiles, D)
            sh["begin_u"]()
            for k, (t, _) in enumerate(tiles):
                m = VE(lambda v: v.scalar_tensor_tensor(out=t, in0=t, scalar=column("ln_g", k), in1=r.ap, op0=MUL,
                                                        op1=MUL), m_r)
                m1 = AC(lambda v: v.activation(t, t, ACT.Silu, bias=column("ln_b", k)), m)
                split_to(U, k, t, (m1,))
            work.give(r, m)
            for c0 in range(0, D, 256):
                w = use(("c_pw", c0))
                for j in range(2):
                    k = c0 // P + j
                    bank, m = feature_tile(w, j * P, U)
                    m1 = VE(lambda v: v.tensor_tensor(gate[0][:, k, :], bank.ap, gate[0][:, k, :], MUL), m,
                            g_ready[0][k])
                    banks.give(bank, m1)
                    g_ready[0][k] = VE(lambda v: v.tensor_tensor(gate[0][:, k, :], gate[0][:, k, :],
                                                                 gate[1][:, k, :], ADD), m1, g_ready[1][k])
                used(w, m)
            sh["begin_u"]()
            for k in range(DT):
                split_to(U, k, gate[0][:, k, :], (g_ready[0][k],))
            for c0 in range(0, D, 256):
                w = use(("c_out", c0))
                for j in range(2):
                    bank, m = feature_tile(w, j * P, U)
                    sh["add_to_x"](c0 // P + j, bank, m, lambda k: modv[:, GATE1 + k, 0:1])
                used(w, m)
            sh["barrier"]()

        def hidden(w, j, t, H, slot):
            ba, ma = feature_tile(w, 0, U)
            bb, mb = feature_tile(w, P, U)
            a = work.take()
            m = AC(lambda v: v.activation(a.ap, ba.ap, ACT.Silu), ma, *a.busy)
            banks.give(ba, m)
            m = VE(lambda v: v.tensor_tensor(a.ap, a.ap, bb.ap, MUL), m, mb)
            banks.give(bb, m)
            work.give(a, *split_to(H, slot, a.ap, (m,)))
            return mb

        sh["begin_u"]()
        sh["norm_to"](U, sh["x_tiles"](), lambda k: gains[:, 2, k:k + 1], D,
                      shifts=lambda k: modv[:, SHIFT2 + k, 0:1])
        sh["mlp"]("ffn3", FF_TILES, 1, hidden, scale=lambda k: modv[:, GATE2 + k, 0:1])
    final_to_x(sh, "g_final_3")



def tile_columns(v):
    return np.ascontiguousarray(np.reshape(v, (-1, P)).T)


def pack_vectors(a):
    cols, n_cols = column_plan()
    dt_pad = np.zeros(P, np.float32)
    out = np.zeros((P, n_cols), np.float32)

    def put(name, block):
        at, n = cols[name]
        out[0:block.shape[0], at:at + n] = block

    put("norm1", tile_columns(a["norm1_w"]))
    put("norm2", tile_columns(a["norm2_w"]))
    put("lb", tile_columns(a["a_lb_logits"]))
    put("a_norm", tile_columns(a["a_norm_w"]))
    put("conv_w", tile_columns(a["b_conv_w"]))
    put("conv_b", tile_columns(a["b_conv_b"]))
    put("d_skip", tile_columns(np.repeat(a["b_d_skip"].reshape(-1), HEAD_P)))
    put("b_norm", tile_columns(a["b_norm_w"]))
    put("dt_bias", a["b_dt_bias"].reshape(N_DT, 1))
    put("a_log", a["b_a_log"].reshape(N_DT, 1))
    put("ffn_cw", tile_columns(a["ffn_conv_w"]))
    put("ffn_cb", tile_columns(a["ffn_conv_b"]))
    put("final", tile_columns(a["final_norm_w"]))
    for n in ("g_mix_2", "g_mlp_2", "g_pe_2", "g_final_2", "g_mix_3", "g_ffn_3", "ln_g", "ln_b", "g_final_3"):
        put(n, tile_columns(a[n if n in a else n + "_3"]))
    c_both = np.stack([a["c_3"].reshape(-1), a["c_ctx_3"].reshape(-1)])
    put("c_c", c_both.reshape(2, DT, P).transpose(2, 1, 0).reshape(P, 16))
    put("b_mod", tile_columns(a["b_mod_3"]))
    put("g_q", tile_columns(a["g_q_3"]))
    put("g_kv", tile_columns(a["g_kv_3"]))
    put("w_dw", tile_columns(a["w_dw_3"]))
    put("b_dw", tile_columns(a["b_dw_3"]))
    return out


def pack_weights(a):
    plan = weight_plan()
    out = np.zeros((len(plan), P, SLOT), np.float32)
    for s, (_, kt, pieces) in enumerate(plan):
        width = sum(p[4] for p in pieces)
        view = out[s, :, 0:kt * width].reshape(P, kt, width)
        at = 0
        for name, i, r0, c0, n in pieces:
            view[:, :, at:at + n] = a[name][i, r0:r0 + kt * P, c0:c0 + n].reshape(kt, P, n).transpose(1, 0, 2)
            at += n
    return out


def host_arrays(a):
    arrays = {
        "x_t": np.ascontiguousarray(a["x"][0].T),
        "p_t": np.ascontiguousarray(a["p_2"][0, 0].T),
        "ctx_t": np.ascontiguousarray(a["ctx_3"][0].T),
        "sinks": np.ascontiguousarray(a["sinks_2"]),
        "rel_bias": np.ascontiguousarray(a["rel_bias_2"]),
        "vectors": pack_vectors(a),
        "weights": pack_weights(a),
    }
    arrays.update(shape_constants())
    return arrays


def kernel(**inputs):
    import concourse.bacc as bacc
    from concourse.bass_utils import run_bass_kernel_spmd

    arrays = host_arrays({k: np.asarray(v) for k, v in inputs.items()})
    nc = bacc.Bacc("TRN2", target_bir_lowering=False, num_devices=1)
    ins = {n: nc.dram_tensor(n, v.shape, mybir.dt.from_np(v.dtype), kind="ExternalInput").ap()
           for n, v in arrays.items()}
    out = nc.dram_tensor("out_t", (D, T), F32, kind="ExternalOutput").ap()
    build(nc, ins, out)
    r = run_bass_kernel_spmd(nc, [arrays], core_ids=[0])
    return np.ascontiguousarray(r.results[0]["out_t"].T)[None]
```

```python
from collections import deque
from contextlib import ExitStack

import numpy as np
import concourse.bass as bass
from concourse import mybir

F32 = mybir.dt.float32
F32R = mybir.dt.float32r
U8 = mybir.dt.uint8
ALU = mybir.AluOpType
ACT = mybir.ActivationFunctionType
AX_X = mybir.AxisListType.X
ADD, SUB, MUL, MAX, MIN = ALU.add, ALU.subtract, ALU.mult, ALU.max, ALU.min

P = 128
T = 512
NT = T // P
D = 1024
DT = D // P
SLOT = 2048
N_STAGE = 2
N_SPLIT = 3
LEAD = 2
N_MOD = 3
MOD_SLOTS = 6 * D // 256
EPS = 1e-6
NEG = -1e30

HG_HEADS = 8
GROUPS = 8
HEADS_PER_GROUP = 4
HEAD_P = 64
D_INNER = 2048
GN = 1024
N_DT = 64
FF = 2816
FF_TILES = FF // P
FF2_TILES = 4096 // P
N_BUCKETS = 32
WINDOW = 128
CTX = 256
KEYS = CTX + T
KT3 = KEYS // P
QK_NOPE = 128
QK_ROPE = 64
ATTN_SCALE = float((QK_NOPE + QK_ROPE) ** -0.5)
CONV_W = 31
HALO = CONV_W // 2
SUB_LEVELS = [1, 2, 4, 8, 16, 32, 64]



def chunks_of(n, size):
    return [(a, min(size, n - a)) for a in range(0, n, size)]


def ffn_plan(tag, n_tiles, hidden_slots, out_name, out_index):
    plan = []
    parts = chunks_of(n_tiles, 4)
    for i in range(len(parts) + 1):
        if i < len(parts):
            for slot in hidden_slots(*parts[i]):
                plan.append(slot)
        if i > 0:
            t0, n = parts[i - 1]
            width = SLOT // n
            for c in range(0, D, width):
                plan.append(((tag + "_out", t0, c), n, [(out_name, out_index, t0 * P, c, width)]))
    return plan


def weight_plan():
    plan = []
    for h in range(HG_HEADS):
        a = ("a_w_in", 0, 0)
        if h % 2 == 0:
            plan.append((("gla_v", h), DT, [(*a, 3 * D + h * P, 2 * P)]))
        plan.append((("gla_qf", h), DT, [(*a, h * P, P), (*a, D + h * P, P)]))
        plan.append((("gla_bg", h), DT, [(*a, 2 * D + h * P, P), (*a, 4 * D + h * P, P)]))
    for c in range(0, D, 256):
        plan.append((("gla_out", c), DT, [("a_w_out", 0, 0, c, 256)]))

    def glu(tag, name, index):
        def slots(t0, n):
            return [((tag, t), DT, [(name, index, 0, t * P, P), (name, index, 0, FF + t * P, P)])
                    for t in range(t0, t0 + n)]
        return slots

    plan += ffn_plan("ffn0", FF_TILES, glu("ffn0", "ffn_w_in", 0), "ffn_w_out", 0)
    b = ("b_w_in", 0, 0)
    plan.append((("m_dt",), DT, [(*b, 2 * D_INNER + 2 * GN, N_DT)]))

    def m_proj(g):
        return [(("m_x", g), DT, [(*b, D_INNER + g * 256, 256)]),
                (("m_bc", g), DT, [(*b, 2 * D_INNER + g * P, P), (*b, 2 * D_INNER + GN + g * P, P)])]
    plan += m_proj(0)
    for g in range(GROUPS):
        plan.append((("m_z", g), DT, [(*b, g * 256, 256)]))
        if g > 0:
            plan.append((("m_out", g - 1), 2, [("b_w_out", 0, (g - 1) * 256, 0, D)]))
        if g + 1 < GROUPS:
            plan += m_proj(g + 1)
    plan.append((("m_out", GROUPS - 1), 2, [("b_w_out", 0, (GROUPS - 1) * 256, 0, D)]))
    plan += ffn_plan("ffn1", FF_TILES, glu("ffn1", "ffn_w_in", 1), "ffn_w_out", 1)

    w = ("w_in_2", 0, 0)
    plan.append((("b2_w_k",), DT, [(*w, 2048 + 64 * (i // 2), 64) for i in range(4)]))
    plan.append((("b2_w_v",), DT, [(*w, 2176, 128)]))
    for c in (0, 256):
        plan.append((("b2_w_q", c), DT, [(*w, 1536 + c, 256)]))
    for p in range(4):
        if p % 2 == 0:
            plan.append((("b2_s_v", p), DT, [(*w, 1024 + p * P, 256)]))
        plan.append((("b2_s_qk", p), DT, [(*w, p * P, P), (*w, 512 + p * P, P)]))
    for c in (0, 512):
        plan.append((("b2_up_a", c), 4, [("w_up_a_2", 0, 0, c, 512)]))
    for c in range(0, D, 256):
        plan.append((("b2_gate_a", c), DT, [(*w, 2304 + c, 256)]))
    for c in (0, 512):
        plan.append((("b2_up_b", c), 4, [("w_up_b_2", 0, 0, c, 512)]))
    for c in range(0, D, 256):
        plan.append((("b2_gate_b", c), DT, [(*w, 3328 + c, 256)]))
    for c in range(0, D, 256):
        plan.append((("b2_o", c), DT, [("w_o_2", 0, 0, c, 256)]))

    def ff1(t0, n):
        return [(("ff2", t), DT, [("w_ff1_2", 0, 0, t * P, 256)]) for t in range(t0, t0 + n, 2)]
    plan += ffn_plan("ff2", FF2_TILES, ff1, "w_ff2_2", 0)
    plan.append((("b2_pe",), 2, [("w_pe_2", 0, 0, 0, D)]))
    for c in range(0, D, 256):
        plan.append((("b2_pg", c), DT, [("w_pg_2", 0, 0, c, 256)]))

    w = ("w_in_3", 0, 0)
    plan.append((("c_kv",), DT, [(*w, 2432, 256)]))
    plan.append((("c_kr",), DT, [(*w, 2688, QK_ROPE)]))
    plan.append((("c_q",), DT, [(*w, 2048, 256)]))
    plan.append((("c_q2",), DT, [(*w, 2304, 128)]))
    for t in range(DT):
        plan.append((("c_conv", t), DT, [(*w, t * P, P), (*w, D + t * P, P)]))
    for h in range(8):
        plan.append((("c_ukv", h), 2, [("w_ukv_3", 0, 0, h * 256, 256)]))
        plan.append((("c_uq", h), 3, [("w_uq_3", 0, 0, h * 192, 192)]))
    for c in range(0, 2 * D, 256):
        plan.append((("c_gate", c), DT, [(*w, 2752 + c, 256)]))
    for c in range(0, D, 256):
        plan.append((("c_omla", c), DT, [("w_o_mla_3", 0, 0, c, 256)]))
    for c in range(0, D, 256):
        plan.append((("c_pw", c), DT, [("w_pw_3", 0, 0, c, 256)]))
    for c in range(0, D, 256):
        plan.append((("c_out", c), DT, [("w_out_3", 0, 0, c, 256)]))
    plan += ffn_plan("ffn3", FF_TILES, glu("ffn3", "w_13_3", 0), "w_2_3", 0)
    return plan


def column_plan():
    n = [("norm1", 16), ("norm2", 16), ("lb", 24), ("a_norm", 1), ("conv_w", 5 * 32), ("conv_b", 32),
         ("d_skip", 16), ("b_norm", 16), ("dt_bias", 1), ("a_log", 1), ("ffn_cw", 2 * 3 * FF_TILES),
         ("ffn_cb", 2 * FF_TILES), ("final", 8), ("g_mix_2", 8), ("g_mlp_2", 8), ("g_pe_2", 8),
         ("g_final_2", 8), ("c_c", 16), ("b_mod", 48), ("g_mix_3", 8), ("g_ffn_3", 8), ("g_q", 3),
         ("g_kv", 2), ("w_dw", 31 * 8), ("b_dw", 8), ("ln_g", 8), ("ln_b", 8), ("g_final_3", 8)]
    at, out = 0, {}
    for name, count in n:
        out[name] = (at, count)
        at += count
    return out, at


def bucket_of(dist):
    d = np.maximum(dist, 0)
    df = np.maximum(d, 1).astype(np.float32)
    large = 16 + (np.log(df / np.float32(16)) / np.float32(np.log(8.0)) * np.float32(16)).astype(np.int32)
    return np.where(d < 16, d, np.minimum(large, N_BUCKETS - 1))


def shape_constants():
    s, t = np.arange(P)[:, None], np.arange(P)[None, :]
    levels = np.zeros((P, len(SUB_LEVELS) + 1, P), np.float32)
    for i, half in enumerate(SUB_LEVELS):
        levels[:, i, :] = (s // (2 * half) == t // (2 * half)) & (s // half != t // half)
    levels[:, len(SUB_LEVELS), :] = s > t
    f = np.zeros((P, 8, P), np.float32)
    f[:, 0, :] = s == t
    f[:, 1, :] = 1.0
    f[:, 2, :] = s <= t
    f[:, 3, :] = s >= t
    f[:, 4, :] = s < t
    f[:, 5, :] = s > t
    for base in range(0, P, 32):
        for i in range(16):
            f[base + 16 + i, 6, base + i] = -1.0
            f[base + i, 6, base + 16 + i] = 1.0
    f[:, 7, :] = s + t == P - 1
    dist = 255 - np.arange(384)
    onehot = np.zeros((N_BUCKETS, 384), np.float32)
    inside = (dist >= 0) & (dist < WINDOW)
    onehot[bucket_of(dist)[inside], np.nonzero(inside)[0]] = 1.0
    outside = np.zeros((8, 384), np.float32)
    outside[:, ~inside] = NEG
    pos = np.arange(T)
    inv = (np.float32(10000.0) ** (-np.arange(0, 32, 2, dtype=np.float32) / np.float32(32))).astype(np.float32)
    row = (pos // 64).astype(np.float32)[None, :] * inv[:, None]
    col = (pos % 64).astype(np.float32)[None, :] * inv[:, None]
    ang = np.concatenate([row, row, col, col] * 2, 0)
    rope = np.stack([np.cos(ang), np.sin(ang)], 1).astype(np.float32)
    return {"const_levels": levels, "const_f": f, "const_onehot": onehot, "const_outside": outside,
            "const_rope": rope}



class Engine:

    def __init__(self, e, done):
        self.e, self.done, self.count, self.passed = e, done, 0, {}

    def wait(self, *marks):
        for sem, value in marks:
            if value > self.passed.get(sem.name, 0):
                self.passed[sem.name] = value
                self.e.wait_ge(sem, value)

    def __call__(self, instruction, *marks):
        self.wait(*marks)
        instruction(self.e).then_inc(self.done, 1)
        self.count += 1
        return (self.done, self.count)

    def quiet(self, instruction, *marks):
        self.wait(*marks)
        instruction(self.e)

    def last(self):
        return (self.done, self.count)


HAND = {2: [("hand", 0)], 3: [("hand", 1)], 4: [("turn", 0)], 5: [("state", 0), ("turn", 1)], 6: [("state", 1)]}
GLA_ORDER = ("apfapap" + "aap" * 7, "apf" + "aap" * 2 + "aaap" * 5)

LOG_EXP = "natural_log_exp_and_others"
TABLES = {ACT.Exp: LOG_EXP, ACT.Ln: LOG_EXP, ACT.Sigmoid: "sigmoid_and_others", ACT.Silu: "silu_and_others"}


class ScalarWithTables:

    def __init__(self, e):
        self.e, self.loaded = e, None

    def wait_ge(self, sem, value):
        self.e.wait_ge(sem, value)

    def activation(self, out, in_, func, **more):
        table = TABLES.get(func, self.loaded)
        if table != self.loaded:
            self.e.preload_act_table_set(table)
            self.loaded = table
        return self.e.activation(out, in_, func, **more)


class Buf:

    def __init__(self, ap):
        self.ap, self.busy = ap, ()


class Pool_of:

    def __init__(self, bufs):
        self.idle = deque(bufs)

    def take(self):
        return self.idle.popleft()

    def give(self, buf, *marks):
        buf.busy = marks
        self.idle.append(buf)


def together(*parts):
    live = [[0, steps, g] for g, steps in parts]
    while live:
        part = min(live, key=lambda p: (p[0] + 1) / p[1])
        try:
            next(part[2])
            part[0] += 1
        except StopIteration:
            live.remove(part)


def in_order(letters, **parts):
    for letter in letters:
        next(parts[letter], None)
    for g in parts.values():
        run(g)


def run(g):
    for _ in g:
        pass


def build(nc, ins, out, debug=None):
    plan = weight_plan()
    cols, n_cols = column_plan()
    ctx = ExitStack()
    with ctx:
        def sb(name, shape, dt=F32, c=ctx):
            return c.enter_context(nc.sbuf_tensor(name, shape, dt))

        def sem(name):
            return ctx.enter_context(nc.semaphore(name))

        PE = Engine(nc.tensor, sem("pe_done"))
        VE = Engine(nc.vector, sem("vector_done"))
        AC = Engine(ScalarWithTables(nc.scalar), sem("scalar_done"))
        PO = Engine(nc.gpsimd, sem("pool_done"))
        SP = Engine(nc.sync, sem("sync_done"))
        s_stage = [sem(f"stage{i}_filled") for i in range(N_STAGE)]
        s_load = sem("constants_loaded")
        s_io = sem("scratch_dma")

        psum = ctx.enter_context(nc.psum_tensor("banks", [P, 8, T], F32))
        banks = Pool_of([Buf(psum[:, i, :]) for i in range(8)])

        x = sb("x", [P, DT, T])
        u_hi, u_lo = sb("u_hi", [P, DT, T], F32R), sb("u_lo", [P, DT, T], F32R)
        stage = sb("stage", [P, N_STAGE, SLOT])
        w_hi, w_lo = sb("w_hi", [P, N_SPLIT, SLOT], F32R), sb("w_lo", [P, N_SPLIT, SLOT], F32R)
        vec = sb("vec", [P, n_cols])
        cf = sb("cf", [P, 8, P])
        ident, ones, m_le, m_ge, m_lt, m_gt, rotate, turn = (cf[:, i, :] for i in range(8))
        levels = sb("levels", [P, len(SUB_LEVELS) + 1, P], U8)
        modv = sb("modv", [P, 48, 2])
        work = Pool_of([Buf(sb(f"work{i}", [P, T])[:, :]) for i in range(4)])

        def column(name, i, n=1):
            return vec[:, cols[name][0] + i:cols[name][0] + i + n]

        def load(dst, src):
            nc.sync.dma_start(dst, src).then_inc(s_load, 16)
            load.count += 16
        load.count = 0
        load(x[:, :, :], ins["x_t"].rearrange("(k p) t -> p k t", p=P))
        load(vec[:, :], ins["vectors"])
        load(cf[:, :, :], ins["const_f"])
        levels_scope = ExitStack()
        levels_f = sb("levels_f", [P, len(SUB_LEVELS) + 1, P], F32, levels_scope)
        load(levels_f[:, :, :], ins["const_levels"])
        loaded = (s_load, load.count)
        VE(lambda e: e.tensor_copy(levels[:, :, :], levels_f[:, :, :]), loaded)

        stream = {"loaded": 0, "split": 0, "used": 0}
        released = {}
        split_busy = [()] * N_SPLIT
        split_at = {}
        n_split = [0]
        split_ready = {}
        limit = len(plan) if debug is None else debug.get("slots", len(plan))

        def slot_size(s):
            return plan[s][1] * sum(piece[4] for piece in plan[s][2])

        def pump():
            while stream["loaded"] < limit:
                s = stream["loaded"]
                if s >= N_STAGE and s - N_STAGE not in released:
                    return
                stream["loaded"] = s + 1
                SP.wait(*released.get(s - N_STAGE, ()))
                n = slot_size(s)
                nc.sync.dma_start(stage[:, s % N_STAGE, 0:n], ins["weights"][s, :, 0:n]).then_inc(
                    s_stage[s % N_STAGE], 16)

        def filled(s):
            return (s_stage[s % N_STAGE], 16 * (s // N_STAGE + 1))

        def split(s):
            if s >= limit or s < stream["split"]:
                return
            stream["split"] = s + 1
            b, n, st = n_split[0] % N_SPLIT, slot_size(s), s % N_STAGE
            n_split[0] += 1
            split_at[s] = b
            m_hi = AC(lambda e: e.activation(w_hi[:, b, 0:n], stage[:, st, 0:n], ACT.Copy),
                      filled(s), *split_busy[b])
            m_lo = PO(lambda e: e.tensor_tensor(w_lo[:, b, 0:n], stage[:, st, 0:n],
                                                w_hi[:, b, 0:n].bitcast(F32), SUB), filled(s), m_hi,
                      *split_busy[b])
            split_ready[s] = (m_hi, m_lo)
            released[s] = (m_hi, m_lo)
            pump()

        pump()

        class Weights:
            pass

        def use(key):
            s = stream["used"]
            assert plan[s][0] == key, (plan[s][0], key)
            stream["used"] = s + 1
            for i in range(s, s + LEAD + 1):
                split(i)
            w = Weights()
            w.s, kt = s, plan[s][1]
            n = slot_size(s)
            w.b = split_at[s]
            w.hi = w_hi[:, w.b, 0:n].rearrange("p (k c) -> p k c", k=kt)
            w.lo = w_lo[:, w.b, 0:n].rearrange("p (k c) -> p k c", k=kt)
            w.ready = split_ready[s]
            return w

        def used(w, mark):
            split_busy[w.b] = (mark,)

        def product(bank, dst, terms, *marks):
            PE.wait(*bank.busy, *marks)
            for i, (a_hi, a_lo, b_hi, b_lo, need) in enumerate(terms):
                PE.wait(*need)
                first, end = i == 0, i == len(terms) - 1
                nc.tensor.matmul(dst, a_hi, b_hi, start=first, stop=False)
                nc.tensor.matmul(dst, a_hi, b_lo, start=False, stop=False)
                last = nc.tensor.matmul(dst, a_lo, b_hi, start=False, stop=end)
            last.then_inc(PE.done, 1)
            PE.count += 1
            return PE.last()

        class Split:

            def __init__(self, hi, lo, n):
                self.hi, self.lo, self.n = hi, lo, n
                self.ready = [()] * n
                self.busy = self.read = ()

        U = Split(u_hi, u_lo, DT)

        def split_to(dst, k, src, m_src, n=T, c0=0, on=None):
            return split_lo(dst, k, src, m_src, split_hi(dst, k, src, m_src, n, c0), n, c0, on)

        def split_hi(dst, k, src, m_src, n=T, c0=0):
            return AC(lambda e: e.activation(dst.hi[:, k, c0:c0 + n], src, ACT.Copy), *m_src, *dst.busy)

        def split_lo(dst, k, src, m_src, m1, n=T, c0=0, on=None):
            hi, lo = dst.hi[:, k, c0:c0 + n], dst.lo[:, k, c0:c0 + n]
            m2 = (on or VE)(lambda e: e.tensor_tensor(lo, src, hi.bitcast(F32), SUB), m1, *m_src, *dst.busy)
            dst.ready[k] = (*dst.ready[k], m1, m2)
            return (m1, m2)

        def feature_tile(w, c, X, width=P, n=T, c0=0):
            bank = banks.take()
            kt = plan[w.s][1]
            terms = [(w.hi[:, k, c:c + width], w.lo[:, k, c:c + width], X.hi[:, k, c0:c0 + n],
                      X.lo[:, k, c0:c0 + n], X.ready[k]) for k in range(kt)]
            m = product(bank, bank.ap[0:width, 0:n], terms, *w.ready)
            X.read = (m,)
            return bank, m

        def token_tile(w, c, width, X, t0):
            bank = banks.take()
            kt = plan[w.s][1]
            terms = [(X.hi[:, k, t0:t0 + P], X.lo[:, k, t0:t0 + P], w.hi[:, k, c:c + width],
                      w.lo[:, k, c:c + width], X.ready[k]) for k in range(kt)]
            m = product(bank, bank.ap[:, 0:width], terms, *w.ready)
            X.read = (m,)
            return bank, m

        def fmm(bank_ap, pairs, *marks):
            PE.wait(*marks)
            for i, (a, b) in enumerate(pairs):
                last = nc.tensor.matmul(bank_ap, a, b, start=i == 0, stop=i == len(pairs) - 1)
            last.then_inc(PE.done, 1)
            PE.count += 1
            return PE.last()

        def inverse_rms(tiles, width, n=T, rows=P):
            bank = banks.take()
            PE.wait(*bank.busy)
            for i, (ap, marks) in enumerate(tiles):
                sq = work.take()
                m = AC(lambda e: e.activation(sq.ap[:, 0:n], ap, ACT.Square), *marks, *sq.busy)
                last = PE(lambda e: e.matmul(bank.ap[:, 0:n], ones, sq.ap[:, 0:n], start=i == 0,
                                             stop=i == len(tiles) - 1), m, loaded)
                work.give(sq, last)
            r = work.take()
            m = VE(lambda e: e.tensor_scalar(r.ap[:, 0:n], bank.ap[:, 0:n], 1.0 / width, EPS, MUL, ADD),
                   last, *r.busy)
            banks.give(bank, m)
            g = work.take()
            v, g_ = r.ap[:, 0:n], g.ap[:, 0:n]
            m = AC(lambda e: e.activation(g_, v, ACT.Ln), m, *g.busy)
            m = AC(lambda e: e.activation(g_, g_, ACT.Exp, scale=-0.5), m)
            m = VE(lambda e: e.scalar_tensor_tensor(out=v, in0=v, scalar=-0.5, in1=g_, op0=MUL, op1=MUL), m)
            m = VE(lambda e: e.tensor_tensor(v, v, g_, MUL), m)
            m = VE(lambda e: e.scalar_tensor_tensor(out=v, in0=v, scalar=1.5, in1=g_, op0=ADD, op1=MUL), m)
            work.give(g, m)
            return r, m

        x_ready = [(loaded,) for _ in range(DT)]

        def norm_to(dst, tiles, gains, width, n=T, c0=0, shifts=None, need=()):
            r, m_r = inverse_rms(tiles, width, n)
            readers, held = [], None
            for k, (ap, marks) in enumerate(tiles):
                t = work.take()
                m = VE(lambda e: e.scalar_tensor_tensor(out=t.ap[:, 0:n], in0=ap, scalar=gains(k),
                                                        in1=r.ap[:, 0:n], op0=MUL, op1=MUL),
                       m_r, loaded, *need, *marks, *t.busy)
                readers.append(m)
                if shifts is not None:
                    m = VE(lambda e: e.tensor_scalar(t.ap[:, 0:n], t.ap[:, 0:n], shifts(k), None, ADD), m)
                dst.ready[k] = () if c0 == 0 else dst.ready[k]
                m_hi = split_hi(dst, k, t.ap[:, 0:n], (m,), n, c0)
                if held is not None:
                    work.give(held[2], *split_lo(dst, held[0], held[1], held[3], held[4], n, c0))
                held = (k, t.ap[:, 0:n], t, (m,), m_hi)
            work.give(held[2], *split_lo(dst, held[0], held[1], held[3], held[4], n, c0))
            work.give(r, readers[-1])
            return readers

        def x_tiles():
            return [(x[:, k, :], x_ready[k]) for k in range(DT)]

        def add_to_x(k, bank, mark, scale=None):
            if scale is None:
                m = VE(lambda e: e.tensor_tensor(x[:, k, :], x[:, k, :], bank.ap, ADD), mark, *x_ready[k])
            else:
                m = VE(lambda e: e.scalar_tensor_tensor(out=x[:, k, :], in0=bank.ap, scalar=scale(k), in1=x[:, k, :],
                                                        op0=MUL, op1=ADD), mark, *x_ready[k])
            x_ready[k] = (m,)
            banks.give(bank, m)

        left = []

        def leave():
            left[:] = [e.last() for e in (PE, VE, AC, PO) if e.count]

        def enter():
            for e in (PE, VE, AC, PO, SP):
                e.wait(*left)

        def barrier():
            leave()
            enter()

        def begin_u():
            U.busy = U.read
            U.ready = [()] * DT

        for e in (PE, VE, AC, PO):
            e.wait(loaded)
        levels_scope.close()
        barrier()

        def hgrn2():
            with ExitStack() as c:
                def s(name, shape, dt=F32):
                    return sb("gla_" + name, shape, dt, c)

                o = s("o", [P, DT, T])
                o_ready = [None] * DT
                lbe = s("lbe", [P, 3, DT])
                lbs = s("lbs", [P, 4, DT])
                reset = s("reset", [P, T])
                v = [Buf(s(f"v{i}", [P, NT, 256])) for i in range(2)]
                names = ("q", "kf", "kb", "lf", "lb", "gs")
                per_head = [{n: s(f"{n}{i}", [P, T]) for n in names} for i in range(2)]
                head_busy, gs_busy = [(), ()], [(), ()]
                ex = [Buf(s(f"ex{i}", [P, 2, T])) for i in range(3)]
                hand = [Buf(s(f"hand{i}", [P, 2, T])) for i in range(2)]
                A = s("att", [P, T])
                k1t = s("k1t", [P, T])
                states = s("states", [P, 2, 3, P])
                e_tot = s("e_tot", [P, 2, NT])
                a_busy = [()]
                k1t_busy = [()]
                states_busy = [()]

                lg = column("lb", 0, 24).rearrange("p (r k) -> p r k", r=3)
                m = VE(lambda e: e.tensor_tensor(lbs[:, 0, :], lg[:, 0, :], lg[:, 1, :], MAX), loaded)
                m = VE(lambda e: e.tensor_tensor(lbs[:, 0, :], lbs[:, 0, :], lg[:, 2, :], MAX), m)
                for i in range(3):
                    last = VE(lambda e: e.tensor_tensor(lbe[:, i, :], lg[:, i, :], lbs[:, 0, :], SUB), m)
                m = AC(lambda e: e.activation(lbe[:, :, :], lbe[:, :, :], ACT.Exp), last)
                m = VE(lambda e: e.tensor_tensor(lbs[:, 1, :], lbe[:, 0, :], lbe[:, 1, :], ADD), m)
                m = VE(lambda e: e.tensor_tensor(lbs[:, 1, :], lbs[:, 1, :], lbe[:, 2, :], ADD), m)
                m = VE(lambda e: e.reciprocal(lbs[:, 1, :], lbs[:, 1, :]), m)
                m = VE(lambda e: e.tensor_tensor(lbs[:, 2, :], lbe[:, 0, :], lbs[:, 1, :], MUL), m)
                m_lb = VE(lambda e: e.tensor_scalar(lbs[:, 3, :], lbs[:, 2, :], -1.0, 1.0, MUL, ADD), m)
                m = VE(lambda e: e.memset(reset[:, :], 1.0))
                for i in range(NT):
                    m_reset = VE(lambda e: e.memset(reset[:, i * P:i * P + 1], 0.0), m)

                for i in range(LEAD + 1):
                    split(i)
                begin_u()
                norm_to(U, x_tiles(), lambda k: column("norm1", k), D)
                kept = {}

                def project(h):
                    b = per_head[h % 2]
                    vb = v[h // 2 % 2]
                    if h % 2 == 0:
                        w = use(("gla_v", h))
                        marks = []
                        for t in range(0, NT, 2):
                            two = [token_tile(w, 0, 256, U, (t + i) * P) for i in range(2)]
                            if t == NT - 2:
                                used(w, two[1][1])
                            yield
                            for i, (bank, m) in enumerate(two):
                                marks.append(AC(lambda e: e.activation(vb.ap[:, t + i, :], bank.ap[:, 0:256],
                                                                       ACT.Copy), m, *vb.busy))
                                banks.give(bank, marks[-1])
                        kept["v", h // 2] = marks
                    def swish(bank, m, dst, busy):
                        m1 = AC(lambda e: e.activation(dst, bank.ap, ACT.Sigmoid), m, *busy)
                        m2 = VE(lambda e: e.tensor_tensor(dst, bank.ap, dst, MUL), m1)
                        banks.give(bank, m2)
                        return m2

                    def gate(bank, m, k_dst, l_dst):
                        m1 = AC(lambda e: e.activation(l_dst, bank.ap, ACT.Sigmoid), m, *head_busy[h % 2])
                        banks.give(bank, m1)
                        m2 = VE(lambda e: e.tensor_scalar(l_dst, l_dst, lbs[:, 3, h:h + 1], lbs[:, 2, h:h + 1],
                                                          MUL, ADD), m1, m_lb)
                        return VE(lambda e: e.tensor_scalar(k_dst, l_dst, -1.0, 1.0, MUL, ADD), m2)

                    w = use(("gla_qf", h))
                    bank, m = feature_tile(w, 0, U)
                    yield
                    held = bank, m
                    bank, m = feature_tile(w, P, U)
                    used(w, m)
                    kept["q", h] = swish(*held, b["q"][:, :], head_busy[h % 2])
                    yield
                    held = bank, m
                    w = use(("gla_bg", h))
                    bank, m = feature_tile(w, 0, U)
                    g1 = gate(*held, b["kf"][:, :], b["lf"][:, :])
                    yield
                    held = bank, m
                    bank, m = feature_tile(w, P, U)
                    used(w, m)
                    g2 = gate(*held, b["kb"][:, :], b["lb"][:, :])
                    yield
                    kept["gs", h] = swish(bank, m, b["gs"][:, :], gs_busy[h % 2])
                    for name, ap, m3 in (("lf", b["lf"][:, :], g1), ("lb", b["lb"][:, :], g2)):
                        kept[name, h] = AC(lambda e: e.activation(ap, ap, ACT.Ln), m3)
                    kept["k", h] = g2
                    yield

                def attend(h):
                    b = per_head[h % 2]
                    q, kf, kb, lf, lbw, gs = (b[n][:, :] for n in names)
                    vv = v[h // 2 % 2].ap[:, :, (h % 2) * P:(h % 2) * P + P]
                    cf_, cb_ = b["lf"], b["lb"]
                    mf = VE(lambda e: e.tensor_tensor_scan(cf_[:, :], reset[:, :], lf, 0.0, MUL, ADD),
                            kept["lf", h], m_reset)
                    mb = VE(lambda e: e.tensor_tensor_scan(cb_[:, ::-1], reset[:, :], lbw[:, ::-1], 0.0, MUL, ADD),
                            kept["lb", h])
                    f4 = cf_[:, :].rearrange("p (c t) -> p c t", c=NT)
                    b4 = cb_[:, :].rearrange("p (c t) -> p c t", c=NT)
                    f_end, b_end = f4[:, :, P - 1:P], b4[:, :, 0:1]
                    m_et = AC(lambda e: e.activation(e_tot[:, 0, :], f_end.rearrange("p c t -> p (c t)"), ACT.Exp),
                              mf, *states_busy[0])
                    m_et = AC(lambda e: e.activation(e_tot[:, 1, :], b_end.rearrange("p c t -> p (c t)"), ACT.Exp), mb)
                    q_ready, k_ready = kept["q", h], kept["k", h]

                    e0 = ex[2]
                    m = VE(lambda e: e.tensor_tensor(e0.ap[:, 0, :], kf, kb, ADD), k_ready, *e0.busy)
                    yield
                    bank = banks.take()
                    PE.wait(*bank.busy, q_ready)
                    for c_ in range(NT):
                        sl = slice(c_ * P, c_ * P + P)
                        m_pe = PE(lambda e: e.matmul(bank.ap[:, sl], e0.ap[:, 0, sl], q[:, sl], start=True,
                                                     stop=True), m)
                    e0.busy = (m_pe,)
                    m_a = VE(lambda e: e.tensor_copy(A[:, :], bank.ap), m_pe, *a_busy[0])
                    banks.give(bank, m_a)

                    def exponents(lv):
                        half, eb = SUB_LEVELS[lv], ex[lv % 3]
                        E = eb.ap[:, :, :].rearrange("p a (n s h) -> p a n s h", s=2, h=half)
                        fv = cf_[:, :].rearrange("p (n s h) -> p n s h", s=2, h=half)
                        bv = cb_[:, :].rearrange("p (n s h) -> p n s h", s=2, h=half)
                        shape = [P, T // (2 * half), half]
                        fr = fv[:, :, 0, half - 1:half].to_broadcast(shape)
                        br = bv[:, :, 1, 0:1].to_broadcast(shape)
                        VE(lambda e: e.tensor_tensor(E[:, 0, :, 0, :], fr, fv[:, :, 0, :], SUB), mf, mb, *eb.busy)
                        VE(lambda e: e.tensor_tensor(E[:, 0, :, 1, :], br, bv[:, :, 1, :], SUB))
                        VE(lambda e: e.tensor_tensor(E[:, 1, :, 0, :], bv[:, :, 0, :], br, SUB))
                        m = VE(lambda e: e.tensor_tensor(E[:, 1, :, 1, :], fv[:, :, 1, :], fr, SUB))
                        return AC(lambda e: e.activation(eb.ap[:, :, :], eb.ap[:, :, :], ACT.Exp), m)

                    def weighted(lv, m):
                        half, eb = SUB_LEVELS[lv], ex[lv % 3]
                        E = eb.ap[:, :, :].rearrange("p a (n s h) -> p a n s h", s=2, h=half)
                        kfv = kf.rearrange("p (n s h) -> p n s h", s=2, h=half)
                        kbv = kb.rearrange("p (n s h) -> p n s h", s=2, h=half)
                        VE(lambda e: e.tensor_tensor(E[:, 0, :, 0, :], E[:, 0, :, 0, :], kfv[:, :, 0, :], MUL), m)
                        m1 = VE(lambda e: e.tensor_tensor(E[:, 0, :, 1, :], E[:, 0, :, 1, :], kbv[:, :, 1, :], MUL))
                        m2 = PO(lambda e: e.tensor_tensor(eb.ap[:, 1, :], eb.ap[:, 1, :], q, MUL), m, q_ready)
                        return m1, m2

                    def scores(lv, m1, m2):
                        eb = ex[lv % 3]
                        bank = banks.take()
                        PE.wait(*bank.busy, m1, m2)
                        for c_ in range(NT):
                            sl = slice(c_ * P, c_ * P + P)
                            m_pe = PE(lambda e: e.matmul(bank.ap[:, sl], eb.ap[:, 0, sl], eb.ap[:, 1, sl],
                                                         start=True, stop=True))
                        eb.busy = (m_pe,)
                        return bank, m_pe

                    def placed(lv, bank, m_pe, m_a):
                        m_a = VE(lambda e: e.copy_predicated(
                            A[:, :].rearrange("p (c t) -> p c t", c=NT),
                            levels[:, lv:lv + 1, :].to_broadcast([P, NT, P]),
                            bank.ap.rearrange("p (c t) -> p c t", c=NT)), m_pe, m_a)
                        banks.give(bank, m_a)
                        return m_a

                    sides = ((kf, cf_, f4, f_end, (0, 1, 2)), (kb, cb_, b4, b_end, (3, 2, 1)))
                    m_k, m_q, m_kt, parts = [None] * 2, [None] * 2, [None] * 2, [None] * 2

                    def handed_on(d):
                        (k_, cum, cum4, end, _), eb = sides[d], hand[d]
                        e4 = eb.ap[:, 0, :].rearrange("p (c t) -> p c t", c=NT)
                        m = VE(lambda e: e.tensor_tensor(e4, end.to_broadcast([P, NT, P]), cum4, SUB), *eb.busy)
                        m = AC(lambda e: e.activation(eb.ap[:, 0, :], eb.ap[:, 0, :], ACT.Exp), m)
                        m_k[d] = PO(lambda e: e.tensor_tensor(eb.ap[:, 0, :], eb.ap[:, 0, :], k_, MUL), m)
                        m = AC(lambda e: e.activation(eb.ap[:, 1, :], cum[:, :], ACT.Exp), mf, mb, *eb.busy)
                        m_q[d] = PO(lambda e: e.tensor_tensor(eb.ap[:, 1, :], eb.ap[:, 1, :], q, MUL), m)

                    def turned(d):
                        bank = banks.take()
                        PE.wait(*bank.busy, m_k[d])
                        for i, c_ in enumerate(sides[d][4]):
                            m = PE(lambda e: e.transpose(bank.ap[:, i * P:i * P + P],
                                                         hand[d].ap[:, 0, c_ * P:c_ * P + P], ident))
                        m_kt[d] = AC(lambda e: e.activation(k1t[:, 0:3 * P], bank.ap[:, 0:3 * P], ACT.Copy), m,
                                     *k1t_busy[0])
                        banks.give(bank, m_kt[d])

                    def state(d):
                        which = sides[d][4]
                        bank = banks.take()
                        PE.wait(*bank.busy, m_kt[d], *kept["v", h // 2])
                        for i, c_ in enumerate(which):
                            m = PE(lambda e: e.matmul(bank.ap[:, i * P:i * P + P], k1t[:, i * P:i * P + P],
                                                      vv[:, c_, :], start=True, stop=True))
                        k1t_busy[0] = (m,)
                        m = VE(lambda e: e.tensor_copy(states[:, d, 0, :], bank.ap[:, 0:P]), m, *states_busy[0])
                        for i in (1, 2):
                            m = VE(lambda e: e.scalar_tensor_tensor(
                                out=states[:, d, i, :], in0=states[:, d, i - 1, :],
                                scalar=e_tot[:, d, which[i]:which[i] + 1], in1=bank.ap[:, i * P:i * P + P],
                                op0=MUL, op1=ADD), m, m_et)
                        banks.give(bank, m)
                        parts[d] = (m_q[d], m)

                    n_lv = len(SUB_LEVELS)
                    m_exp, m_in, products = {}, {}, {}
                    for step in range(n_lv + 3):
                        if 0 <= step - 2 < n_lv:
                            products[step - 2] = scores(step - 2, *m_in[step - 2])
                        if 0 <= step - 1 < n_lv:
                            m_in[step - 1] = weighted(step - 1, m_exp[step - 1])
                        if step < n_lv:
                            m_exp[step] = exponents(step)
                        if step >= 3:
                            m_a = placed(step - 3, *products[step - 3], m_a)
                        for job, d in HAND.get(step, ()):
                            {"hand": handed_on, "turn": turned, "state": state}[job](d)
                        yield
                    o_bank = banks.take()
                    PE.wait(*o_bank.busy, m_a, *parts[0], *parts[1])
                    for c_ in range(NT):
                        sl = slice(c_ * P, c_ * P + P)
                        pairs = [(vv[:, c_, :], A[:, sl])]
                        if c_ > 0:
                            pairs.append((states[:, 0, c_ - 1, :], hand[0].ap[:, 1, sl]))
                        if c_ < NT - 1:
                            pairs.append((states[:, 1, NT - 2 - c_, :], hand[1].ap[:, 1, sl]))
                        m_o = fmm(o_bank.ap[:, sl], pairs)
                    a_busy[0] = states_busy[0] = (m_o,)
                    hand[0].busy = hand[1].busy = (m_o,)
                    if h % 2 == 1:
                        v[h // 2 % 2].busy = (m_o,)
                    kept["o", h] = o_bank, m_o
                    head_busy[h % 2] = (VE.last(), AC.last(), PO.last(), m_o)
                    yield

                def finish(h):
                    o_bank, m_o = kept["o", h]
                    gs = per_head[h % 2]["gs"][:, :]
                    r, m_r = inverse_rms([(o_bank.ap, (m_o,))], P)
                    t = work.take()
                    m = VE(lambda e: e.scalar_tensor_tensor(out=t.ap, in0=o_bank.ap, scalar=column("a_norm", 0),
                                                            in1=r.ap, op0=MUL, op1=MUL), m_r, m_o, *t.busy)
                    banks.give(o_bank, m)
                    work.give(r, m)
                    m = VE(lambda e: e.tensor_tensor(o[:, h, :], t.ap, gs, MUL), m, kept["gs", h])
                    work.give(t, m)
                    o_ready[h] = m
                    gs_busy[h % 2] = (m,)
                    yield

                run(project(0))
                for h in range(1, HG_HEADS + 1):
                    in_order(GLA_ORDER[h % 2], a=attend(h - 1), p=project(h) if h < HG_HEADS else iter(()),
                             f=finish(h - 2) if h > 1 else iter(()))
                run(finish(HG_HEADS - 1))
                begin_u()
                for h in range(HG_HEADS):
                    split_to(U, h, o[:, h, :], (o_ready[h],))
                for c0 in range(0, D, 256):
                    w = use(("gla_out", c0))
                    for j in range(2):
                        bank, m = feature_tile(w, j * P, U)
                        add_to_x(c0 // P + j, bank, m)
                    used(w, m)
                leave()

        s_mod = [sem(f"mod{i}_filled") for i in range(N_MOD)]

        def mod_begin(c):
            mod_slot.w = sb("mod_w", [P, N_MOD, SLOT], F32, c)
            mod_slot.busy = [()] * N_MOD
            for i in range(N_MOD - 1):
                mod_load(i)

        def mod_load(i):
            if i < MOD_SLOTS:
                SP.wait(*mod_slot.busy[i % N_MOD])
                nc.sync.dma_start(mod_slot.w[:, i % N_MOD, :], ins["mod_weights"][i]).then_inc(s_mod[i % N_MOD], 16)

        def mod_slot():
            n = mod_slot.next
            mod_slot.next += 1
            mod_load(n + N_MOD - 1)
            w = mod_slot.w[:, n % N_MOD, :].rearrange("p (k c) -> p k c", k=DT)
            users = 2 if 2 * n < 2 * DT else 1
            t = work.take()
            sums = t.ap.rearrange("p (o c) -> p o c", o=2)
            for o in range(users):
                m = VE(lambda e: e.tensor_scalar(sums[:, o, :], w[:, 0, :], mod_slot.c[:, 0, o:o + 1], None, MUL),
                       (s_mod[n % N_MOD], 16 * (n // N_MOD + 1)), mod_slot.ready, *t.busy)
                for k in range(1, DT):
                    m = VE(lambda e: e.scalar_tensor_tensor(out=sums[:, o, :], in0=w[:, k, :],
                                                            scalar=mod_slot.c[:, k, o:o + 1], in1=sums[:, o, :],
                                                            op0=MUL, op1=ADD), m)
            mod_slot.busy[n % N_MOD] = (m,)
            mod_slot.summed = (n, t, sums, users, m)

        def mod_finish():
            n, t, sums, users, m = mod_slot.summed
            bank = banks.take()
            PE.wait(*bank.busy, m)
            for j in range(2):
                for o in range(users):
                    m = PE(lambda e: e.matmul(bank.ap[:, users * j + o:users * j + o + 1],
                                              sums[:, o, j * P:(j + 1) * P], ones[:, 0:1], start=True, stop=True))
            work.give(t, m)
            bias = column("b_mod", 2 * n, 2).rearrange("p (j o) -> p j o", o=1).to_broadcast([P, 2, users])
            m = VE(lambda e: e.tensor_tensor(modv[:, 2 * n:2 * n + 2, 0:users], bank.ap[:, 0:2 * users].rearrange(
                "p (j o) -> p j o", j=2), bias, ADD), m, loaded)
            banks.give(bank, m)
            mod_slot.done = m
        mod_slot.next = 0

        silu_c = sb("silu_c", [P, DT, 2])
        m = AC(lambda e: e.activation(silu_c[:, :, :], column("c_c", 0, 16).rearrange(
            "p (k o) -> p k o", k=DT), ACT.Silu), loaded)
        mod_slot.ready, mod_slot.c = m, silu_c

        def mlp(tag, n_tiles, per_slot, hidden, extra=0, scale=None):
            enter()
            with ExitStack() as c:
                bufs = [Split(sb(f"{tag}_h_hi{i}", [P, 4, T], F32R, c), sb(f"{tag}_h_lo{i}", [P, 4, T], F32R, c), 4)
                        for i in range(2)]
                mod = extra > 0
                if mod:
                    mod_begin(c)
                parts = chunks_of(n_tiles, 4)
                for i in range(len(parts) + 1):
                    if i < len(parts):
                        H = bufs[i % 2]
                        H.ready = [()] * 4
                        t0, n = parts[i]
                        for t in range(t0, t0 + n, per_slot):
                            w = use((tag, t))
                            for j in range(per_slot):
                                m = hidden(w, j, t + j, H, t + j - t0)
                            used(w, m)
                            if extra:
                                extra -= 1
                                if mod_slot.next:
                                    mod_finish()
                                mod_slot()
                    if i > 0:
                        H = bufs[(i - 1) % 2]
                        t0, n = parts[i - 1]
                        width = SLOT // n
                        for c0 in range(0, D, width):
                            w = use((tag + "_out", t0, c0))
                            for j in range(width // P):
                                bank, m = feature_tile(w, j * P, H)
                                add_to_x(c0 // P + j, bank, m, scale)
                            used(w, m)
                        H.busy = (m,)
                if mod:
                    while extra:
                        extra -= 1
                        mod_finish()
                        mod_slot()
                    mod_finish()
                leave()

        def conv_glu(layer):
            tag = f"ffn{layer}"

            def hidden(w, j, t, H, slot):
                gate, mg = feature_tile(w, 0, U)
                val, mv = feature_tile(w, P, U)
                tap = [column("ffn_cw", (layer * 3 + i) * FF_TILES + t) for i in range(3)]
                a = work.take()
                m = VE(lambda e: e.tensor_scalar(a.ap, gate.ap, tap[1], column("ffn_cb", layer * FF_TILES + t),
                                                 MUL, ADD), mg, *a.busy)
                m = VE(lambda e: e.scalar_tensor_tensor(out=a.ap[:, 1:T], in0=gate.ap[:, 0:T - 1], scalar=tap[0],
                                                        in1=a.ap[:, 1:T], op0=MUL, op1=ADD), m)
                m = VE(lambda e: e.scalar_tensor_tensor(out=a.ap[:, 0:T - 1], in0=gate.ap[:, 1:T], scalar=tap[2],
                                                        in1=a.ap[:, 0:T - 1], op0=MUL, op1=ADD), m)
                banks.give(gate, m)
                m = AC(lambda e: e.activation(a.ap, a.ap, ACT.Silu), m)
                m = VE(lambda e: e.tensor_tensor(a.ap, a.ap, val.ap, MUL), m, mv)
                banks.give(val, m)
                work.give(a, *split_to(H, slot, a.ap, (m,), on=VE))
                return mv

            begin_u()
            norm_to(U, x_tiles(), lambda k: column("norm2", layer * DT + k), D)
            mlp(tag, FF_TILES, 1, hidden, extra=MOD_SLOTS if layer == 0 else 0)

        def scope(**k):
            return k

        shared = scope(nc=nc, sb=sb, PE=PE, VE=VE, AC=AC, PO=PO, SP=SP, banks=banks, work=work, x=x, U=U,
                       column=column, use=use, used=used, feature_tile=feature_tile, token_tile=token_tile,
                       fmm=fmm, inverse_rms=inverse_rms, norm_to=norm_to, x_tiles=x_tiles, add_to_x=add_to_x,
                       barrier=barrier, leave=leave, enter=enter, begin_u=begin_u, Split=Split,
                       split_to=split_to, ident=ident, ones=ones,
                       m_le=m_le, m_ge=m_ge, m_lt=m_lt, m_gt=m_gt, rotate=rotate, turn=turn, levels=levels, modv=modv,
                       mod_slot=mod_slot, mlp=mlp, ins=ins, s_io=s_io, loaded=loaded, x_ready=x_ready, sem=sem,
                       product=product)
        stop = "all" if debug is None else debug.get("stop", "all")
        def phases():
            hgrn2()
            yield "gla"
            conv_glu(0)
            yield "ffn0"
            mamba2(shared)
            yield "mamba"
            conv_glu(1)
            final_to_x(shared, "final")
            yield "b1"
            block2(shared)
            yield "b2"
            block3(shared)
            yield "all"
        if debug is not None and debug.get("mods"):
            with ExitStack() as c:
                mod_begin(c)
                for _ in range(MOD_SLOTS):
                    mod_slot()
                    mod_finish()
                barrier()
        if debug is not None and "only" in debug:
            {"b2": lambda: block2(shared), "b3": lambda: block3(shared), "mamba": lambda: mamba2(shared)}[debug["only"]]()
        else:
            for name in phases():
                if name == stop:
                    break
        SP.wait(*[m for k in range(DT) for m in x_ready[k]])
        s_out = sem("result_stored")
        nc.sync.dma_start(out.rearrange("(k p) t -> p k t", p=P), x[:, :, :]).then_inc(s_out, 16)
        nc.sync.wait_ge(s_out, 16)


def final_to_x(sh, gain):
    VE, work, x, x_ready = sh["VE"], sh["work"], sh["x"], sh["x_ready"]
    r, m_r = sh["inverse_rms"](sh["x_tiles"](), D)
    for k in range(DT):
        m = VE(lambda e: e.scalar_tensor_tensor(out=x[:, k, :], in0=x[:, k, :], scalar=sh["column"](gain, k),
                                                in1=r.ap, op0=MUL, op1=MUL), m_r, *x_ready[k])
        x_ready[k] = (m,)
    work.give(r, m)



ORDER = "spspspspp" + "sp" * 8

ATANH = [1.0 / (2 * k + 1) for k in range(9)]


def mamba2(sh):
    nc, PE, VE, AC, PO = sh["nc"], sh["PE"], sh["VE"], sh["AC"], sh["PO"]
    banks, work, column, use, used = sh["banks"], sh["work"], sh["column"], sh["use"], sh["used"]
    feature_tile, fmm, ident, levels, U = sh["feature_tile"], sh["fmm"], sh["ident"], sh["levels"], sh["U"]
    with ExitStack() as c:
        def s(name, shape, dt=F32):
            return sh["sb"]("m_" + name, shape, dt, c)

        acum = s("acum", [N_DT, T])
        neg_a = s("neg_a", [N_DT, 1])
        tok = s("tok", [P, 3, NT, N_DT])
        dt_tok, ac_tok, dec_tok = (tok[:, i, :, :] for i in range(3))
        e_last = s("e_last", [P, NT, N_DT])
        side = [{"x": s(f"xs{i}", [P, 2, T]), "B": s(f"B{i}", [P, T]), "C": s(f"C{i}", [P, T])} for i in range(2)]
        side_busy = [(), ()]
        z = s("z", [P, 2, T])
        z_busy = [()]
        x_tok, b_tok = s("x_tok", [P, NT, 256]), s("b_tok", [P, NT, P])
        xd = [s("xd_f", [P, NT, 256]), s("xd_b", [P, NT, 256])]
        cbs = [s("cb_f", [P, T]), s("cb_b", [P, T])]
        H = s("H", [P, 2, 3, 256])
        pair = [(Buf(s(f"E{i}", [P, T])[:, :]), Buf(s(f"W{i}", [P, T])[:, :])) for i in range(2)]
        decayed = [Buf(s(f"decayed{i}", [P, 2, T])[:, :, :]) for i in range(3)]
        s_sums = [sh["sem"](f"m_sums{i}_loaded") for i in range(3)]
        Y = sh["Split"](s("y_hi", [P, 2, T], F32R), s("y_lo", [P, 2, T], F32R), 2)
        group_busy = [()]

        sh["begin_u"]()
        sh["norm_to"](U, sh["x_tiles"](), lambda k: column("norm1", DT + k), D)
        sh["enter"]()

        kept = {}

        def conv(bank, m, tile, dst, busy):
            tap = [column("conv_w", i * 32 + tile) for i in range(5)]
            m = VE(lambda v: v.tensor_scalar(dst, bank.ap, tap[2], column("conv_b", tile), MUL, ADD), m, *busy)
            for i in (0, 1, 3, 4):
                o = i - 2
                a, b = max(0, -o), T - max(0, o)
                m = VE(lambda v: v.scalar_tensor_tensor(out=dst[:, a:b], in0=bank.ap[:, a + o:b + o], scalar=tap[i],
                                                        in1=dst[:, a:b], op0=MUL, op1=ADD), m)
            banks.give(bank, m)
            return AC(lambda v: v.activation(dst, dst, ACT.Silu), m)

        def project(g):
            sd, busy = side[g % 2], side_busy[g % 2]
            todo = [(("m_x", g), 0, 2 * g, sd["x"][:, 0, :]), (("m_x", g), P, 2 * g + 1, sd["x"][:, 1, :]),
                    (("m_bc", g), 0, 16 + g, sd["B"][:, :]), (("m_bc", g), P, 24 + g, sd["C"][:, :])]
            marks, held = [], None
            for key, c0, tile, dst in todo:
                w = w if c0 else use(key)
                bank, m = feature_tile(w, c0, U)
                if c0:
                    used(w, m)
                if held:
                    marks.append(conv(*held, busy))
                held = (bank, m, tile, dst)
                yield
            marks.append(conv(*held, busy))
            kept["x", g], kept["B", g], kept["C", g] = tuple(marks[0:2]), marks[2], marks[3]
            yield

        w = use(("m_dt",))
        bank, m = feature_tile(w, 0, U, width=N_DT)
        used(w, m)
        first = project(0)
        next(first)
        zb, nb, rb = work.take(), work.take(), work.take()
        zz, e, r = zb.ap[0:N_DT, :], nb.ap[0:N_DT, :], rb.ap[0:N_DT, :]
        m = VE(lambda v: v.tensor_scalar(zz, bank.ap[0:N_DT, :], column("dt_bias", 0)[0:N_DT, :], None, ADD), m,
               *zb.busy)
        banks.give(bank, m)
        m = VE(lambda v: v.tensor_scalar(e, zz, -1.0, None, MUL), m, *nb.busy)
        m = VE(lambda v: v.tensor_tensor(e, e, zz, MIN), m)
        m = AC(lambda v: v.activation(e, e, ACT.Exp), m)
        next(first)
        m = VE(lambda v: v.tensor_scalar(r, e, 2.0, None, ADD), m, *rb.busy)
        m = VE(lambda v: v.reciprocal(r, r), m)
        m = VE(lambda v: v.tensor_tensor(r, r, e, MUL), m)
        m = VE(lambda v: v.tensor_tensor(e, r, r, MUL), m)
        qb = work.take()
        q = qb.ap[0:N_DT, :]
        m = VE(lambda v: v.tensor_scalar(q, e, ATANH[-1], None, MUL), m, *qb.busy)
        for coef in ATANH[-2:0:-1]:
            m = VE(lambda v: v.scalar_tensor_tensor(out=q, in0=q, scalar=coef, in1=e, op0=ADD, op1=MUL), m)
        m = VE(lambda v: v.scalar_tensor_tensor(out=q, in0=q, scalar=1.0, in1=r, op0=ADD, op1=MUL), m)
        m = VE(lambda v: v.tensor_scalar(q, q, 2.0, None, MUL), m)
        m_dt = VE(lambda v: v.scalar_tensor_tensor(out=zz, in0=zz, scalar=0.0, in1=q, op0=MAX, op1=ADD), m)
        m = AC(lambda v: v.activation(neg_a[:, :], column("a_log", 0)[0:N_DT, :], ACT.Exp))
        m = VE(lambda v: v.tensor_scalar(neg_a[:, :], neg_a[:, :], -1.0, None, MUL), m)
        m_la = VE(lambda v: v.tensor_scalar(e, zz, neg_a[:, 0:1], None, MUL), m, m_dt)
        m = VE(lambda v: v.memset(r, 1.0), m_dt)
        for i in range(NT):
            m = VE(lambda v: v.memset(r[:, i * P:i * P + 1], 0.0), m)
        VE(lambda v: v.tensor_tensor_scan(acum[0:32, :], r[0:32, :], e[0:32, :], 0.0, MUL, ADD), m, m_la)
        m_ac = VE(lambda v: v.tensor_tensor_scan(acum[32:64, ::-1], r[32:64, :], e[32:64, ::-1], 0.0, MUL, ADD), m)
        next(first)
        a4 = acum[:, :].rearrange("p (c t) -> p c t", c=NT)
        d4 = q.rearrange("p (c t) -> p c t", c=NT)
        ends = ((slice(0, 32), a4[0:32, :, P - 1:P]), (slice(32, 64), a4[32:64, :, 0:1]))
        for rows, end in ends:
            m = VE(lambda v: v.tensor_tensor(d4[rows], end.to_broadcast([32, NT, P]), a4[rows], SUB), m_ac)
        m = AC(lambda v: v.activation(q, q, ACT.Exp), m)
        m = VE(lambda v: v.tensor_tensor(q, q, zz, MUL), m)
        next(first)
        bank, bank2 = banks.take(), banks.take()
        PE.wait(*bank.busy, *bank2.busy, m, m_dt, m_ac)
        for i, (src, to) in enumerate(((zz, bank.ap[:, 0:256]), (acum[:, :], bank.ap[:, 256:512]), (q, bank2.ap))):
            for k in range(NT):
                m = PE(lambda v: v.transpose(to[:, k * N_DT:(k + 1) * N_DT], src[:, k * P:(k + 1) * P],
                                             ident[0:N_DT, 0:N_DT]))
        last = s("last", [N_DT, NT])
        for rows, end in ends:
            m_l = VE(lambda v: v.tensor_copy(last[rows, :], end.rearrange("p c t -> p (c t)")), m_ac)
        PE.wait(m_l)
        for k in range(NT):
            m = PE(lambda v: v.matmul(bank2.ap[:, 256 + k * N_DT:256 + (k + 1) * N_DT],
                                      last[:, k:k + 1].to_broadcast([N_DT, P]), ident[0:N_DT, 0:N_DT],
                                      start=True, stop=True))
        m1 = VE(lambda v: v.tensor_copy(tok[:, 0:2, :, :].rearrange("p a c j -> p (a c j)"), bank.ap), m)
        banks.give(bank, m1)
        m2 = VE(lambda v: v.tensor_copy(tok[:, 2, :, :].rearrange("p c j -> p (c j)"), bank2.ap[:, 0:256]), m)
        m3 = AC(lambda v: v.activation(e_last[:, :, :].rearrange("p c j -> p (c j)"), bank2.ap[:, 256:512], ACT.Exp), m2)
        banks.give(bank2, m2, m3)
        for b in (zb, nb, rb, qb):
            work.give(b, m, m2, m3)
        setup = (m1, m2, m3)

        SP, s_w, heads_all = sh["SP"], sh["sem"]("m_sums_stored"), GROUPS * HEADS_PER_GROUP
        rows_dram = nc.dram_tensor("running_sums", (N_DT, T), F32, kind="Internal").ap()
        SP.wait(m_ac)
        nc.sync.dma_start(rows_dram, acum[:, :]).then_inc(s_w, 16)
        nc.sync.wait_ge(s_w, 16)
        by_direction = rows_dram.rearrange("(d h) t -> h d t", d=2)

        def load_sums(n):
            if n < heads_all:
                SP.wait(*decayed[n % 3].busy)
                nc.sync.dma_start(decayed[n % 3].ap, by_direction[n:n + 1].to_broadcast([P, 2, T])).then_inc(
                    s_sums[n % 3], 16)

        def sums_loaded(n):
            return (s_sums[n % 3], 16 * (n // 3 + 1))

        load_sums(0)
        load_sums(1)
        load_sums(2)

        def ssd(g):
            sd = side[g % 2]
            xs, B, C = sd["x"], sd["B"], sd["C"]
            row = (4 * g, 32 + 4 * g)
            for j in range(3):
                bank = banks.take()
                src = xs[:, j, :] if j < 2 else B[:, :]
                PE.wait(*bank.busy, kept["x", g][j] if j < 2 else kept["B", g])
                for k in range(NT):
                    m = PE(lambda v: v.transpose(bank.ap[:, k * P:(k + 1) * P], src[:, k * P:(k + 1) * P], ident))
                dst = x_tok[:, :, j * P:(j + 1) * P] if j < 2 else b_tok[:, :, :]
                m = (AC if j else VE)(lambda v: (v.activation(dst, bank.ap.rearrange("p (c t) -> p c t", c=NT), ACT.Copy)
                                                 if j else
                                                 v.tensor_copy(dst, bank.ap.rearrange("p (c t) -> p c t", c=NT))),
                                      m, *group_busy[0])
                banks.give(bank, m)
                if j == 0:
                    m_x0 = m
                elif j == 1:
                    m_x1 = m
                else:
                    m_bt = m
            bank = banks.take()
            PE.wait(*bank.busy, kept["B", g], kept["C", g])
            for k in range(NT):
                sl = slice(k * P, (k + 1) * P)
                m = PE(lambda v: v.matmul(bank.ap[:, sl], B[:, sl], C[:, sl], start=True, stop=True))
            m_cb = []
            for d, mask in enumerate((sh["m_le"], sh["m_ge"])):
                m_cb.append(VE(lambda v: v.tensor_tensor(
                    cbs[d][:, :].rearrange("p (c t) -> p c t", c=NT), bank.ap.rearrange("p (c t) -> p c t", c=NT),
                    mask.rearrange("p (o t) -> p o t", o=1).to_broadcast([P, NT, P]), MUL), m, *group_busy[0]))
            banks.give(bank, m_cb[1])
            yield

            def by_head(t, d):
                return t[:, :, row[d]:row[d] + 4].rearrange("p c (h o) -> p c h o", o=1).to_broadcast(
                    [P, NT, 4, HEAD_P])

            def heads(t):
                return t.rearrange("p c (h q) -> p c h q", h=4)

            y_banks = []

            def column_of(j, d):
                return ac_tok[:, :, row[d] + j:row[d] + j + 1].to_broadcast([P, NT, P])

            def chunked(t):
                return t.rearrange("p (c t) -> p c t", c=NT)

            def decays(j):
                n = 4 * g + j
                (E, W), ce = pair[n % 2], decayed[n % 3]
                VE(lambda v: v.tensor_tensor(chunked(E.ap), chunked(ce.ap[:, 0, :]), column_of(j, 0), SUB),
                   sums_loaded(n), *setup, *E.busy)
                m = VE(lambda v: v.tensor_tensor(chunked(W.ap), chunked(ce.ap[:, 1, :]), column_of(j, 1), SUB), *W.busy)
                m2 = VE(lambda v: v.copy_predicated(chunked(E.ap), levels[:, len(SUB_LEVELS):, :].to_broadcast(
                    [P, NT, P]), chunked(W.ap)), m)
                m_e = AC(lambda v: v.activation(ce.ap, ce.ap, ACT.Exp), sums_loaded(n), m)
                m_ce = PO(lambda v: v.tensor_tensor(
                    ce.ap, ce.ap, C[:, :].rearrange("p (o t) -> p o t", o=1).to_broadcast([P, 2, T]), MUL), m_e,
                          kept["C", g])
                return AC(lambda v: v.activation(E.ap, E.ap, ACT.Exp), m2), m_ce

            m_xe = [PO(lambda v: v.tensor_tensor(heads(xd[d][:, :, :]), heads(x_tok[:, :, :]), by_head(dec_tok, d),
                                                 MUL), m_x0, m_x1, *group_busy[0], *setup) for d in range(2)]
            m_xd, m_H = [], []
            for d in range(2):
                which = (0, 1, 2) if d == 0 else (3, 2, 1)
                if d == 1:
                    ahead = decays(0)
                yield
                b1, b2 = banks.take(), banks.take()
                PE.wait(*b1.busy, *b2.busy, m_xe[d], m_bt)
                places = [b1.ap[:, 0:256], b1.ap[:, 256:512], b2.ap[:, 0:256]]
                for i, k in enumerate(which):
                    m = PE(lambda v: v.matmul(places[i], b_tok[:, k, :], xd[d][:, k, :], start=True, stop=True))
                m_st = m
                m = VE(lambda v: v.tensor_copy(H[:, d, 0, :], places[0]), m, *group_busy[0])
                for i in (1, 2):
                    k = which[i]
                    factor = e_last[:, k, row[d]:row[d] + 4].rearrange("p (h o) -> p h o", o=1).to_broadcast(
                        [P, 4, HEAD_P])
                    m = VE(lambda v: v.tensor_tensor(H[:, d, i, :].rearrange("p (h q) -> p h q", h=4),
                                                     H[:, d, i - 1, :].rearrange("p (h q) -> p h q", h=4), factor,
                                                     MUL), m)
                    m = VE(lambda v: v.tensor_tensor(H[:, d, i, :], H[:, d, i, :], places[i], ADD), m)
                banks.give(b1, m)
                banks.give(b2, m)
                m_H.append(m)
                m_xd.append(VE(lambda v: v.tensor_tensor(heads(xd[d][:, :, :]), heads(x_tok[:, :, :]),
                                                         by_head(dt_tok, d), MUL), m_st))

            def weighted(j, m):
                E, W = pair[(4 * g + j) % 2]
                m_w = VE(lambda v: v.tensor_tensor(W.ap, E.ap, cbs[0][:, :], MUL), m, m_cb[0], *W.busy)
                return VE(lambda v: v.tensor_tensor(E.ap, E.ap, cbs[1][:, :], MUL), m_w, m_cb[1])

            def outputs(j, m_w2, m_ce):
                n = 4 * g + j
                (E, W), ce = pair[n % 2], decayed[n % 3]
                if j % 2 == 0:
                    y_banks.append(banks.take())
                    PE.wait(*y_banks[-1].busy)
                rows = slice((j % 2) * HEAD_P, (j % 2) * HEAD_P + HEAD_P)
                hc = slice(j * HEAD_P, (j + 1) * HEAD_P)
                PE.wait(m_w2, *m_xd, m_ce, *m_H)
                for k in range(NT):
                    sl = slice(k * P, (k + 1) * P)
                    pairs = [(xd[0][:, k, hc], W.ap[:, sl]), (xd[1][:, k, hc], E.ap[:, sl])]
                    if k > 0:
                        pairs.append((H[:, 0, k - 1, hc], ce.ap[:, 0, sl]))
                    if k < NT - 1:
                        pairs.append((H[:, 1, NT - 2 - k, hc], ce.ap[:, 1, sl]))
                    m_y = fmm(y_banks[-1].ap[rows, sl], pairs)
                E.busy = W.busy = ce.busy = (m_y,)
                load_sums(n + 3)
                return m_y

            for j in range(HEADS_PER_GROUP):
                m_e, m_ce = ahead
                m_w = weighted(j, m_e)
                if j + 1 < HEADS_PER_GROUP:
                    ahead = decays(j + 1)
                yield
                m_y = outputs(j, m_w, m_ce)
                yield
            kept["y", g] = (y_banks, m_y)
            group_busy[0] = (VE.last(), AC.last(), PO.last(), m_y)
            yield

        def finish(g):
            xs = side[g % 2]["x"]
            y_banks, m_y = kept["y", g]
            y_tiles = []
            for i in range(2):
                m = VE(lambda v: v.scalar_tensor_tensor(out=xs[:, i, :], in0=xs[:, i, :],
                                                        scalar=column("d_skip", 2 * g + i), in1=y_banks[i].ap,
                                                        op0=MUL, op1=ADD), m_y)
                banks.give(y_banks[i], m)
                m = VE(lambda v: v.tensor_tensor(xs[:, i, :], xs[:, i, :], z[:, i, :], MUL), m, kept["z", g][i])
                y_tiles.append((xs[:, i, :], (m,)))
            z_busy[0] = (m,)
            yield
            Y.ready = [(), ()]
            last = sh["norm_to"](Y, y_tiles, lambda k: column("b_norm", 2 * g + k), 256)
            side_busy[g % 2] = (last[-1], m_y, PO.last())

        def project_z(g):
            before = finish(g - 1) if g else iter(())
            next(before, None)
            yield
            w = use(("m_z", g))
            both = [feature_tile(w, 0, U)]
            next(before, None)
            yield
            both.append(feature_tile(w, P, U))
            used(w, both[1][1])
            yield
            kept["z", g] = []
            for j, (bank, m) in enumerate(both):
                kept["z", g].append(AC(lambda v: v.activation(z[:, j, :], bank.ap, ACT.Silu), m, *z_busy[0]))
                banks.give(bank, kept["z", g][-1])

        def out(g):
            w = use(("m_out", g))
            held = []
            for i in range(0, DT, 2):
                two = [(j, *feature_tile(w, j * P, Y)) for j in (i, i + 1)]
                if i == DT - 2:
                    used(w, two[1][2])
                    Y.busy = (two[1][2],)
                for tile in held:
                    sh["add_to_x"](*tile)
                held = two
                yield
            for tile in held:
                sh["add_to_x"](*tile)

        def chain(*gens):
            for g in gens:
                yield from g

        run(first)
        for g in range(GROUPS):
            gens = [project_z(g)]
            if g > 0:
                gens.append(out(g - 1))
            if g + 1 < GROUPS:
                gens.append(project(g + 1))
            in_order(ORDER, s=ssd(g), p=chain(*gens))
        run(finish(GROUPS - 1))
        run(out(GROUPS - 1))
        sh["leave"]()



STICK_ORDER = "ssspspsp" "sp" "ssp" "sss" "sp" "ssp"


def block2(sh):
    nc, PE, VE, AC, PO, SP = (sh[n] for n in ("nc", "PE", "VE", "AC", "PO", "SP"))
    banks, work, column, use, used = sh["banks"], sh["work"], sh["column"], sh["use"], sh["used"]
    feature_tile, token_tile, fmm, ident, U = (sh[n] for n in ("feature_tile", "token_tile", "fmm", "ident", "U"))
    ins, x, x_ready, ones, Split, split_to = (sh[n] for n in ("ins", "x", "x_ready", "ones", "Split", "split_to"))
    SCALE = float(HEAD_P) ** -0.5
    with ExitStack() as outer:
        o = sh["sb"]("b2_o", [P, 8, T], F32, outer)
        o_ready = [None] * 8
        with ExitStack() as c:
            def s(name, shape, dt=F32):
                return sh["sb"]("b2_" + name, shape, dt, c)

            qk = [s(f"qk{i}", [P, 2, T]) for i in range(2)]
            qk_busy = [(), ()]
            v_s = [Buf(s(f"v{i}", [P, NT, 256])) for i in range(2)]
            q_w, k_w, v_w = s("q_w", [P, 4, T]), s("k_w", [P, 2, T]), s("v_w", [P, NT, P])
            bias = s("bias", [P, 8, 256])
            sink = s("sink", [P, 8])
            rel, onehot, outside = s("rel", [N_BUCKETS, 8]), s("onehot", [N_BUCKETS, 384]), s("outside", [8, 384])
            N_TRI = sum(T - P * i for i in range(NT))
            at = [sum(T - P * k for k in range(i)) for i in range(NT)]
            tri = [Buf((s(f"nl{i}", [P, N_TRI]), s(f"lb{i}", [P, N_TRI]))) for i in range(2)]

            sh["begin_u"]()
            sh["norm_to"](U, sh["x_tiles"](), lambda k: column("g_mix_2", k), D)
            sh["enter"]()
            s_in, s_w = sh["sem"]("b2_small_loaded"), sh["s_io"]
            nc.sync.dma_start(rel[:, :], ins["rel_bias"]).then_inc(s_in, 16)
            nc.sync.dma_start(onehot[:, :], ins["const_onehot"]).then_inc(s_in, 16)
            nc.sync.dma_start(outside[:, :], ins["const_outside"]).then_inc(s_in, 16)
            nc.sync.dma_start(sink[:, :], ins["sinks"].to_broadcast([P, 8])).then_inc(s_in, 16)
            small = (s_in, 64)
            bank = banks.take()
            PE.wait(*bank.busy, small)
            m = fmm(bank.ap[0:8, 0:384], [(rel[:, :], onehot[:, :])])
            m = VE(lambda v: v.tensor_tensor(outside[:, :], bank.ap[0:8, 0:384], outside[:, :], ADD), m, small)
            banks.give(bank, m)
            rows = nc.dram_tensor("bias_rows", (8, 384), F32, kind="Internal").ap()
            SP.wait(m)
            nc.sync.dma_start(rows, outside[:, :]).then_inc(s_w, 16)
            SP.wait((s_w, 16))
            shifted = bass.AP(tensor=rows.tensor, offset=0, ap=[[1, P], [384, 8], [1, 256]])
            nc.sync.dma_start(bias[:, :, :], shifted).then_inc(s_w, 16)
            kept = {}

            def to_sbuf(dst, bank, width, m, busy=(), n=T):
                mark = AC(lambda v: v.activation(dst, bank.ap[:, 0:n] if width is None else bank.ap[:, 0:width],
                                                 ACT.Copy), m, *busy)
                banks.give(bank, mark)
                return mark

            def project_keys():
                w = use(("b2_w_k",))
                for j in range(2):
                    bank, m = feature_tile(w, j * P, U)
                    kept["wk"] = to_sbuf(k_w[:, j, :], bank, None, m)
                used(w, m)
                w = use(("b2_w_v",))
                for k in range(NT):
                    bank, m = token_tile(w, 0, P, U, k * P)
                    kept["wv"] = to_sbuf(v_w[:, k, :], bank, P, m)
                used(w, m)

            def project_queries(c0):
                w = use(("b2_w_q", c0))
                for j in range(2):
                    bank, m = feature_tile(w, j * P, U)
                    if j:
                        used(w, m)
                    yield
                    kept["wq", c0 // P + j] = to_sbuf(q_w[:, c0 // P + j, :], bank, None, m)

            def project(p):
                if p % 2 == 0:
                    vb = v_s[p // 2]
                    w = use(("b2_s_v", p))
                    for k in range(0, NT, 2):
                        two = [(i, *token_tile(w, 0, 256, U, i * P)) for i in (k, k + 1)]
                        if k:
                            used(w, two[1][2])
                        yield
                        for i, bank, m in two:
                            kept["v", p // 2] = to_sbuf(vb.ap[:, i, :], bank, 256, m)
                w = use(("b2_s_qk", p))
                for j in range(2):
                    bank, m = feature_tile(w, j * P, U)
                    if j:
                        used(w, m)
                    yield
                    kept["qk", p] = to_sbuf(qk[p % 2][:, j, :], bank, None, m, qk_busy[p % 2])

            def stick_of(n):
                return n // 2, tri[n % 2], slice((n % 2) * HEAD_P, (n % 2 + 1) * HEAD_P)

            def stick_logs(n, blocks):
                p, buf, r = stick_of(n)
                nl, lb = buf.ap
                q, k = qk[p % 2][r, 0, :], qk[p % 2][r, 1, :]
                for i in blocks:
                    width, t0 = T - i * P, i * P
                    part = slice(at[i], at[i] + width)
                    bank = banks.take()
                    PE.wait(*bank.busy)
                    m = fmm(bank.ap[:, 0:width], [(k[:, t0:t0 + P], q[:, t0:T])], kept["qk", p])
                    m1 = AC(lambda v: v.activation(lb[:, part], bank.ap[:, 0:width], ACT.Abs, scale=SCALE), m,
                            *buf.busy)
                    m2 = AC(lambda v: v.activation(lb[:, part], lb[:, part], ACT.Exp, scale=-1.0), m1)
                    m2 = AC(lambda v: v.activation(lb[:, part], lb[:, part], ACT.Ln, bias=1.0), m2)
                    m3 = VE(lambda v: v.tensor_scalar(nl[:, part], bank.ap[:, 0:width], SCALE, 0.0, MUL, MAX), m1,
                            *buf.busy)
                    m3 = VE(lambda v: v.tensor_tensor(nl[:, part], nl[:, part], lb[:, part], ADD), m2, m3)
                    m4 = VE(lambda v: v.scalar_tensor_tensor(out=lb[:, part], in0=bank.ap[:, 0:width], scalar=SCALE,
                                                             in1=nl[:, part], op0=MUL, op1=SUB), m3)
                    banks.give(bank, m4)
                    diag = slice(at[i], at[i] + P)
                    m_nl = PO(lambda v: v.tensor_tensor(nl[:, diag], nl[:, diag], sh["m_lt"], MUL), m4)
                    kept["log", n, i] = (m4, m_nl)
                qk_busy[p % 2] = (m,)

            def stick_sums(n):
                _, buf, _ = stick_of(n)
                nl, lb = buf.ap
                for i in range(NT):
                    width = T - i * P
                    part = slice(at[i], at[i] + width)
                    bank = banks.take()
                    PE.wait(*bank.busy, *(m for j in range(i, NT) for m in kept["log", n, j]))
                    for j in range(i, NT):
                        m = PE(lambda v: v.matmul(bank.ap[:, (j - i) * P:width], sh["m_gt"] if j == i else ones,
                                                  nl[:, at[j]:at[j] + T - j * P], start=j == i,
                                                  stop=j == NT - 1))
                    m = VE(lambda v: v.tensor_tensor(lb[:, part], lb[:, part], bank.ap[:, 0:width], SUB), m)
                    banks.give(bank, m)
                    m = AC(lambda v: v.activation(lb[:, part], lb[:, part], ACT.Exp), m)
                    diag = slice(at[i], at[i] + P)
                    kept["weight", n, i] = PO(lambda v: v.tensor_tensor(lb[:, diag], lb[:, diag], sh["m_lt"], MUL), m)

            def stick_values(n):
                p, buf, r = stick_of(n)
                if n % 2 == 0:
                    kept["o", p] = banks.take()
                    PE.wait(*kept["o", p].busy)
                o_bank = kept["o", p]
                c0 = (p % 2) * P + (n % 2) * HEAD_P
                PE.wait(kept["v", p // 2])
                for i in range(NT):
                    m_o = PE(lambda v: v.matmul(o_bank.ap[r, i * P:T], v_s[p // 2].ap[:, i, c0:c0 + HEAD_P],
                                                buf.ap[1][:, at[i]:at[i] + T - i * P], start=i == 0, stop=i == NT - 1),
                             kept["weight", n, i])
                buf.busy = (m_o,)
                if n % 2:
                    o_ready[p] = VE(lambda v: v.tensor_copy(o[:, p, :], o_bank.ap), m_o)
                    banks.give(o_bank, o_ready[p])

            def sticks():
                stick_logs(0, (0, 1))
                yield
                stick_logs(0, (2, 3))
                yield
                for n in range(8):
                    if n:
                        stick_values(n - 1)
                    if n < 7:
                        stick_logs(n + 1, (0, 1))
                        yield
                    stick_sums(n)
                    yield
                    if n < 7:
                        stick_logs(n + 1, (2, 3))
                        yield
                stick_values(7)

            def window_of(h):
                buf = tri[h % 2]
                return (buf, buf.ap[0][:, 0:1024].rearrange("p (n s) -> p n s", n=NT), buf.ap[1][:, 0:T],
                        buf.ap[1][:, T:2 * T])

            def window_scores(h):
                buf = tri[h % 2]
                S = buf.ap[0][:, 0:1024].rearrange("p (n s) -> p n s", n=NT)
                cur, prev = buf.ap[1][:, 0:T], buf.ap[1][:, T:2 * T]
                stats = buf.ap[0][:, 1024:1024 + 20].rearrange("p (k n) -> p k n", n=4)
                r = slice((h % 2) * HEAD_P, (h % 2 + 1) * HEAD_P)
                q, k = q_w[r, h // 2, :], k_w[r, h // 4, :]
                kv = slice((h // 4) * HEAD_P, (h // 4 + 1) * HEAD_P)
                b2 = [banks.take(), banks.take()]
                PE.wait(*b2[0].busy, *b2[1].busy, kept["wk"], kept["wq", h // 2])
                for n in range(NT):
                    lo = max(0, n - 1) * P
                    dst = b2[n // 2].ap[:, (n % 2) * 256 + (256 - ((n + 1) * P - lo)):(n % 2) * 256 + 256]
                    m = PE(lambda v: v.matmul(dst, q[:, n * P:(n + 1) * P], k[:, lo:(n + 1) * P], start=True,
                                              stop=True))
                m0 = VE(lambda v: v.memset(S[:, 0, 0:P], NEG), *buf.busy)
                VE(lambda v: v.scalar_tensor_tensor(out=S[:, 0, P:256], in0=b2[0].ap[:, P:256], scalar=SCALE,
                                                    in1=bias[:, h, P:256], op0=MUL, op1=ADD), m, m_bias)
                m1 = VE(lambda v: v.scalar_tensor_tensor(out=S[:, 1, :], in0=b2[0].ap[:, 256:512], scalar=SCALE,
                                                         in1=bias[:, h, :], op0=MUL, op1=ADD))
                m2 = VE(lambda v: v.scalar_tensor_tensor(
                    out=S[:, 2:4, :], in0=b2[1].ap.rearrange("p (n s) -> p n s", n=2), scalar=SCALE,
                    in1=bias[:, h:h + 1, :].to_broadcast([P, 2, 256]), op0=MUL, op1=ADD))
                banks.give(b2[0], m1)
                banks.give(b2[1], m2)
                m = VE(lambda v: v.tensor_reduce(stats[:, 0, :], S, AX_X, MAX), m2)
                sk = sink[:, h:h + 1]
                m = VE(lambda v: v.tensor_scalar(stats[:, 0, :], stats[:, 0, :], sk, None, MAX), m, small)
                VE(lambda v: v.tensor_scalar(stats[:, 1, :], stats[:, 0, :], -1.0, sk, MUL, ADD), m)
                m = VE(lambda v: v.tensor_tensor(S, S, stats[:, 0, :].rearrange("p (n o) -> p n o", o=1).to_broadcast(
                    [P, NT, 256]), SUB))
                AC(lambda v: v.activation(stats[:, 1, :], stats[:, 1, :], ACT.Exp), m)
                m = AC(lambda v: v.activation(S, S, ACT.Exp))
                m = VE(lambda v: v.tensor_reduce(stats[:, 2, :], S, AX_X, ADD), m)
                m = VE(lambda v: v.tensor_tensor(stats[:, 2, :], stats[:, 2, :], stats[:, 1, :], ADD), m)
                m = VE(lambda v: v.reciprocal(stats[:, 3, :], stats[:, 2, :]), m)
                m = VE(lambda v: v.tensor_tensor(S, S, stats[:, 3, :].rearrange("p (n o) -> p n o", o=1).to_broadcast(
                    [P, NT, 256]), MUL), m)
                kept["window", h] = m

            def window_turned(h):
                buf, S, cur, prev = window_of(h)
                m = kept["window", h]
                b2 = [banks.take(), banks.take()]
                PE.wait(*b2[0].busy, *b2[1].busy, m)
                for n in range(NT):
                    m = PE(lambda v: v.transpose(b2[0].ap[:, n * P:(n + 1) * P], S[:, n, P:256], ident))
                    if n:
                        m = PE(lambda v: v.transpose(b2[1].ap[:, n * P:(n + 1) * P], S[:, n, 0:P], ident))
                m1 = AC(lambda v: v.activation(cur, b2[0].ap, ACT.Copy), m)
                m2 = AC(lambda v: v.activation(prev[:, P:T], b2[1].ap[:, P:T], ACT.Copy))
                banks.give(b2[0], m1)
                banks.give(b2[1], m2)
                kept["window", h] = m2

            def window_values(h):
                buf, S, cur, prev = window_of(h)
                r = slice((h % 2) * HEAD_P, (h % 2 + 1) * HEAD_P)
                kv = slice((h // 4) * HEAD_P, (h // 4 + 1) * HEAD_P)
                m2 = kept["window", h]
                if h % 2 == 0:
                    kept["wo"] = banks.take()
                    PE.wait(*kept["wo"].busy)
                o_bank = kept["wo"]
                PE.wait(m2, kept["wv"])
                for n in range(NT):
                    sl = slice(n * P, (n + 1) * P)
                    pairs = [(v_w[:, n, kv], cur[:, sl])]
                    if n:
                        pairs.append((v_w[:, n - 1, kv], prev[:, sl]))
                    m_o = fmm(o_bank.ap[r, sl], pairs)
                buf.busy = (m_o,)
                if h % 2:
                    i = 4 + h // 2
                    o_ready[i] = VE(lambda v: v.tensor_copy(o[:, i, :], o_bank.ap), m_o)
                    banks.give(o_bank, o_ready[i])

            def windows():
                window_scores(0)
                yield
                for h in range(8):
                    if h < 7:
                        window_scores(h + 1)
                        yield
                    window_turned(h)
                    yield
                    window_values(h)

            def chain(*gens):
                for g in gens:
                    yield from g

            project_keys()
            run(project_queries(0))
            for i in range(4):
                part = bias[:, 2 * i:2 * i + 2, :].rearrange("p h s -> p (h s)")
                bank = banks.take()
                m = fmm(bank.ap, [(sh["turn"], part)], (s_w, 32), *bank.busy)
                m_bias = VE(lambda v: v.tensor_copy(part, bank.ap), m)
                banks.give(bank, m_bias)

            together((chain(project_queries(256), project(0), project(1)), 8), (windows(), 16))
            in_order(STICK_ORDER, s=sticks(), p=chain(project(2), project(3)))
            sh["barrier"]()
        with ExitStack() as c:
            def s(name, shape, dt=F32):
                return sh["sb"]("b2_" + name, shape, dt, c)

            y = [s("y_a", [P, DT, T]), s("y_b", [P, DT, T])]
            V = Split(s("o_hi", [P, 4, T], F32R), s("o_lo", [P, 4, T], F32R), 4)
            merged = [None] * DT
            for b, name in enumerate("ab"):
                V.ready = [()] * 4
                for k in range(4):
                    split_to(V, k, o[:, 4 * b + k, :], (o_ready[4 * b + k],))
                up = []
                for c0 in (0, 512):
                    w = use(("b2_up_" + name, c0))
                    for j in range(4):
                        bank, m = feature_tile(w, j * P, V)
                        up.append(VE(lambda v: v.tensor_copy(y[b][:, c0 // P + j, :], bank.ap), m))
                        banks.give(bank, up[-1])
                    used(w, m)
                V.busy = (m,)
                for c0 in range(0, D, 256):
                    w = use(("b2_gate_" + name, c0))
                    for j in range(2):
                        k = c0 // P + j
                        bank, m = feature_tile(w, j * P, U)
                        t = work.take()
                        m1 = AC(lambda v: v.activation(t.ap, bank.ap, ACT.Sigmoid), m, *t.busy)
                        banks.give(bank, m1)
                        m2 = VE(lambda v: v.tensor_tensor(y[b][:, k, :], y[b][:, k, :], t.ap, MUL), m1, up[k])
                        work.give(t, m2)
                        if b:
                            m2 = VE(lambda v: v.tensor_tensor(y[1][:, k, :], y[1][:, k, :], y[0][:, k, :], ADD), m2)
                            merged[k] = m2
                    used(w, m)
            sh["begin_u"]()
            for k in range(DT):
                split_to(U, k, y[1][:, k, :], (merged[k],))
            for c0 in range(0, D, 256):
                w = use(("b2_o", c0))
                for j in range(2):
                    bank, m = feature_tile(w, j * P, U)
                    sh["add_to_x"](c0 // P + j, bank, m)
                used(w, m)
            sh["leave"]()

    def hidden(w, j, t, H, slot):
        bank, m = feature_tile(w, j * P, U)
        a = work.take()
        m1 = AC(lambda v: v.activation(a.ap, bank.ap, ACT.Relu), m, *a.busy)
        banks.give(bank, m1)
        m1 = VE(lambda v: v.tensor_tensor(a.ap, a.ap, a.ap, MUL), m1)
        work.give(a, *split_to(H, slot, a.ap, (m1,)))
        return m

    sh["begin_u"]()
    sh["norm_to"](U, sh["x_tiles"](), lambda k: column("g_mlp_2", k), D)
    sh["mlp"]("ff2", FF2_TILES, 2, hidden)

    with ExitStack() as c:
        sh["begin_u"]()
        sh["norm_to"](U, sh["x_tiles"](), lambda k: column("g_pe_2", k), D)
        sh["enter"]()
        p_in = sh["sb"]("b2_p", [P, 2, T], F32, c)
        V = Split(sh["sb"]("b2_p_hi", [P, 2, T], F32R, c), sh["sb"]("b2_p_lo", [P, 2, T], F32R, c), 2)
        pe_out = sh["sb"]("b2_pe", [P, DT, T], F32, c)
        s_p = sh["sem"]("b2_p_loaded")
        nc.sync.dma_start(p_in[:, :, :], ins["p_t"].rearrange("(k p) t -> p k t", p=P)).then_inc(s_p, 16)
        for k in range(2):
            split_to(V, k, p_in[:, k, :], ((s_p, 16),))
        w = use(("b2_pe",))
        m_pe = []
        for k in range(DT):
            bank, m = feature_tile(w, k * P, V)
            m_pe.append(AC(lambda v: v.activation(pe_out[:, k, :], bank.ap, ACT.Copy), m))
            banks.give(bank, m_pe[-1])
        used(w, m)
        for c0 in range(0, D, 256):
            w = use(("b2_pg", c0))
            for j in range(2):
                k = c0 // P + j
                bank, m = feature_tile(w, j * P, U)
                t = work.take()
                m1 = AC(lambda v: v.activation(t.ap, bank.ap, ACT.Sigmoid), m, *t.busy)
                banks.give(bank, m1)
                m1 = VE(lambda v: v.tensor_tensor(t.ap, t.ap, pe_out[:, k, :], MUL), m1, m_pe[k])
                m1 = VE(lambda v: v.tensor_tensor(x[:, k, :], x[:, k, :], t.ap, ADD), m1, *x_ready[k])
                work.give(t, m1)
                x_ready[k] = (m1,)
            used(w, m)
        sh["barrier"]()
    final_to_x(sh, "g_final_2")



MLA_ORDER = "aapapapapapaap"


def block3(sh):
    nc, PE, VE, AC, PO, SP = (sh[n] for n in ("nc", "PE", "VE", "AC", "PO", "SP"))
    banks, work, column, use, used = sh["banks"], sh["work"], sh["column"], sh["use"], sh["used"]
    feature_tile, token_tile, fmm, ident, U = (sh[n] for n in ("feature_tile", "token_tile", "fmm", "ident", "U"))
    ins, x, x_ready, ones, Split, split_to = (sh[n] for n in ("ins", "x", "x_ready", "ones", "Split", "split_to"))
    modv, m_mod = sh["modv"], sh["mod_slot"].done
    SHIFT1, SCALE1, GATE1, SHIFT2, SCALE2, GATE2 = range(0, 48, DT)
    with ExitStack() as outer:
        gains = sh["sb"]("c_gains", [P, 3, DT], F32, outer)
        for i, (g, at, who) in enumerate((("g_mix_3", SCALE1, 0), ("g_mix_3", SCALE1, 1), ("g_ffn_3", SCALE2, 0))):
            m = VE(lambda v: v.tensor_scalar(gains[:, i, :], modv[:, at:at + DT, who], 1.0, None, ADD), m_mod)
            m_gain = VE(lambda v: v.tensor_tensor(gains[:, i, :], gains[:, i, :], column(g, 0, DT), MUL), m)
        saved = nc.dram_tensor("x_saved", (P, DT, T), F32, kind="Internal").ap()
        s_save = sh["sem"]("x_saved_and_back")
        conv = sh["sb"]("c_conv", [P, DT, T + 2 * HALO], F32, outer)
        m_halo = PO(lambda v: v.memset(conv[:, :, 0:HALO], 0.0))
        m_halo = PO(lambda v: v.memset(conv[:, :, HALO + T:], 0.0))
        conv_ready, conv_done = [None] * DT, [None] * DT

        O, o_ready = x, [None] * DT
        with ExitStack() as c:
            def s(name, shape, dt=F32, c=c):
                return sh["sb"]("c_" + name, shape, dt, c)

            kv = Split(s("kv_hi", [P, 2, KEYS], F32R), s("kv_lo", [P, 2, KEYS], F32R), 2)
            qa = Split(s("qa_hi", [P, 3, T], F32R), s("qa_lo", [P, 3, T], F32R), 3)
            kr = s("kr", [QK_ROPE, KEYS])
            rope = s("rope", [QK_ROPE, 2, T])
            s_in = sh["sem"]("c_context_loaded")
            nc.sync.dma_start(rope[:, :, :], ins["const_rope"][0:QK_ROPE]).then_inc(s_in, 16)

            def rotary(buf, ap, mark):
                bank = banks.take()
                m = fmm(bank.ap[0:QK_ROPE, :], [(sh["rotate"][0:QK_ROPE, 0:QK_ROPE], ap)], mark, *bank.busy)
                t = work.take()
                m1 = VE(lambda v: v.tensor_tensor(t.ap[0:QK_ROPE, :], bank.ap[0:QK_ROPE, :], rope[:, 1, :], MUL), m,
                        (s_in, 16), *t.busy)
                banks.give(bank, m1)
                m2 = VE(lambda v: v.tensor_tensor(ap, ap, rope[:, 0, :], MUL), m1)
                m2 = VE(lambda v: v.tensor_tensor(ap, ap, t.ap[0:QK_ROPE, :], ADD), m2)
                work.give(t, m2)
                return m2

            with ExitStack() as early:
                ctx = s("ctx", [P, DT, CTX], c=early)
                nc.sync.dma_start(ctx[:, :, :], ins["ctx_t"].rearrange("(k p) t -> p k t", p=P)).then_inc(s_in, 16)
                hc = Split(s("hc_hi", [P, DT, CTX], F32R, early), s("hc_lo", [P, DT, CTX], F32R, early), DT)
                sh["norm_to"](hc, [(ctx[:, k, :], ((s_in, 32),)) for k in range(DT)],
                              lambda k: gains[:, 1, k:k + 1], D, n=CTX, shifts=lambda k: modv[:, SHIFT1 + k, 1:2],
                              need=(m_gain,))
                sh["begin_u"]()
                readers = sh["norm_to"](U, sh["x_tiles"](), lambda k: gains[:, 0, k:k + 1], D,
                                        shifts=lambda k: modv[:, SHIFT1 + k, 0:1], need=(m_gain,))
                SP.wait(*[m for k in range(DT) for m in x_ready[k]])
                nc.sync.dma_start(saved, x[:, :, :]).then_inc(s_save, 16)
                w = use(("c_kv",))
                held = []
                for X, n, c0 in ((hc, CTX, 0), (U, T, CTX)):
                    tiles = []
                    for j in range(2):
                        bank, m = feature_tile(w, j * P, X, n=n)
                        tiles.append((bank, m))
                    held.append((tiles, n, c0))
                used(w, m)
                for tiles, n, c0 in held:
                    marks = sh["norm_to"](kv, [(b.ap[:, 0:n], (m,)) for b, m in tiles],
                                          lambda k: column("g_kv", k), 2 * P, n=n, c0=c0)
                    for (b, _), mk in zip(tiles, marks):
                        banks.give(b, mk)
                w = use(("c_kr",))
                for X, n, c0 in ((hc, CTX, 0), (U, T, CTX)):
                    bank, m = feature_tile(w, 0, X, width=QK_ROPE, n=n)
                    m_kr = AC(lambda v: v.activation(kr[:, c0:c0 + n], bank.ap[0:QK_ROPE, 0:n], ACT.Copy), m)
                    banks.give(bank, m_kr)
                used(w, m)
                m_kr = (m_kr, rotary(None, kr[:, CTX:KEYS], m_kr))
                tiles = []
                for key, n in ((("c_q",), 2), (("c_q2",), 1)):
                    w = use(key)
                    for j in range(n):
                        tiles.append(feature_tile(w, j * P, U))
                    used(w, tiles[-1][1])
                marks = sh["norm_to"](qa, [(b.ap, (m,)) for b, m in tiles], lambda k: column("g_q", k), 3 * P)
                for (b, _), mk in zip(tiles, marks):
                    banks.give(b, mk)
                sh["leave"]()

            def project_conv():
                for t in range(DT):
                    w = use(("c_conv", t))
                    ba, ma = feature_tile(w, 0, U)
                    bg, mg = feature_tile(w, P, U)
                    used(w, mg)
                    sg = work.take()
                    m = AC(lambda v: v.activation(sg.ap, bg.ap, ACT.Sigmoid), mg, *sg.busy)
                    banks.give(bg, m)
                    conv_ready[t] = VE(lambda v: v.tensor_tensor(conv[:, t, HALO:HALO + T], ba.ap, sg.ap, MUL), m,
                                       ma, m_halo)
                    banks.give(ba, conv_ready[t])
                    work.give(sg, conv_ready[t])
                    yield

            acc = [Buf(s(f"acc{i}", [P, T])[:, :]) for i in range(2)]

            def convolve():
                for t in range(DT):
                    a = acc[t % 2]
                    m = VE(lambda v: v.tensor_scalar(a.ap, conv[:, t, 0:T], column("w_dw", t), column("b_dw", t), MUL,
                                                     ADD), conv_ready[t], *a.busy)
                    for i in range(1, CONV_W):
                        m = VE(lambda v: v.scalar_tensor_tensor(out=a.ap, in0=conv[:, t, i:i + T],
                                                                scalar=column("w_dw", i * DT + t), in1=a.ap, op0=MUL,
                                                                op1=ADD), m)
                        if i % 3 == 0:
                            yield
                    conv_done[t] = AC(lambda v: v.activation(conv[:, t, HALO:HALO + T], a.ap, ACT.Copy), m)
                    a.busy = (conv_done[t],)
                    yield

            side = [{"kn": s(f"kn{i}", [P, KEYS]), "vt": s(f"vt{i}", [P, KT3, P])} for i in range(2)]
            side_busy = [(), ()]
            qn, qr = s("qn", [P, T]), s("qr", [QK_ROPE, T])
            q_busy = [()]
            prob = [Buf(s(f"prob{i}", [P, KEYS])[:, :]) for i in range(2)]
            prob_t = Buf(s("prob_t", [P, KT3, P]))
            st = s("stats", [P, 2, 8])
            kept = {}

            def project_head(h):
                b, busy, marks = side[h % 2], side_busy[h % 2], []

                def leaves(dst, src, bank, m, busy=busy):
                    marks.append(AC(lambda v: v.activation(dst, src, ACT.Copy), m, *busy))
                    banks.give(bank, marks[-1])

                w = use(("c_ukv", h))
                held = []
                for c0, n in ((0, T), (T, KEYS - T)):
                    bank, m = feature_tile(w, 0, kv, n=n, c0=c0)
                    held.append((b["kn"][:, c0:c0 + n], bank.ap[:, 0:n], bank, m))
                yield
                for k in range(0, KT3, 2):
                    for one in held:
                        leaves(*one)
                    held = []
                    for i in (k, k + 1):
                        bank, m = token_tile(w, P, P, kv, i * P)
                        held.append((b["vt"][:, i, :], bank.ap[:, 0:P], bank, m))
                    if k == KT3 - 2:
                        used(w, m)
                    yield
                for one in held:
                    leaves(*one)
                w = use(("c_uq", h))
                bank, m = feature_tile(w, P, qa, width=QK_ROPE)
                held = [(qr[:, :], bank.ap[0:QK_ROPE, :], bank, m)]
                bank, m = feature_tile(w, 0, qa)
                used(w, m)
                leaves(*held[0], q_busy[0])
                yield
                m_rot = rotary(None, qr[:, :], marks[-1])
                leaves(qn[:, :], bank.ap, bank, m, q_busy[0])
                kept["head", h] = (*marks, m_rot)
                yield

            def attend(h):
                b, marks = side[h % 2], kept["head", h]
                kn, vt = b["kn"], b["vt"]
                o_bank = banks.take()
                PE.wait(*o_bank.busy)

                def scores(n):
                    q = slice(n * P, (n + 1) * P)
                    two = [banks.take(), banks.take()]
                    PE.wait(*two[0].busy, *two[1].busy, *marks, *m_kr)
                    for bank, (c0, width) in zip(two, ((0, T), (T, KEYS - T))):
                        m = fmm(bank.ap[:, 0:width], [(qn[:, q], kn[:, c0:c0 + width]), (qr[:, q], kr[:, c0:c0 + width])])
                    q_busy[0] = (m,)
                    pb, stat = prob[n % 2], st[:, n % 2, :]
                    VE(lambda v: v.tensor_reduce(stat[:, 0:1], two[0].ap, AX_X, MAX), m, *pb.busy)
                    m = VE(lambda v: v.tensor_reduce(stat[:, 1:2], two[1].ap[:, 0:KEYS - T], AX_X, MAX))
                    m = VE(lambda v: v.tensor_scalar(stat[:, 2:3], stat[:, 0:1], stat[:, 1:2], -ATTN_SCALE, MAX,
                                                     MUL), m)
                    m1 = AC(lambda v: v.activation(pb.ap[:, 0:T], two[0].ap, ACT.Exp, bias=stat[:, 2:3],
                                                   scale=ATTN_SCALE, accum_out=stat[:, 3:4]), m, *pb.busy)
                    m2 = AC(lambda v: v.activation(pb.ap[:, T:KEYS], two[1].ap[:, 0:KEYS - T], ACT.Exp,
                                                   bias=stat[:, 2:3], scale=ATTN_SCALE, accum_out=stat[:, 4:5]))
                    banks.give(two[0], m1)
                    banks.give(two[1], m2)
                    return m1, m2

                def divided(n, m1, m2):
                    pb, stat = prob[n % 2], st[:, n % 2, :]
                    m = VE(lambda v: v.tensor_tensor(stat[:, 5:6], stat[:, 3:4], stat[:, 4:5], ADD), m1, m2)
                    m = VE(lambda v: v.reciprocal(stat[:, 6:7], stat[:, 5:6]), m)
                    return VE(lambda v: v.tensor_scalar(pb.ap, pb.ap, stat[:, 6:7], None, MUL), m)

                def turned(n, m_p):
                    pb = prob[n % 2]
                    two = [banks.take(), banks.take()]
                    PE.wait(*two[0].busy, *two[1].busy, m_p)
                    for k in range(KT3):
                        m = PE(lambda v: v.transpose(two[k // 4].ap[:, (k % 4) * P:(k % 4 + 1) * P],
                                                     pb.ap[:, k * P:(k + 1) * P], ident))
                    pb.busy = (m,)
                    flat = prob_t.ap[:, :, :].rearrange("p k t -> p (k t)")
                    m1 = AC(lambda v: v.activation(flat[:, 0:T], two[0].ap, ACT.Copy), m, *prob_t.busy)
                    m2 = AC(lambda v: v.activation(flat[:, T:KEYS], two[1].ap[:, 0:KEYS - T], ACT.Copy))
                    banks.give(two[0], m1)
                    banks.give(two[1], m2)
                    return m1, m2

                def values(n, m1, m2):
                    m = fmm(o_bank.ap[:, n * P:(n + 1) * P], [(vt[:, k, :], prob_t.ap[:, k, :]) for k in range(KT3)],
                            m1, m2)
                    prob_t.busy = (m,)
                    return m

                m_s = scores(0)
                yield
                for n in range(NT):
                    m_p = divided(n, *m_s)
                    if n + 1 < NT:
                        m_s = scores(n + 1)
                    m_t = turned(n, m_p)
                    yield
                    m_o = values(n, *m_t)
                    yield
                side_busy[h % 2] = (m_o,)
                o_ready[h] = VE(lambda v: v.tensor_copy(O[:, h, :], o_bank.ap), m_o, (s_save, 16), *readers)
                banks.give(o_bank, o_ready[h])

            def heads():
                yield from project_head(0)
                for h in range(8):
                    both = {"a": attend(h), "p": project_head(h + 1) if h < 7 else iter(())}
                    for letter in MLA_ORDER:
                        next(both[letter], None)
                        yield
                    for g in both.values():
                        yield from g

            run(project_conv())
            sh["enter"]()
            together((heads(), 6 + 8 * len(MLA_ORDER)), (convolve(), 88))
            sh["barrier"]()
        with ExitStack() as c:
            gate = [sh["sb"]("c_gate_conv", [P, DT, T], F32, c), sh["sb"]("c_gate_mla", [P, DT, T], F32, c)]
            g_ready = [[None] * DT, [None] * DT]
            for c0 in range(0, 2 * D, 256):
                w = use(("c_gate", c0))
                for j in range(2):
                    i, k = divmod(c0 // P + j, DT)
                    bank, m = feature_tile(w, j * P, U)
                    g_ready[i][k] = AC(lambda v: v.activation(gate[i][:, k, :], bank.ap, ACT.Sigmoid), m)
                    banks.give(bank, g_ready[i][k])
                used(w, m)
            sh["begin_u"]()
            m_o = []
            for k in range(DT):
                m_o += split_to(U, k, O[:, k, :], (o_ready[k],))
            SP.wait(*m_o)
            nc.sync.dma_start(x[:, :, :], saved).then_inc(s_save, 16)
            for k in range(DT):
                x_ready[k] = ((s_save, 32),)
            bank = banks.take()
            PE.wait(*bank.busy)
            for k in range(DT):
                m = PE(lambda v: v.matmul(bank.ap, ones, conv[:, k, HALO:HALO + T], start=k == 0, stop=k == DT - 1),
                       conv_done[k])
            mu = work.take()
            m = VE(lambda v: v.tensor_scalar(mu.ap, bank.ap, 1.0 / D, None, MUL), m, *mu.busy)
            banks.give(bank, m)
            tiles = []
            for k in range(DT):
                t = conv[:, k, HALO:HALO + T]
                m1 = VE(lambda v: v.tensor_tensor(t, t, mu.ap, SUB), m)
                tiles.append((t, (m1,)))
            work.give(mu, m1)
            m_conv = []
            for c0 in range(0, D, 256):
                w = use(("c_omla", c0))
                for j in range(2):
                    k = c0 // P + j
                    bank, m = feature_tile(w, j * P, U)
                    g_ready[1][k] = VE(lambda v: v.tensor_tensor(gate[1][:, k, :], bank.ap, gate[1][:, k, :], MUL), m,
                                       g_ready[1][k])
                    banks.give(bank, g_ready[1][k])
                used(w, m)
                if c0 == 256:
                    r, m_r = sh["inverse_rms"](tiles, D)
                    for k, (t, _) in enumerate(tiles):
                        m = VE(lambda v: v.scalar_tensor_tensor(out=t, in0=t, scalar=column("ln_g", k), in1=r.ap,
                                                                op0=MUL, op1=MUL), m_r)
                        m_conv.append(AC(lambda v: v.activation(t, t, ACT.Silu, bias=column("ln_b", k)), m))
                    work.give(r, m)
            sh["begin_u"]()
            for k in range(DT):
                split_to(U, k, tiles[k][0], (m_conv[k],))
            for c0 in range(0, D, 256):
                w = use(("c_pw", c0))
                for j in range(2):
                    k = c0 // P + j
                    bank, m = feature_tile(w, j * P, U)
                    m1 = VE(lambda v: v.tensor_tensor(gate[0][:, k, :], bank.ap, gate[0][:, k, :], MUL), m,
                            g_ready[0][k])
                    banks.give(bank, m1)
                    g_ready[0][k] = VE(lambda v: v.tensor_tensor(gate[0][:, k, :], gate[0][:, k, :],
                                                                 gate[1][:, k, :], ADD), m1, g_ready[1][k])
                used(w, m)
            sh["begin_u"]()
            for k in range(DT):
                split_to(U, k, gate[0][:, k, :], (g_ready[0][k],))
            for c0 in range(0, D, 256):
                w = use(("c_out", c0))
                for j in range(2):
                    bank, m = feature_tile(w, j * P, U)
                    sh["add_to_x"](c0 // P + j, bank, m, lambda k: modv[:, GATE1 + k, 0:1])
                used(w, m)
            sh["barrier"]()

        def hidden(w, j, t, H, slot):
            ba, ma = feature_tile(w, 0, U)
            bb, mb = feature_tile(w, P, U)
            a = work.take()
            m = AC(lambda v: v.activation(a.ap, ba.ap, ACT.Silu), ma, *a.busy)
            banks.give(ba, m)
            m = VE(lambda v: v.tensor_tensor(a.ap, a.ap, bb.ap, MUL), m, mb)
            banks.give(bb, m)
            work.give(a, *split_to(H, slot, a.ap, (m,)))
            return mb

        sh["begin_u"]()
        sh["norm_to"](U, sh["x_tiles"](), lambda k: gains[:, 2, k:k + 1], D,
                      shifts=lambda k: modv[:, SHIFT2 + k, 0:1])
        sh["mlp"]("ffn3", FF_TILES, 1, hidden, scale=lambda k: modv[:, GATE2 + k, 0:1])
    final_to_x(sh, "g_final_3")



def tile_columns(v):
    return np.ascontiguousarray(np.reshape(v, (-1, P)).T)


def pack_vectors(a):
    cols, n_cols = column_plan()
    dt_pad = np.zeros(P, np.float32)
    out = np.zeros((P, n_cols), np.float32)

    def put(name, block):
        at, n = cols[name]
        out[0:block.shape[0], at:at + n] = block

    put("norm1", tile_columns(a["norm1_w"]))
    put("norm2", tile_columns(a["norm2_w"]))
    put("lb", tile_columns(a["a_lb_logits"]))
    put("a_norm", tile_columns(a["a_norm_w"]))
    put("conv_w", tile_columns(a["b_conv_w"]))
    put("conv_b", tile_columns(a["b_conv_b"]))
    put("d_skip", tile_columns(np.repeat(a["b_d_skip"].reshape(-1), HEAD_P)))
    put("b_norm", tile_columns(a["b_norm_w"]))
    put("dt_bias", a["b_dt_bias"].reshape(N_DT, 1))
    put("a_log", a["b_a_log"].reshape(N_DT, 1))
    put("ffn_cw", tile_columns(a["ffn_conv_w"]))
    put("ffn_cb", tile_columns(a["ffn_conv_b"]))
    put("final", tile_columns(a["final_norm_w"]))
    for n in ("g_mix_2", "g_mlp_2", "g_pe_2", "g_final_2", "g_mix_3", "g_ffn_3", "ln_g", "ln_b", "g_final_3"):
        put(n, tile_columns(a[n if n in a else n + "_3"]))
    c_both = np.stack([a["c_3"].reshape(-1), a["c_ctx_3"].reshape(-1)])
    put("c_c", c_both.reshape(2, DT, P).transpose(2, 1, 0).reshape(P, 16))
    put("b_mod", tile_columns(a["b_mod_3"]))
    put("g_q", tile_columns(a["g_q_3"]))
    put("g_kv", tile_columns(a["g_kv_3"]))
    put("w_dw", tile_columns(a["w_dw_3"]))
    put("b_dw", tile_columns(a["b_dw_3"]))
    return out


def pack_weights(a):
    plan = weight_plan()
    out = np.zeros((len(plan), P, SLOT), np.float32)
    for s, (_, kt, pieces) in enumerate(plan):
        width = sum(p[4] for p in pieces)
        view = out[s, :, 0:kt * width].reshape(P, kt, width)
        at = 0
        for name, i, r0, c0, n in pieces:
            view[:, :, at:at + n] = a[name][i, r0:r0 + kt * P, c0:c0 + n].reshape(kt, P, n).transpose(1, 0, 2)
            at += n
    return out


def host_arrays(a):
    arrays = {
        "x_t": np.ascontiguousarray(a["x"][0].T),
        "p_t": np.ascontiguousarray(a["p_2"][0, 0].T),
        "ctx_t": np.ascontiguousarray(a["ctx_3"][0].T),
        "sinks": np.ascontiguousarray(a["sinks_2"]),
        "rel_bias": np.ascontiguousarray(a["rel_bias_2"]),
        "vectors": pack_vectors(a),
        "weights": pack_weights(a),
        "mod_weights": np.ascontiguousarray(a["w_mod_3"].reshape(DT, P, MOD_SLOTS, 256).transpose(2, 1, 0, 3)).reshape(
            MOD_SLOTS, P, SLOT),
    }
    arrays.update(shape_constants())
    return arrays


def kernel(**inputs):
    import concourse.bacc as bacc
    from concourse.bass_utils import run_bass_kernel_spmd

    arrays = host_arrays({k: np.asarray(v) for k, v in inputs.items()})
    nc = bacc.Bacc("TRN2", target_bir_lowering=False, num_devices=1)
    ins = {n: nc.dram_tensor(n, v.shape, mybir.dt.from_np(v.dtype), kind="ExternalInput").ap()
           for n, v in arrays.items()}
    out = nc.dram_tensor("out_t", (D, T), F32, kind="ExternalOutput").ap()
    build(nc, ins, out)
    r = run_bass_kernel_spmd(nc, [arrays], core_ids=[0])
    return np.ascontiguousarray(r.results[0]["out_t"].T)[None]
```
